# Optimizing a Trainium2 kernel written in Bass

```python
import math
import jax
import jax.numpy as jnp
from jax import lax
import numpy as np

D_MODEL = 1024
BATCH = 1
SEQ = 128
DEPTH = 2
DEC_BATCH = 1
DEC_SEQ = 256
PAST_LEN = 128

F32 = jnp.float32
GRID_W = 64
ROPE_THETA = 10000.0
NORM_EPS = 1e-6
NEG_BIG = -1e30
LOG_TINY = 1e-30
Q_BLOCK = 128
N_EVEN = (DEPTH + 1) // 2
N_ODD = DEPTH // 2

SWA_HEADS = 8
SWA_KV_HEADS = 2
SWA_GROUP = SWA_HEADS // SWA_KV_HEADS
SWA_HEAD_DIM = 64
SWA_WIDTH = SWA_HEADS * SWA_HEAD_DIM
SWA_WINDOW = 128
SWA_BLOCK = 128

HGRN_HEADS = 4
HGRN_KEY_DIM = 128
HGRN_VAL_DIM = 128
HGRN_WIDTH = HGRN_HEADS * HGRN_KEY_DIM
HGRN_CHUNK = 64

EVEN_SIZES = (SWA_WIDTH, SWA_KV_HEADS * SWA_HEAD_DIM, SWA_KV_HEADS * SWA_HEAD_DIM,
              HGRN_WIDTH, HGRN_WIDTH, HGRN_WIDTH, HGRN_WIDTH, HGRN_WIDTH)
EVEN_SPLIT_POINTS = tuple(sum(EVEN_SIZES[:i + 1]) for i in range(len(EVEN_SIZES) - 1))
EVEN_IN_WIDTH = sum(EVEN_SIZES)
EVEN_MIX_WIDTH = SWA_WIDTH + HGRN_WIDTH

MLA_HEADS = 16
MLA_Q_RANK = 384
MLA_KV_RANK = 256
MLA_NOPE_DIM = 64
MLA_ROPE_DIM = 32
MLA_V_DIM = 64
MLA_QK_DIM = MLA_NOPE_DIM + MLA_ROPE_DIM

MOE_GROUPS = 4
MOE_EXPERTS_PER_GROUP = 8
MOE_EXPERTS = MOE_GROUPS * MOE_EXPERTS_PER_GROUP
MOE_TOP_K = 2
MOE_HIDDEN = 256

kernel_name = 'hybrid_flow_prefix_step'

def rms_norm(x, w):
    xf = x.astype(F32)
    y = xf * lax.rsqrt(jnp.mean(xf * xf, axis=-1, keepdims=True) + NORM_EPS)
    return (y * w.astype(F32)).astype(x.dtype)

def adaln_input(x, w, shift, scale):
    return rms_norm(x, w) * (1 + scale) + shift

def rope_2d(x):
    T = x.shape[1]
    rows = T // GRID_W
    row = jnp.repeat(jnp.arange(rows, dtype=F32), GRID_W)
    col = (jnp.arange(T) % GRID_W).astype(F32)
    half = x.shape[-1] // 2
    nf = half // 2
    inv = jnp.exp(-math.log(ROPE_THETA) * jnp.arange(nf, dtype=F32) / nf)
    bshape = (1, T) + (1,) * (x.ndim - 3) + (nf,)

    def rot(xh, pos):
        ang = (pos[:, None] * inv[None, :]).reshape(bshape)
        cos, sin = jnp.cos(ang), jnp.sin(ang)
        x1 = xh[..., :nf].astype(F32)
        x2 = xh[..., nf:].astype(F32)
        return jnp.concatenate([x1 * cos - x2 * sin, x1 * sin + x2 * cos], axis=-1)

    return jnp.concatenate([rot(x[..., :half], row), rot(x[..., half:], col)], axis=-1).astype(x.dtype)

def dense_attention(q, k, v, scale, sink=None):
    B, T, KV, G, D = q.shape
    nb = T // Q_BLOCK
    qb = jnp.moveaxis(q.reshape(B, nb, Q_BLOCK, KV, G, D), 1, 0)

    def one(qblk):
        s = jnp.einsum('bqkgd,bskd->bkgqs', qblk, k).astype(F32) * scale
        if sink is not None:
            sk = jnp.broadcast_to(sink.astype(F32).reshape(1, KV, G, 1, 1), s.shape[:-1] + (1,))
            p = jax.nn.softmax(jnp.concatenate([sk, s], axis=-1), axis=-1)[..., 1:]
        else:
            p = jax.nn.softmax(s, axis=-1)
        return jnp.einsum('bkgqs,bske->bqkge', p.astype(v.dtype), v)

    o = lax.map(one, qb)
    return jnp.moveaxis(o, 0, 1).reshape(B, T, KV, G, v.shape[-1])

def swa_latent(q, k, v, k_ctx, v_ctx, sink, scale):
    B, T, KV, G, D = q.shape
    E = v.shape[-1]
    nb = T // SWA_BLOCK
    S = k_ctx.shape[1]
    qb = q.reshape(B, nb, SWA_BLOCK, KV, G, D)

    def band(a):
        pad = jnp.zeros((B, SWA_BLOCK) + a.shape[2:], a.dtype)
        ab = jnp.concatenate([pad, a, pad], axis=1).reshape((B, nb + 2, SWA_BLOCK) + a.shape[2:])
        return jnp.concatenate([ab[:, :-2], ab[:, 1:-1], ab[:, 2:]], axis=2)

    kw, vw = band(k), band(v)
    qi = jnp.arange(SWA_BLOCK)[:, None]
    r = jnp.arange(3 * SWA_BLOCK)[None, :]
    rel = qi + SWA_BLOCK - r
    kpos = (jnp.arange(nb)[:, None, None] - 1) * SWA_BLOCK + r[None]
    mask = (jnp.abs(rel)[None] <= SWA_WINDOW) & (kpos >= 0) & (kpos < T)
    s_loc = jnp.einsum('bnqkgd,bnskd->bkgnqs', qb, kw).astype(F32) * scale
    s_loc = jnp.where(mask, s_loc, NEG_BIG)
    s_ctx = jnp.einsum('bnqkgd,bskd->bkgnqs', qb, k_ctx).astype(F32) * scale
    sk = jnp.broadcast_to(sink.astype(F32).reshape(1, KV, G, 1, 1, 1), s_ctx.shape[:-1] + (1,))
    p = jax.nn.softmax(jnp.concatenate([sk, s_ctx, s_loc], axis=-1), axis=-1)
    p_ctx = p[..., 1:1 + S].astype(v.dtype)
    p_loc = p[..., 1 + S:].astype(v.dtype)
    o = (jnp.einsum('bkgnqs,bske->bnqkge', p_ctx, v_ctx)
         + jnp.einsum('bkgnqs,bnske->bnqkge', p_loc, vw))
    return o.reshape(B, T, KV, G, E)

def gla_chunk_scan(q, k, v, logf, s0):
    B, T, H, DK = q.shape
    DV = v.shape[-1]
    C = HGRN_CHUNK
    nc = T // C

    def chunks(a):
        return a.reshape(B, nc, C, H, a.shape[-1]).transpose(1, 0, 3, 2, 4)

    tri = jnp.tril(jnp.ones((C, C), dtype=bool))[:, :, None]

    def step(S, inp):
        qc, kc, vc, gc = inp
        b = jnp.cumsum(gc, axis=2)
        diff = b[:, :, :, None, :] - b[:, :, None, :, :]
        decay = jnp.exp(jnp.where(tri, diff, NEG_BIG))
        att = jnp.einsum('bhtd,bhsd,bhtsd->bhts', qc, kc, decay)
        o = att @ vc + jnp.einsum('bhtd,bhde->bhte', qc * jnp.exp(b), S)
        b_last = b[:, :, -1:, :]
        S = (jnp.exp(b_last[:, :, 0, :])[..., None] * S
             + jnp.einsum('bhsd,bhse->bhde', kc * jnp.exp(b_last - b), vc))
        return S, o

    S, o = lax.scan(step, s0.astype(F32), (chunks(q), chunks(k), chunks(v), chunks(logf)))
    return o.transpose(1, 0, 3, 2, 4).reshape(B, T, H, DV), S

def layer_lower_bounds(p):
    pr = jax.nn.softmax(p.astype(F32), axis=0)
    return jnp.cumsum(pr, axis=0) - pr[0:1]

def even_project(h, w_in, lb_f, lb_b):
    B, T, _ = h.shape
    qa, ka, va, qb, ff, fb, ib, gb = jnp.split(h @ w_in, EVEN_SPLIT_POINTS, axis=-1)
    qa = qa.reshape(B, T, SWA_KV_HEADS, SWA_GROUP, SWA_HEAD_DIM)
    ka = ka.reshape(B, T, SWA_KV_HEADS, SWA_HEAD_DIM)
    va = va.reshape(B, T, SWA_KV_HEADS, SWA_HEAD_DIM)
    hshape = (B, T, HGRN_HEADS, HGRN_KEY_DIM)
    qh = (jax.nn.silu(qb.astype(F32)) * HGRN_KEY_DIM ** -0.5).reshape(hshape)

    def log_forget(f, lb):
        lb = jnp.clip(lb, 0.0, 1.0 - 1e-6)
        return jnp.logaddexp(jnp.log(jnp.maximum(lb, LOG_TINY)),
                             jnp.log1p(-lb) + jax.nn.log_sigmoid(f.astype(F32))).reshape(hshape)

    lf_f = log_forget(ff, lb_f)
    lf_b = log_forget(fb, lb_b)
    iv = ib.astype(F32).reshape(B, T, HGRN_HEADS, HGRN_VAL_DIM)
    return qa, ka, va, qh, lf_f, lf_b, iv, gb

def hgrn_bidir(qh, lf_f, lf_b, iv, s0_f, s0_b):
    flip = lambda a: jnp.flip(a, axis=1)
    o_f, s_f = gla_chunk_scan(qh, -jnp.expm1(lf_f), iv, lf_f, s0_f)
    o_b, s_b = gla_chunk_scan(flip(qh), flip(-jnp.expm1(lf_b)), flip(iv), flip(lf_b), s0_b)
    return o_f + flip(o_b), s_f, s_b

def hgrn_readout(o, g, gnorm_w, dtype):
    B, T = o.shape[:2]
    gate = jax.nn.silu(g.astype(F32)).reshape(o.shape)
    return (rms_norm(o, gnorm_w) * gate).reshape(B, T, HGRN_WIDTH).astype(dtype)

def even_context(h, w_in, w_out, sink, lb_f, lb_b, gnorm_w):
    B, T, _ = h.shape
    qa, ka, va, qh, lf_f, lf_b, iv, gb = even_project(h, w_in, lb_f, lb_b)
    a = dense_attention(qa, ka, va, SWA_HEAD_DIM ** -0.5, sink).reshape(B, T, SWA_WIDTH)
    s0 = jnp.zeros((B, HGRN_HEADS, HGRN_KEY_DIM, HGRN_VAL_DIM), F32)
    o, s_f, s_b = hgrn_bidir(qh, lf_f, lf_b, iv, s0, s0)
    out = jnp.concatenate([a, hgrn_readout(o, gb, gnorm_w, h.dtype)], axis=-1) @ w_out
    return out, ka, va, jnp.stack([s_f, s_b], axis=1).astype(h.dtype)

def even_latent(h, k_ctx, v_ctx, s_ctx, w_in, w_out, sink, lb_f, lb_b, gnorm_w):
    B, T, _ = h.shape
    qa, ka, va, qh, lf_f, lf_b, iv, gb = even_project(h, w_in, lb_f, lb_b)
    a = swa_latent(rope_2d(qa), rope_2d(ka), va, k_ctx, v_ctx, sink,
                   SWA_HEAD_DIM ** -0.5).reshape(B, T, SWA_WIDTH)
    o, _, _ = hgrn_bidir(qh, lf_f, lf_b, iv, s_ctx[:, 0], s_ctx[:, 1])
    return jnp.concatenate([a, hgrn_readout(o, gb, gnorm_w, h.dtype)], axis=-1) @ w_out

def mla_queries(h, w_dq, qn_w, w_uq, rotate):
    B, T, _ = h.shape
    q = (rms_norm(h @ w_dq, qn_w) @ w_uq).reshape(B, T, MLA_HEADS, MLA_QK_DIM)
    if rotate:
        q = jnp.concatenate([q[..., :MLA_NOPE_DIM], rope_2d(q[..., MLA_NOPE_DIM:])], axis=-1)
    return q

def mla_compress_kv(h, w_dkv, kvn_w, rotate):
    kv = h @ w_dkv
    ckv = rms_norm(kv[..., :MLA_KV_RANK], kvn_w)
    kr = kv[..., MLA_KV_RANK:]
    if rotate:
        kr = rope_2d(kr[:, :, None, :])[:, :, 0, :]
    return ckv, kr

def mla_attend(q, ckv, kr, w_ukv, w_o):
    B, T, H, _ = q.shape
    S = ckv.shape[1]
    kvu = (ckv @ w_ukv).reshape(B, S, H, MLA_NOPE_DIM + MLA_V_DIM)
    k = jnp.concatenate([kvu[..., :MLA_NOPE_DIM],
                         jnp.broadcast_to(kr[:, :, None, :], (B, S, H, MLA_ROPE_DIM))], axis=-1)
    v = kvu[..., MLA_NOPE_DIM:]
    o = dense_attention(q[:, :, :, None, :], k, v, MLA_QK_DIM ** -0.5)
    return o.reshape(B, T, H * MLA_V_DIM) @ w_o

def hier_moe(h, wg, bg, we, be, w_gate, w_up, w_down):
    B, T, D = h.shape
    x = h.reshape(B * T, D)
    n = x.shape[0]
    g_prob = jax.nn.softmax((x @ wg).astype(F32) + bg.astype(F32), axis=-1)
    g_w, g_idx = lax.top_k(g_prob, 1)
    e_logits = jnp.einsum('nd,gde->nge', x, we).astype(F32) + be.astype(F32)
    e_sel = jnp.take_along_axis(e_logits, g_idx[:, :, None], axis=1)[:, 0]
    e_w, e_idx = lax.top_k(jax.nn.softmax(e_sel, axis=-1), MOE_TOP_K)
    e_w = e_w / jnp.sum(e_w, axis=-1, keepdims=True)
    in_group = jnp.sum(jax.nn.one_hot(e_idx, MOE_EXPERTS_PER_GROUP, dtype=F32) * e_w[..., None], axis=1)
    comb = (jax.nn.one_hot(g_idx[:, 0], MOE_GROUPS, dtype=F32)[:, :, None]
            * (g_w[:, :, None] * in_group[:, None, :]))
    wg4 = w_gate.reshape(MOE_GROUPS, MOE_EXPERTS_PER_GROUP, D, MOE_HIDDEN)
    wu4 = w_up.reshape(MOE_GROUPS, MOE_EXPERTS_PER_GROUP, D, MOE_HIDDEN)
    wd4 = w_down.reshape(MOE_GROUPS, MOE_EXPERTS_PER_GROUP, MOE_HIDDEN, D)
    y = jnp.zeros((n, D), F32)
    for g in range(MOE_GROUPS):
        a = jax.nn.silu(jnp.einsum('nd,edf->nef', x, wg4[g])) * jnp.einsum('nd,edf->nef', x, wu4[g])
        a = a * comb[:, g, :, None].astype(a.dtype)
        y = y + jnp.einsum('nef,efd->nd', a, wd4[g]).astype(F32)
    return y.astype(h.dtype).reshape(B, T, D)

def setup_inputs(seed: int = 0) -> dict:
    key = jax.random.key(seed)
    ks = iter(jax.random.split(key, 48))
    nrm = lambda shape, s: jax.random.normal(next(ks), shape, F32) * s
    D = D_MODEL
    E, F = MOE_EXPERTS, MOE_HIDDEN
    return {
        'x_prompt': nrm((BATCH, SEQ, D), 1.0),
        'x_sample': nrm((DEC_BATCH, DEC_SEQ, D), 1.0),
        'c': nrm((DEC_BATCH, D), 1.0),
        'cache_swa_k': nrm((DEC_BATCH, N_EVEN, PAST_LEN, SWA_KV_HEADS, SWA_HEAD_DIM), 1.0),
        'cache_swa_v': nrm((DEC_BATCH, N_EVEN, PAST_LEN, SWA_KV_HEADS, SWA_HEAD_DIM), 1.0),
        'state_hgrn': nrm((DEC_BATCH, N_EVEN, 2, HGRN_HEADS, HGRN_KEY_DIM, HGRN_VAL_DIM), 0.3),
        'cache_mla_ckv': nrm((DEC_BATCH, N_ODD, PAST_LEN, MLA_KV_RANK), 1.0),
        'cache_mla_krope': nrm((DEC_BATCH, N_ODD, PAST_LEN, MLA_ROPE_DIM), 1.0),
        'c_ctx': nrm((D,), 1.0),
        'mod_w': nrm((DEPTH, D, 6 * D), 0.5 * D ** -0.5),
        'mod_b': nrm((DEPTH, 6 * D), 0.02),
        'norm1_w': 1.0 + nrm((DEPTH, D), 0.02),
        'norm2_w': 1.0 + nrm((DEPTH, D), 0.02),
        'final_norm_w': 1.0 + nrm((D,), 0.02),
        'even_w_in': nrm((N_EVEN, D, EVEN_IN_WIDTH), D ** -0.5),
        'even_w_out': nrm((N_EVEN, EVEN_MIX_WIDTH, D), EVEN_MIX_WIDTH ** -0.5),
        'swa_sink': nrm((N_EVEN, SWA_HEADS), 0.5),
        'hgrn_lb_fwd': nrm((N_EVEN, HGRN_WIDTH), 1.0),
        'hgrn_lb_bwd': nrm((N_EVEN, HGRN_WIDTH), 1.0),
        'hgrn_gnorm_w': 1.0 + nrm((N_EVEN, HGRN_VAL_DIM), 0.02),
        'mla_w_dq': nrm((N_ODD, D, MLA_Q_RANK), D ** -0.5),
        'mla_qnorm_w': 1.0 + nrm((N_ODD, MLA_Q_RANK), 0.02),
        'mla_w_uq': nrm((N_ODD, MLA_Q_RANK, MLA_HEADS * MLA_QK_DIM), MLA_Q_RANK ** -0.5),
        'mla_w_dkv': nrm((N_ODD, D, MLA_KV_RANK + MLA_ROPE_DIM), D ** -0.5),
        'mla_kvnorm_w': 1.0 + nrm((N_ODD, MLA_KV_RANK), 0.02),
        'mla_w_ukv': nrm((N_ODD, MLA_KV_RANK, MLA_HEADS * (MLA_NOPE_DIM + MLA_V_DIM)), MLA_KV_RANK ** -0.5),
        'mla_w_o': nrm((N_ODD, MLA_HEADS * MLA_V_DIM, D), (MLA_HEADS * MLA_V_DIM) ** -0.5),
        'moe_router_group_w': nrm((DEPTH, D, MOE_GROUPS), D ** -0.5),
        'moe_router_group_b': nrm((DEPTH, MOE_GROUPS), 0.01),
        'moe_router_expert_w': nrm((DEPTH, MOE_GROUPS, D, MOE_EXPERTS_PER_GROUP), D ** -0.5),
        'moe_router_expert_b': nrm((DEPTH, MOE_GROUPS, MOE_EXPERTS_PER_GROUP), 0.01),
        'moe_w_gate': nrm((DEPTH, E, D, F), D ** -0.5),
        'moe_w_up': nrm((DEPTH, E, D, F), D ** -0.5),
        'moe_w_down': nrm((DEPTH, E, F, D), F ** -0.5),
    }

def reference(x_prompt, x_sample, c, cache_swa_k, cache_swa_v, state_hgrn, cache_mla_ckv,
              cache_mla_krope, c_ctx, mod_w, mod_b, norm1_w, norm2_w, final_norm_w,
              even_w_in, even_w_out, swa_sink, hgrn_lb_fwd, hgrn_lb_bwd, hgrn_gnorm_w,
              mla_w_dq, mla_qnorm_w, mla_w_uq, mla_w_dkv, mla_kvnorm_w, mla_w_ukv, mla_w_o,
              moe_router_group_w, moe_router_group_b, moe_router_expert_w, moe_router_expert_b,
              moe_w_gate, moe_w_up, moe_w_down):
    lb_fwd = layer_lower_bounds(hgrn_lb_fwd)
    lb_bwd = layer_lower_bounds(hgrn_lb_bwd)
    ctx, lat = x_prompt, x_sample
    new_k, new_v, new_s, new_ckv, new_kr = [], [], [], [], []
    for l in range(DEPTH):
        j = l // 2
        mc = jnp.split(jax.nn.silu(c_ctx) @ mod_w[l] + mod_b[l], 6, axis=-1)
        ms = [m[:, None, :] for m in jnp.split(jax.nn.silu(c) @ mod_w[l] + mod_b[l], 6, axis=-1)]
        hc = adaln_input(ctx, norm1_w[l], mc[0], mc[1])
        hs = adaln_input(lat, norm1_w[l], ms[0], ms[1])
        if l % 2 == 0:
            oc, kc, vc, sc = even_context(hc, even_w_in[j], even_w_out[j], swa_sink[j],
                                          lb_fwd[j], lb_bwd[j], hgrn_gnorm_w[j])
            os_ = even_latent(hs, cache_swa_k[:, j], cache_swa_v[:, j], state_hgrn[:, j],
                              even_w_in[j], even_w_out[j], swa_sink[j],
                              lb_fwd[j], lb_bwd[j], hgrn_gnorm_w[j])
            new_k.append(kc)
            new_v.append(vc)
            new_s.append(sc)
        else:
            qc = mla_queries(hc, mla_w_dq[j], mla_qnorm_w[j], mla_w_uq[j], False)
            ckv_c, kr_c = mla_compress_kv(hc, mla_w_dkv[j], mla_kvnorm_w[j], False)
            oc = mla_attend(qc, ckv_c, kr_c, mla_w_ukv[j], mla_w_o[j])
            qs = mla_queries(hs, mla_w_dq[j], mla_qnorm_w[j], mla_w_uq[j], True)
            ckv_s, kr_s = mla_compress_kv(hs, mla_w_dkv[j], mla_kvnorm_w[j], True)
            os_ = mla_attend(qs, jnp.concatenate([cache_mla_ckv[:, j], ckv_s], axis=1),
                             jnp.concatenate([cache_mla_krope[:, j], kr_s], axis=1),
                             mla_w_ukv[j], mla_w_o[j])
            new_ckv.append(ckv_c)
            new_kr.append(kr_c)
        ctx = ctx + mc[2] * oc
        lat = lat + ms[2] * os_
        hc = adaln_input(ctx, norm2_w[l], mc[3], mc[4])
        hs = adaln_input(lat, norm2_w[l], ms[3], ms[4])
        ctx = ctx + mc[5] * hier_moe(hc, moe_router_group_w[l], moe_router_group_b[l],
                                     moe_router_expert_w[l], moe_router_expert_b[l],
                                     moe_w_gate[l], moe_w_up[l], moe_w_down[l])
        lat = lat + ms[5] * hier_moe(hs, moe_router_group_w[l], moe_router_group_b[l],
                                     moe_router_expert_w[l], moe_router_expert_b[l],
                                     moe_w_gate[l], moe_w_up[l], moe_w_down[l])
    y_prompt = rms_norm(ctx, final_norm_w)
    y_sample = rms_norm(lat, final_norm_w)
    return (y_prompt, y_sample, jnp.stack(new_k, axis=1), jnp.stack(new_v, axis=1),
            jnp.stack(new_s, axis=1), jnp.stack(new_ckv, axis=1), jnp.stack(new_kr, axis=1))


_drawn_inputs = setup_inputs


def setup_inputs(seed=0):
    import zlib

    import numpy as np

    out = dict(_drawn_inputs(seed))
    spreads = {}
    factors = {'cache_swa_k': 3.148,
     'cache_swa_v': 2.874,
     'state_hgrn': 8.0,
     'cache_mla_ckv': 2.956,
     'cache_mla_krope': 4.329,
     'norm1_w': 2.83,
     'norm2_w': 3.135,
     'final_norm_w': 7.49,
     'swa_sink': 64.0,
     'hgrn_gnorm_w': 5.84,
     'mla_qnorm_w': 8.0,
     'mla_kvnorm_w': 2.671,
     'moe_router_group_b': 6.415,
     'moe_router_expert_b': 4.902}
    for name, (base, spread) in spreads.items():
        noise = np.random.default_rng([zlib.crc32(name.encode()), seed]).standard_normal(out[name].shape)
        drawn = base * np.exp(spread * noise) if base else spread * noise
        out[name] = jnp.asarray(drawn.astype(out[name].dtype))
    for name, factor in factors.items():
        out[name] = (out[name] * factor).astype(out[name].dtype)
    return out
```

```python
import concourse.bass as bass
from concourse import mybir
from contextlib import ExitStack

P = 128
D = 1024
DC = D // P
NT = 3
TOK = NT * P
HEADS, KVH, HD = 8, 2, 64
GH = 4
QKV = (HEADS + 2 * KVH) * HD
MH, QR, KVR, RD, ND, VD = 16, 384, 256, 32, 64, 64
EXPERTS, GROUPS, PER = 32, 4, 8
FF = 256
BANKS = 8
RING = 3
SLOT = 4096
LEVELS = [64, 32, 16, 8, 4, 2, 1]
EPS = 1e-6
WORK = 25312
HGRN_SCALE = P ** -0.5
LN2 = 0.6931471805599453
KEYT = 4


def attention_groups(layer):
    return [(g, t) for g in range(2 if layer == 0 else 4) for t in range(NT)]


def key_tiles(t):
    return [0] if t == 0 else [1, 2, 3]


def score_heads(layer, t):
    if t == 0:
        return [[0, 1, 2, 3]] if layer else [[0, 2], [1, 3]]
    return [[0], [1], [2], [3]]


def matmul_jobs():
    jobs = []

    def add(key, eng):
        jobs.append((key, eng))

    def attention(layer):
        groups = attention_groups(layer)

        def scores(n):
            g, t = groups[n]
            if layer == 1 and t == 0:
                for i in range(2):
                    add(("kT", g, i), "v")
                for i in range(4):
                    add(("qT1", g, i), "v")
            for i in range(len(score_heads(layer, t))):
                add(("score", layer, n, i), "a")
        scores(0)
        for n in range(len(groups)):
            if n + 1 < len(groups):
                scores(n + 1)
            for i in range(len(key_tiles(groups[n][1]))):
                add(("pT", layer, n, i), "a" if i == 0 else "v")
            add(("pv", layer, n), "v")

    def to_features(kind, layer):
        for t in range(NT):
            for k in range(2):
                add((kind, layer, t, k), "v" if k else "a")

    for layer in range(2):
        for b in range(12):
            add(("mod", layer, b), "v")
        to_features("hT", layer)
        if layer == 0:
            for b in (0, 1):
                for t in range(NT):
                    add(("qkv", b, t), "a")
            for b in range(3):
                for h in range(GH):
                    add(("qff", b, h), "a")
            for b in range(2):
                for t in range(NT):
                    add(("vg", b, t), "a")
            for t in range(NT):
                add(("qT", t), "v")
            for k in range(2):
                add(("kT0", k), "v")
            attention(0)
            for lv in range(len(LEVELS)):
                for d in range(2):
                    for t in range(NT):
                        add(("lvl", lv, d, t), "v")
            for t in range(NT):
                add(("diag", t), "v")
            for u in range(4):
                add(("kdT", u), "a")
                add(("state", u), "v")
            for t in range(NT):
                add(("o", t), "a")
        else:
            for b in range(2):
                for t in range(NT):
                    add(("dqkv", b, t), "a")
            for t in range(NT):
                add(("cqT", t), "v")
            for k in range(2):
                add(("ckvT", k), "v")
            add(("krT",), "v")
            for kt in range(KEYT):
                for k in range(2):
                    add(("val", kt, k), "a")
            attention(1)
        to_features("mixT", layer)
        for n in range(2):
            for t in range(NT):
                add(("proj", layer, n, t), "v")
        to_features("h2T", layer)
        add(("router", layer), "v")
    return jobs


def build(nc, I, O, mod_dram):
    f32, i32 = mybir.dt.float32, mybir.dt.int32
    ALU, ACT = mybir.AluOpType, mybir.ActivationFunctionType
    AX = mybir.AxisListType.X

    jobs = matmul_jobs()
    number = {key: n for n, (key, _) in enumerate(jobs)}
    drains = []
    count = {"v": 0, "a": 0}
    for _, e in jobs:
        count[e] += 1
        drains.append(count[e])

    with ExitStack() as ctx:
        def sb(name, shape, dt=f32):
            return ctx.enter_context(nc.sbuf_tensor(name, shape, dt))

        def sem(name):
            return ctx.enter_context(nc.semaphore(name))

        X = sb("X", [P, NT, D])
        hT = sb("hT", [P, DC, TOK])
        MOD = sb("MOD", [P, 2, 3, D])
        RINGB = sb("RINGB", [P, RING, SLOT])
        W = sb("W", [P, WORK])
        ident = sb("ident", [P, P])
        normw = sb("normw", [P, D])
        WR = sb("WR", [P, DC, 36])
        BR = sb("BR", [P, 36])
        cond = sb("cond", [P, 2, DC])
        cond2 = sb("cond2", [P, 2, DC])
        small = sb("small", [P, 64])
        banks = [ctx.enter_context(nc.psum_tensor(f"bank{i}", [P, 512], f32)) for i in range(BANKS)]

        def cut(at, shape, dt=None):
            n = 1
            for s in shape:
                n *= s
            v = W[:, at:at + n]
            if dt is not None:
                v = v.bitcast(dt)
            if len(shape) == 2:
                v = v.rearrange("p (a b) -> p a b", a=shape[0])
            if len(shape) == 3:
                v = v.rearrange("p (a b c) -> p a b c", a=shape[0], b=shape[1])
            return v

        modbias = cut(0, (2, 512))
        modrow = cut(1024, (2, 512))
        MIX = cut(0, (NT, D))
        ATT = cut(3072, (NT, GH, P))
        QH = cut(4608, (GH, TOK))
        LF = cut(6144, (2, GH * TOK))
        KK = cut(9216, (2, GH * TOK))
        VV = cut(12288, (NT, GH * P))
        GG = cut(13824, (NT, GH * P))
        MASK = cut(15360, (15, P), i32)
        T0 = 17280
        QKVt = cut(T0, (NT, QKV))
        QT = cut(T0 + 2304, (4, TOK))
        KT = cut(T0 + 3840, (2, KEYT * P))
        KD = cut(T0 + 4864, (KEYT, KVH, 2 * HD))
        ROT = cut(T0 + 5888, (2, 640))
        VC = cut(T0 + 7424, (P,))
        band = cut(T0 + 7552, (2, P))
        P0 = [cut(9216 + 1536 * i, (4, TOK)) for i in range(2)]
        PT0 = [cut(3072, (NT, 4 * P)), cut(T0 + 5888, (NT, 4 * P))]
        LE = [cut(T0 + 3072 * i, (GH * TOK,)) for i in range(2)]
        LK = [cut(T0 + 3072 * i + 1536, (GH * TOK,)) for i in range(2)]
        BIG = cut(T0, (2 * GH * TOK,))
        BIG2 = cut(T0 + 3072, (2 * GH * TOK,))
        KD4 = cut(T0, (4, GH * P))
        KDT = cut(T0 + 2048, (4, GH * P))
        QI = cut(T0 + 4096, (2, GH * 2 * P))
        ST = cut(9216, (6, GH * P))
        OB = cut(T0, (NT, GH * P))
        OB2 = cut(T0 + 1536, (NT, GH * P))
        CQ = cut(3072, (NT, QR + KVR + RD))
        CACHE = cut(5088, (KVR,))
        KR = cut(5344, (KEYT, 96))
        CQT = cut(5728, (3, TOK))
        CKVT = cut(6880, (2, KEYT * P))
        VAL = cut(7904, (KEYT, MH * VD))
        Q1 = [cut(12000 + 1536 * i, (4, TOK)) for i in range(2)]
        K1 = [cut(15072 + 2048 * i, (4, KEYT * P)) for i in range(2)]
        P1 = [cut(19168 + 1536 * i, (4, TOK)) for i in range(2)]
        PT1 = [cut(22240, (NT, 4 * P))]
        KRT = cut(23776, (KEYT * P,))
        SQ = cut(24288, (QR,))
        qnw = cut(24672, (QR + KVR,))
        WQB = cut(3072, (3, 4 * P))
        YACC = cut(0, (NT, D))
        COMB = cut(3072, (NT, EXPERTS))
        EE = cut(3200, (2, TOK))
        AT = cut(5000, (2, 2, TOK))
        RT = cut(7000, (NT * 36 * 4,))

        rope_cs = sb("rope_cs", [P, 2, 2, HD])
        rope32 = sb("rope32", [P, 2, 2, RD])
        ropeT = sb("ropeT", [P, 2 * P])
        smallp = sb("smallp", [P, 3, 32])
        sink = sb("sink", [P, HEADS])
        lbc = sb("lbc", [P, 2, GH])
        lbs = sb("lbs", [P, 6, 2, GH])
        gnw = sb("gnw", [P, P])
        iota = sb("iota", [P, 16])

        consts_in = sem("consts_in")
        cond_in = sem("cond_in")
        tokens_in = sem("tokens_in")
        weight_in = [sem(f"weight_in{i}") for i in range(RING)]
        modbias_in = [sem(f"modbias_in{i}") for i in range(2)]
        block_used = sem("block_used")
        bank_filled = sem("bank_filled")
        emptied = {"v": sem("emptied_by_vector"), "a": sem("emptied_by_scalar")}
        v_step = sem("v_step")
        a_step = sem("a_step")
        to_act = sem("input_for_scalar")
        from_act = sem("output_of_scalar")
        to_pe = sem("input_for_tensor")
        cond_ready = sem("cond_ready")
        modrow_ready = sem("modrow_ready")
        modrow_out = [sem(f"modrow_out{i}") for i in range(2)]
        mod_in = sem("mod_in")
        mod_free = sem("mod_free")
        router_in = sem("router_in")
        l1params_in = sem("l1params_in")
        pool_free = sem("pool_free")
        stored = sem("stored")
        out_ready = sem("out_ready")
        gu_in = [sem(f"expert_gu_in{i}") for i in range(2)]
        dn_in = [sem(f"expert_down_in{i}") for i in range(2)]
        gu_done = sem("gate_up_done")
        gexp_done = sem("gate_exp_done")
        act_ready = sem("expert_act_ready")
        y_done = sem("expert_y_done")
        y_emptied = sem("expert_y_emptied")
        v_loop = sem("v_step_in_experts")

        blocks = []

        def rows(ap, chunks):
            return ap.rearrange("(p c) n -> p c n", c=chunks)

        for layer in range(2):
            for b in range(12):
                blocks.append((("mod", layer, b), rows(I["mod_w"][layer], DC)[:, :, b * 512:b * 512 + 512], (DC, 512)))
            if layer == 0:
                win = rows(I["even_w_in"][0], DC)
                for b, (lo, hi) in enumerate([(0, 512), (512, 768), (768, 1280), (1280, 1792), (1792, 2304),
                                              (2304, 2816), (2816, 3328)]):
                    blocks.append((("win", b), win[:, :, lo:hi], (DC, hi - lo)))
                for n in range(2):
                    blocks.append((("wout", 0, n), rows(I["even_w_out"][0], DC)[:, :, n * 512:n * 512 + 512], (DC, 512)))
            else:
                blocks.append((("dq",), rows(I["mla_w_dq"][0], DC), (DC, QR)))
                blocks.append((("dkv",), rows(I["mla_w_dkv"][0], DC), (DC, KVR + RD)))
                blocks.append((("ukv",), rows(I["mla_w_ukv"][0], 2), (2, 2048)))
                for n in range(2):
                    blocks.append((("uq", n), rows(I["mla_w_uq"][0], 3)[:, :, n * 768:n * 768 + 768], (3, 768)))
                for n in range(2):
                    blocks.append((("wout", 1, n), rows(I["mla_w_o"][0], DC)[:, :, n * 512:n * 512 + 512], (DC, 512)))
        blockno = {key: n for n, (key, _, _) in enumerate(blocks)}
        first1 = blockno[("mod", 1, 0)]

        def block_view(key):
            n = blockno[key]
            c, w = blocks[n][2]
            return RINGB[:, n % RING, 0:c * w].rearrange("p (c n) -> p c n", c=c)

        def weights_arrived(eng, key):
            n = blockno[key]
            eng.wait_ge(weight_in[n % RING], 16 * (n // RING + 1))

        def filled(eng, key):
            n = number[key]
            eng.wait_ge(bank_filled, n + 1)
            return banks[n % BANKS]

        def emptied_now(eng, key):
            n = number[key]
            eng.wait_ge(emptied[jobs[n][1]], drains[n])

        block = ctx.enter_context(nc.Block())

        wg = lambda layer, e: I["moe_w_gate"][layer, e, :, :].rearrange("(p c) n -> p c n", c=DC)
        wu = lambda layer, e: I["moe_w_up"][layer, e, :, :].rearrange("(p c) n -> p c n", c=DC)
        wd = lambda layer, e: I["moe_w_down"][layer, e, :, :].rearrange("(p c) n -> p c n", c=2)

        def gu_slot(q):
            return RINGB[:, q, :].rearrange("p (g c n) -> p g c n", g=2, c=DC)

        def dn_slot(q):
            return RINGB[:, 2, q * 2048:q * 2048 + 2048].rearrange("p (c n) -> p c n", c=2)

        @block.sync
        def _(sp):
            def load(n):
                if n >= RING:
                    sp.wait_ge(block_used, n - RING + 1)
                key, src, (c, w) = blocks[n]
                sp.dma_start(block_view(key), src).then_inc(weight_in[n % RING], 16)
                if key[0] == "mod":
                    b = key[2]
                    if key[1] and b == 0:
                        sp.wait_ge(mod_free, 2)
                    if b >= 2:
                        sp.wait_ge(modrow_ready, 12 * key[1] + b - 1)
                    for g in range(2):
                        sp.dma_start(modbias[g:g + 1, b % 2, :],
                                     I["mod_b"][key[1]:key[1] + 1, b * 512:b * 512 + 512]).then_inc(modbias_in[b % 2], 16)

            def experts(layer):
                base = layer * 2 * EXPERTS

                def load_expert(e, q, wait):
                    if wait is not None:
                        sp.wait_ge(gu_done, wait)
                    sp.dma_start(gu_slot(q)[:, 0], wg(layer, e)).then_inc(gu_in[q], 16)
                    sp.dma_start(gu_slot(q)[:, 1], wu(layer, e)).then_inc(gu_in[q], 16)
                    if wait is not None:
                        sp.wait_ge(y_done, wait * 3)
                    sp.dma_start(dn_slot(q), wd(layer, e)).then_inc(dn_in[q], 16)

                sp.wait_ge(block_used, first1 if layer == 0 else len(blocks))
                for q in range(2):
                    load_expert(q, q, None)
                with sp.Fori(0, EXPERTS // 2 - 1) as i:
                    for q in range(2):
                        load_expert(2 * i + 2 + q, q, base + 4 * i + 2 * q + 2)

            for n in range(first1):
                load(n)
            experts(0)
            sp.wait_ge(y_done, 6 * EXPERTS)
            for n in range(first1, len(blocks)):
                load(n)
            experts(1)

        @block.gpsimd
        def _(pool):
            def dma(out, src, s):
                pool.dma_start(out, src).then_inc(s, 16)
            dma(cond2[:, 0, :], I["c_ctx"].rearrange("(p c) -> p c", c=DC), cond_in)
            dma(cond2[:, 1, :], I["c"][0].rearrange("(p c) -> p c", c=DC), cond_in)
            dma(X[:, 0, :], I["x_prompt"][0], tokens_in)
            dma(X[:, 1:3, :], I["x_sample"][0].rearrange("(t p) d -> p t d", p=P), tokens_in)
            dma(ident[:], I["k_ident"], consts_in)
            dma(MASK, I["k_mask"], consts_in)
            dma(rope_cs[:], I["k_rope64"], consts_in)
            dma(rope32[:], I["k_rope32"], consts_in)
            dma(ropeT[:], I["k_ropeT"], consts_in)
            dma(sink[:], I["swa_sink"][0:1, :].to_broadcast([P, HEADS]), consts_in)
            dma(gnw[:], I["hgrn_gnorm_w"][0:1, :].to_broadcast([P, P]), consts_in)
            dma(band, I["k_band"], consts_in)
            dma(normw[:], I["norm1_w"][0:1, :].to_broadcast([P, D]), consts_in)
            for d, nm in enumerate(("hgrn_lb_fwd", "hgrn_lb_bwd")):
                with nc.allow_non_contiguous_dma(reason="512 values, once"):
                    dma(lbc[:, d, :], I[nm][0].rearrange("(h p) -> p h", p=P), consts_in)

            def modulation(layer, part, nth):
                if nth:
                    pool.wait_ge(mod_free, nth)
                for par in range(2):
                    pool.wait_ge(modrow_out[par], 16 * 6 * (layer + 1))
                for g in range(2):
                    src = mod_dram[layer, g:g + 1, part * 3 * D:(part + 1) * 3 * D]
                    dma(MOD[:, g, :, :].rearrange("p v d -> p (v d)"), src.to_broadcast([P, 3 * D]), mod_in)

            def rowblocks(layer):
                for b in range(12):
                    pool.wait_ge(modrow_ready, 12 * layer + b + 1)
                    dma(mod_dram[layer, :, b * 512:b * 512 + 512], modrow[0:2, b % 2, :], modrow_out[b % 2])

            def router(layer):
                if layer:
                    emptied_now(pool, ("router", 0))
                dma(WR[:, :, 0:4], I["moe_router_group_w"][layer].rearrange("(p c) n -> p c n", c=DC), router_in)
                for g in range(GROUPS):
                    dma(WR[:, :, 4 + 8 * g:12 + 8 * g],
                        I["moe_router_expert_w"][layer, g].rearrange("(p c) n -> p c n", c=DC), router_in)
                dma(BR[:, 0:4], I["moe_router_group_b"][layer:layer + 1, :].to_broadcast([P, 4]), router_in)
                dma(BR[:, 4:36], I["moe_router_expert_b"][layer].rearrange("g e -> (g e)").unsqueeze(0).to_broadcast([P, 32]), router_in)

            router(0)
            rowblocks(0)
            modulation(0, 0, 0)
            for dup in range(2):
                dma(KD[:, 1, :, dup * HD:dup * HD + HD], I["cache_swa_k"][0, 0], l1params_in)
            dma(VC, I["cache_swa_v"][0, 0].rearrange("s h d -> s (h d)"), l1params_in)
            emptied_now(pool, ("qkv", 1, 0))
            dma(O[2][0, 0].rearrange("s h d -> s (h d)"), QKVt[:, 0, 512:640], stored)
            dma(O[3][0, 0].rearrange("s h d -> s (h d)"), QKVt[:, 0, 640:768], stored)
            pool.wait_ge(out_ready, 1)
            dma(ST[:, 0, :].rearrange("p (h e) -> p h e", h=GH), I["state_hgrn"][0, 0, 0].rearrange("h k v -> k h v"), l1params_in)
            dma(ST[:, 1, :].rearrange("p (h e) -> p h e", h=GH), I["state_hgrn"][0, 0, 1].rearrange("h k v -> k h v"), l1params_in)
            for d in range(2):
                pool.wait_ge(out_ready, 2 + d)
                dma(O[4][0, 0, d].rearrange("h k v -> k h v"), ST[:, 2 + d, :].rearrange("p (h e) -> p h e", h=GH), stored)
            modulation(0, 1, 1)
            pool.wait_ge(pool_free, 1)
            dma(normw[:], I["norm2_w"][0:1, :].to_broadcast([P, D]), consts_in)
            pool.wait_ge(pool_free, 2)
            dma(normw[:], I["norm1_w"][1:2, :].to_broadcast([P, D]), consts_in)
            router(1)
            rowblocks(1)
            modulation(1, 0, 2)
            dma(qnw[:, 0:QR], I["mla_qnorm_w"][0:1, :].to_broadcast([P, QR]), l1params_in)
            dma(qnw[:, QR:QR + KVR], I["mla_kvnorm_w"][0:1, :].to_broadcast([P, KVR]), l1params_in)
            dma(CACHE, I["cache_mla_ckv"][0, 0], l1params_in)
            pool.wait_ge(out_ready, 4)
            dma(KR[:, 1, 64:96], I["cache_mla_krope"][0, 0], l1params_in)
            pool.wait_ge(out_ready, 5)
            dma(O[5][0, 0], CQ[:, 0, QR:QR + KVR], stored)
            dma(O[6][0, 0], CQ[:, 0, QR + KVR:], stored)
            modulation(1, 1, 3)
            pool.wait_ge(pool_free, 3)
            dma(normw[:], I["norm2_w"][1:2, :].to_broadcast([P, D]), consts_in)
            pool.wait_ge(pool_free, 4)
            dma(normw[:], I["final_norm_w"].unsqueeze(0).to_broadcast([P, D]), consts_in)
            pool.wait_ge(out_ready, 6)
            dma(O[0][0], MIX[:, 0, :], stored)
            dma(O[1][0].rearrange("(t p) d -> p t d", p=P), MIX[:, 1:3, :], stored)
            pool.wait_ge(stored, 16 * 8)

        CONSTS = 16 * 11

        @block.tensor
        def _(pe):
            inputs = [0]

            def new_input():
                inputs[0] += 1
                pe.wait_ge(to_pe, inputs[0])

            def bank(key):
                n = number[key]
                if n >= BANKS:
                    pe.wait_ge(emptied[jobs[n - BANKS][1]], drains[n - BANKS])
                return banks[n % BANKS]

            def contract(out, lhs, rhs, chunks):
                for c in range(chunks):
                    last = nc.tensor.matmul(out, lhs(c), rhs(c), start=(c == 0), stop=(c == chunks - 1))
                return last

            def transposed(kind, layer, src):
                for t in range(NT):
                    new_input()
                    for k in range(2):
                        b = bank((kind, layer, t, k))
                        for j in range(4):
                            last = nc.tensor.transpose(b[:, j * P:(j + 1) * P], src[:, t, 4 * k + j::DC], ident[:])
                        last.then_inc(bank_filled, 1)

            def modulation(layer):
                for b in range(12):
                    key = ("mod", layer, b)
                    weights_arrived(pe, key)
                    w = block_view(key)
                    out = bank(key)
                    contract(out[0:2, :], lambda c: cond[:, :, c], lambda c: w[:, c, :], DC).then_inc(bank_filled, 1)
                    used(key)

            def used(key):
                pe.wait_ge(bank_filled, number[key] + 1)
                pe.sem_inc(block_used, 1)

            def attention(layer):
                groups = attention_groups(layer)

                def scores(n):
                    g, t = groups[n]
                    if layer == 1 and t == 0:
                        if g == 0:
                            weights_arrived(pe, ("uq", 0))
                        if g == 2:
                            weights_arrived(pe, ("uq", 1))
                        kv = block_view(("ukv",)).rearrange("p c (h n) -> p c h n", h=MH)
                        for i in range(2):
                            key = ("kT", g, i)
                            out = bank(key)
                            h = 4 * g + 2 * i
                            for j in range(2):
                                last = contract(out[64 * j:64 * j + 64, :], lambda c: kv[:, c, h + j, 0:ND],
                                                lambda c: CKVT[:, c, :], 2)
                            last.then_inc(bank_filled, 1)
                        new_input()
                        for i in range(4):
                            out = bank(("qT1", g, i))
                            contract(out[:, 0:TOK], lambda c: WQB[:, c, i * P:(i + 1) * P], lambda c: CQT[:, c, :], 3)\
                                .then_inc(bank_filled, 1)
                        if g == 3:
                            for _ in range(3):
                                used(("qT1", g, 3))
                        new_input()
                    kts = key_tiles(t)
                    nk = len(kts) * P
                    for i, hs in enumerate(score_heads(layer, t)):
                        out = bank(("score", layer, n, i))
                        for j, h in enumerate(hs):
                            o = out[:, j * nk:(j + 1) * nk]
                            if layer == 0:
                                hh = (4 * g + h) % 2
                                q = QT[64 * hh:64 * hh + 64, (4 * g + h) // 2, t * P:(t + 1) * P]
                                k = KT[64 * hh:64 * hh + 64, g, kts[0] * P:kts[0] * P + nk]
                            else:
                                q = Q1[g % 2][0:96, h, t * P:(t + 1) * P]
                                k = K1[g % 2][0:96, h, kts[0] * P:kts[0] * P + nk]
                            masked = layer == 0 and t > 0
                            last = nc.tensor.matmul(o, q, k, start=True, stop=not masked)
                            if masked:
                                far = 3 if t == 1 else 2
                                last = nc.tensor.matmul(out[:, (far - 1) * P:far * P], ident[:], band[:, t - 1, :],
                                                        start=False, stop=True)
                        last.then_inc(bank_filled, 1)

                scores(0)
                for n, (g, t) in enumerate(groups):
                    if n + 1 < len(groups):
                        scores(n + 1)
                    kts = key_tiles(t)
                    prob = (P0 if layer == 0 else P1)[n % 2]
                    pt = (PT0 if layer == 0 else PT1)
                    pt = pt[n % len(pt)]
                    emptied_now(pe, ("score", layer, n, len(score_heads(layer, t)) - 1))
                    pr = prob.rearrange("p h k -> p (h k)")[:, 0:4 * P * len(kts)].rearrange("p (h k) -> p h k", h=4)
                    for i in range(len(kts)):
                        out = bank(("pT", layer, n, i))
                        for h in range(4):
                            last = nc.tensor.transpose(out[:, h * P:(h + 1) * P], pr[:, h, i * P:(i + 1) * P], ident[:])
                        last.then_inc(bank_filled, 1)
                    out = bank(("pv", layer, n))
                    emptied_now(pe, ("pT", layer, n, 0))
                    emptied_now(pe, ("pT", layer, n, len(kts) - 1))
                    for h in range(4):
                        for i, kt in enumerate(kts):
                            if layer == 0:
                                v = VC[:, g * HD:(g + 1) * HD] if kt == 1 else \
                                    QKVt[:, 0 if kt == 0 else kt - 1, 640 + g * HD:640 + (g + 1) * HD]
                            else:
                                v = VAL[:, kt, (4 * g + h) * VD:(4 * g + h + 1) * VD]
                            last = nc.tensor.matmul(out[:, h * 64:(h + 1) * 64], pt[:, i, h * P:(h + 1) * P], v,
                                                    start=(i == 0), stop=(i == len(kts) - 1))
                    last.then_inc(bank_filled, 1)

            def project(layer):
                transposed("mixT", layer, MIX)
                for n in range(2):
                    weights_arrived(pe, ("wout", layer, n))
                    w = block_view(("wout", layer, n))
                    for t in range(NT):
                        if n == 0:
                            emptied_now(pe, ("mixT", layer, t, 0))
                            emptied_now(pe, ("mixT", layer, t, 1))
                        out = bank(("proj", layer, n, t))
                        contract(out[:, :], lambda c: hT[:, c, t * P:(t + 1) * P], lambda c: w[:, c, :], DC)\
                            .then_inc(bank_filled, 1)
                    used(("proj", layer, n, NT - 1))

            def router(layer):
                transposed("h2T", layer, MIX)
                pe.wait_ge(router_in, 16 * 7 * (layer + 1))
                out = bank(("router", layer))
                for t in range(NT):
                    emptied_now(pe, ("h2T", layer, t, 0))
                    emptied_now(pe, ("h2T", layer, t, 1))
                    last = contract(out[:, t * 36:t * 36 + 36], lambda c: hT[:, c, t * P:(t + 1) * P],
                                    lambda c: WR[:, c, :], DC)
                last.then_inc(bank_filled, 1)

            def experts(layer):
                new_input()
                with pe.Fori(0, EXPERTS // 2) as i:
                    for q in range(2):
                        pe.wait_ge(gu_in[q], 32 * (EXPERTS // 2 * layer + 1) + 32 * i)
                        for f in range(2):
                            pe.wait_ge(act_ready, layer * (2 * EXPERTS + 2) + 2 * q + f + 1 + 4 * i)
                            for g in range(2):
                                last = contract(banks[2 * g + f][:, 0:TOK],
                                                lambda c: gu_slot(q)[:, g, c, f::2],
                                                lambda c: hT[:, c, :], DC)
                            last.then_inc(gu_done, 1)
                        pe.wait_ge(dn_in[q], 16 * (EXPERTS // 2 * layer + 1) + 16 * i)
                        pe.wait_ge(act_ready, layer * (2 * EXPERTS + 2) + 2 * q + 4 + 4 * i)
                        for j in range(6):
                            n, t = divmod(j, NT)
                            k = 6 * q + j
                            pe.wait_ge(y_emptied, layer * (6 * EXPERTS + 4) + k + 1 + 12 * i)
                            contract(banks[4 + k % 4][:, :], lambda c: AT[:, q, c, t * P:(t + 1) * P],
                                     lambda c: dn_slot(q)[:, c, n * 512:(n + 1) * 512], 2).then_inc(y_done, 1)
                pe.wait_ge(y_emptied, (layer + 1) * (6 * EXPERTS + 4))

            pe.wait_ge(cond_ready, 1)
            for layer in range(2):
                modulation(layer)
                if layer == 0:
                    pe.wait_ge(consts_in, CONSTS)
                transposed("hT", layer, MIX)
                for t in range(NT):
                    for k in range(2):
                        emptied_now(pe, ("hT", layer, t, k))
                if layer == 0:
                    for b in range(7):
                        weights_arrived(pe, ("win", b))
                        w = block_view(("win", b))
                        if b in (0, 1, 5, 6):
                            for t in range(NT):
                                key = ("qkv", b, t) if b < 2 else ("vg", b - 5, t)
                                out = bank(key)
                                contract(out[:, 0:blocks[blockno[("win", b)]][2][1]],
                                         lambda c: hT[:, c, t * P:(t + 1) * P], lambda c: w[:, c, :], DC)\
                                    .then_inc(bank_filled, 1)
                        else:
                            for h in range(GH):
                                key = ("qff", b - 2, h)
                                out = bank(key)
                                contract(out[:, 0:TOK], lambda c: w[:, c, h * P:(h + 1) * P], lambda c: hT[:, c, :], DC)\
                                    .then_inc(bank_filled, 1)
                        used(key)
                    new_input()
                    for t in range(NT):
                        out = bank(("qT", t))
                        for j in range(4):
                            last = nc.tensor.transpose(out[:, j * P:(j + 1) * P], QKVt[:, t, j * P:(j + 1) * P], ident[:])
                        last.then_inc(bank_filled, 1)
                    for k in range(2):
                        out = bank(("kT0", k))
                        for j in range(4):
                            last = nc.tensor.transpose(out[:, j * P:(j + 1) * P], KD[:, 2 * k + j // 2, j % 2, :], ident[:])
                        last.then_inc(bank_filled, 1)
                    emptied_now(pe, ("qT", 2))
                    emptied_now(pe, ("kT0", 1))
                    attention(0)
                    for lv in range(len(LEVELS)):
                        for d in range(2):
                            new_input()
                            for t in range(NT):
                                out = bank(("lvl", lv, d, t))
                                for h in range(GH):
                                    at = h * TOK + t * P
                                    last = nc.tensor.matmul(out[:, h * P:(h + 1) * P], LK[d][:, at:at + P],
                                                            LE[d][:, at:at + P], start=True, stop=True)
                                last.then_inc(bank_filled, 1)
                    new_input()
                    for t in range(NT):
                        out = bank(("diag", t))
                        for h in range(GH):
                            at = h * TOK + t * P
                            last = nc.tensor.matmul(out[:, h * P:(h + 1) * P], LK[0][:, at:at + P],
                                                    QH[:, h, t * P:(t + 1) * P], start=True, stop=True)
                        last.then_inc(bank_filled, 1)
                    new_input()
                    for u, (d, t) in enumerate(((0, 0), (1, 0), (0, 1), (1, 2))):
                        out = bank(("kdT", u))
                        for h in range(GH):
                            last = nc.tensor.transpose(out[:, h * P:(h + 1) * P], KD4[:, u, h * P:(h + 1) * P], ident[:])
                        last.then_inc(bank_filled, 1)
                        out = bank(("state", u))
                        emptied_now(pe, ("kdT", u))
                        for h in range(GH):
                            last = nc.tensor.matmul(out[:, h * P:(h + 1) * P], KDT[:, u, h * P:(h + 1) * P],
                                                    VV[:, t, h * P:(h + 1) * P], start=True, stop=True)
                        last.then_inc(bank_filled, 1)
                    emptied_now(pe, ("state", 3))
                    emptied_now(pe, ("diag", 2))
                    for t in range(NT):
                        out = bank(("o", t))
                        for h in range(GH):
                            hs = slice(h * P, (h + 1) * P)
                            last = nc.tensor.matmul(out[:, hs], ATT[:, t, h, :], VV[:, t, hs], start=True, stop=(t == 0))
                            if t:
                                at = (h * 2 + t - 1) * P
                                for d in range(2):
                                    s = (0 if t == 1 else 4) if d == 0 else (1 if t == 2 else 5)
                                    last = nc.tensor.matmul(out[:, hs], QI[:, d, at:at + P], ST[:, s, hs],
                                                            start=False, stop=(d == 1))
                        last.then_inc(bank_filled, 1)
                else:
                    for b, (nm, n) in enumerate((("dq", QR), ("dkv", KVR + RD))):
                        weights_arrived(pe, (nm,))
                        w = block_view((nm,))
                        for t in range(NT):
                            out = bank(("dqkv", b, t))
                            contract(out[:, 0:n], lambda c: hT[:, c, t * P:(t + 1) * P], lambda c: w[:, c, :], DC)\
                                .then_inc(bank_filled, 1)
                        used(("dqkv", b, NT - 1))
                    new_input()
                    for t in range(NT):
                        out = bank(("cqT", t))
                        for c in range(3):
                            last = nc.tensor.transpose(out[:, c * P:(c + 1) * P], CQ[:, t, c:QR:3], ident[:])
                        last.then_inc(bank_filled, 1)
                    for k in range(2):
                        out = bank(("ckvT", k))
                        for j in range(4):
                            kt, c = 2 * k + j // 2, j % 2
                            src = CACHE[:, c::2] if kt == 1 else CQ[:, 0 if kt == 0 else kt - 1, QR + c:QR + KVR:2]
                            last = nc.tensor.transpose(out[:, j * P:(j + 1) * P], src, ident[:])
                        last.then_inc(bank_filled, 1)
                    out = bank(("krT",))
                    for kt in range(KEYT):
                        last = nc.tensor.transpose(out[0:96, kt * P:(kt + 1) * P], KR[:, kt, :], ident[:])
                    last.then_inc(bank_filled, 1)
                    emptied_now(pe, ("krT",))
                    weights_arrived(pe, ("ukv",))
                    kv = block_view(("ukv",)).rearrange("p c (h n) -> p c h n", h=MH)
                    for kt in range(KEYT):
                        for k in range(2):
                            out = bank(("val", kt, k))
                            contract(out[:, :], lambda c: CKVT[:, c, kt * P:(kt + 1) * P],
                                     lambda c: kv[:, c, 8 * k:8 * k + 8, ND:], 2).then_inc(bank_filled, 1)
                    for kt in range(KEYT):
                        emptied_now(pe, ("val", kt, 1))
                    attention(1)
                project(layer)
                router(layer)
                experts(layer)

        @block.scalar
        def _(act):
            step = [0]
            given = [0]

            def link(ins):
                step[0] += 1
                ins.then_inc(a_step, 1)
                act.wait_ge(a_step, step[0])

            def go():
                given[0] += 1
                act.wait_ge(to_act, given[0])

            def done(ins):
                ins.then_inc(from_act, 1)

            def emptied_by_me(ins):
                ins.then_inc(emptied["a"], 1)

            nc.scalar.preload_act_table_set("natural_log_exp_and_others")

            def norm():
                go()
                link(nc.scalar.activation(small[:, 4:7], small[:, 0:3], ACT.Ln, bias=small[:, 62:63]))
                done(nc.scalar.activation(small[:, 8:11], small[:, 4:7], ACT.Exp, scale=-0.5))

            def to_features(kind, layer):
                for t in range(NT):
                    b = filled(act, (kind, layer, t, 0))
                    emptied_by_me(nc.scalar.activation(hT[:, 0:4, t * P:(t + 1) * P],
                                                       b[:, :].rearrange("p (c n) -> p c n", c=4), ACT.Copy))

            def attention(layer):
                groups = attention_groups(layer)
                scale = 0.125 if layer == 0 else 96 ** -0.5

                def exps(n):
                    g, t = groups[n]
                    nk = len(key_tiles(t)) * P
                    prob = (P0 if layer == 0 else P1)[n % 2]
                    pr = prob.rearrange("p h k -> p (h k)")[:, 0:4 * nk].rearrange("p (h k) -> p h k", h=4)
                    go()
                    if n >= 2:
                        gp, tp = groups[n - 2]
                        act.wait_ge(bank_filled, number[("pT", layer, n - 2, len(key_tiles(tp)) - 1)] + 1)
                    nb = smallp[:, n % 3, 0:4]
                    rs = smallp[:, n % 3, 4:8]
                    if layer == 0:
                        nc.scalar.activation(smallp[:, n % 3, 12:16], smallp[:, n % 3, 8:12], ACT.Exp)
                    share = score_heads(layer, t)
                    for h in range(4):
                        i = [h in hs for hs in share].index(True)
                        j = share[i].index(h)
                        b = banks[number[("score", layer, n, i)] % BANKS]
                        src = b[:, j * nk:(j + 1) * nk]
                        ins = nc.scalar.activation(pr[:, h, :], src, ACT.Exp, bias=nb[:, h:h + 1], scale=scale,
                                                   accum_out=rs[:, h:h + 1])
                        if h == share[i][-1]:
                            emptied_by_me(ins)

                exps(0)
                for n, (g, t) in enumerate(groups):
                    if n + 1 < len(groups):
                        exps(n + 1)
                    pt = (PT0 if layer == 0 else PT1)
                    b = filled(act, ("pT", layer, n, 0))
                    if n >= len(pt):
                        act.wait_ge(bank_filled, number[("pv", layer, n - len(pt))] + 1)
                    emptied_by_me(nc.scalar.activation(pt[n % len(pt)][:, 0, :], b[:, :], ACT.Copy))

            act.wait_ge(cond_in, 32)
            done(nc.scalar.activation(cond[:], cond2[:], ACT.Exp, scale=-1.0))
            for layer in range(2):
                norm()
                to_features("hT", layer)
                if layer == 0:
                    for b in range(2):
                        for t in range(NT):
                            bk = filled(act, ("qkv", b, t))
                            w = 512 if b == 0 else 256
                            emptied_by_me(nc.scalar.activation(QKVt[:, t, 512 * b:512 * b + w], bk[:, 0:w], ACT.Copy))
                    for b in range(3):
                        for h in range(GH):
                            bk = filled(act, ("qff", b, h))
                            dst = QH[:, h, :] if b == 0 else LF[:, b - 1, h * TOK:(h + 1) * TOK]
                            emptied_by_me(nc.scalar.activation(dst, bk[:, 0:TOK], ACT.Copy))
                    for b in range(2):
                        for t in range(NT):
                            bk = filled(act, ("vg", b, t))
                            emptied_by_me(nc.scalar.activation((VV, GG)[b][:, t, :], bk[:, :], ACT.Copy))
                    attention(0)
                    go()
                    nc.scalar.activation(BIG[:, 0:1536], QH.rearrange("p h t -> p (h t)"), ACT.Exp, scale=-1.0)
                    nc.scalar.activation(BIG[:, 1536:3072], GG.rearrange("p h t -> p (h t)"), ACT.Exp, scale=-1.0)
                    done(nc.scalar.activation(lbs[:, 0, :, :], lbs[:, 1, :, :], ACT.Exp))
                    go()
                    nc.scalar.activation(lbs[:, 3, :, :], lbs[:, 2, :, :], ACT.Ln, scale=float(2.0 ** 60))
                    done(nc.scalar.activation(lbs[:, 4, :, :], lbs[:, 1, :, :], ACT.Ln, scale=-1.0, bias=1.0))
                    go()
                    LFf = LF.rearrange("p d n -> p (d n)")
                    link(nc.scalar.activation(BIG, LFf, ACT.Abs))
                    link(nc.scalar.activation(BIG, BIG, ACT.Exp, scale=-1.0))
                    done(nc.scalar.activation(BIG, BIG, ACT.Ln, bias=1.0))
                    go()
                    link(nc.scalar.activation(BIG, BIG, ACT.Abs))
                    link(nc.scalar.activation(BIG, BIG, ACT.Exp, scale=-1.0))
                    done(nc.scalar.activation(BIG, BIG, ACT.Ln, bias=1.0))
                    go()
                    done(nc.scalar.activation(KK.rearrange("p d n -> p (d n)"), LFf, ACT.Exp))
                    for lv in range(len(LEVELS)):
                        for d in range(2):
                            go()
                            link(nc.scalar.activation(LE[d], LE[d], ACT.Abs))
                            done(nc.scalar.activation(LE[d], LE[d], ACT.Exp, scale=-1.0))
                    go()
                    nc.scalar.activation(KD4.rearrange("p u n -> p (u n)"), KD4.rearrange("p u n -> p (u n)"), ACT.Exp)
                    nc.scalar.activation(QI[:, 0, :], QI[:, 0, :], ACT.Exp)
                    nc.scalar.activation(QI[:, 1, :], QI[:, 1, :], ACT.Exp)
                    done(nc.scalar.activation(smallp[:, 0:2, 0:8], smallp[:, 0:2, 0:8], ACT.Exp))
                    for u in range(4):
                        bk = filled(act, ("kdT", u))
                        emptied_by_me(nc.scalar.activation(KDT[:, u, :], bk[:, :], ACT.Copy))
                    for t in range(NT):
                        bk = filled(act, ("o", t))
                        emptied_by_me(nc.scalar.activation(OB[:, t, :], bk[:, :], ACT.Copy))
                    go()
                    link(nc.scalar.activation(small[:, 32:44], small[:, 16:28], ACT.Ln, bias=small[:, 62:63]))
                    done(nc.scalar.activation(small[:, 48:60], small[:, 32:44], ACT.Exp, scale=-0.5))
                else:
                    for b in range(2):
                        for t in range(NT):
                            bk = filled(act, ("dqkv", b, t))
                            lo, w = (0, QR) if b == 0 else (QR, KVR + RD)
                            emptied_by_me(nc.scalar.activation(CQ[:, t, lo:lo + w], bk[:, 0:w], ACT.Copy))
                    go()
                    link(nc.scalar.activation(small[:, 32:38], small[:, 16:22], ACT.Ln, bias=small[:, 62:63]))
                    done(nc.scalar.activation(small[:, 48:54], small[:, 32:38], ACT.Exp, scale=-0.5))
                    for kt in range(KEYT):
                        for k in range(2):
                            bk = filled(act, ("val", kt, k))
                            emptied_by_me(nc.scalar.activation(VAL[:, kt, k * 512:(k + 1) * 512], bk[:, :], ACT.Copy))
                    attention(1)
                to_features("mixT", layer)
                norm()
                to_features("h2T", layer)
                go()
                done(nc.scalar.activation(RT[:, 128:140], RT[:, 128:140], ACT.Exp))
                go()
                done(nc.scalar.activation(RT[:, 256:280], RT[:, 256:280], ACT.Exp))
                with act.Fori(0, EXPERTS // 2) as i:
                    for q in range(2):
                        for f in range(2):
                            act.wait_ge(gu_done, layer * 2 * EXPERTS + 2 * q + f + 1 + 4 * i)
                            act.wait_ge(act_ready, layer * (2 * EXPERTS + 2) + 2 * q + f + 1 + 4 * i)
                            nc.scalar.activation(EE[:, f, :], banks[f][:, 0:TOK], ACT.Exp, scale=-1.0).then_inc(gexp_done, 1)
            norm()

        @block.vector
        def _(dve):
            v = nc.vector
            step = [0]
            waited = [0]

            def link(ins):
                step[0] += 1
                ins.then_inc(v_step, 1)
                dve.wait_ge(v_step, step[0])

            def give(ins):
                ins.then_inc(to_act, 1)

            def get():
                waited[0] += 1
                dve.wait_ge(from_act, waited[0])

            fed = [0]

            def feed(ins):
                fed[0] += 1
                ins.then_inc(to_pe, 1)

            def emptied_by_me(ins):
                ins.then_inc(emptied["v"], 1)

            def rstd(src, n):
                for t in range(NT):
                    link(v.tensor_tensor_reduce(out=MIX[:, t, 0:n], in0=src[:, t, :], in1=src[:, t, :], scale=1.0 / n,
                                                scalar=0.0, op0=ALU.mult, op1=ALU.add, accum_out=small[:, t:t + 1]))
                dve.sem_inc(to_act, 1)
                get()

            def adaln(kind, layer, consts, nth):
                dve.wait_ge(mod_in, 32 * nth)
                rstd(X, D)
                dve.wait_ge(consts_in, consts)
                for g in range(2):
                    link(v.scalar_tensor_tensor(out=MOD[:, g, 1, :], in0=MOD[:, g, 1, :], scalar=1.0, in1=normw[:],
                                                op0=ALU.add, op1=ALU.mult))
                for t in range(NT):
                    g = 0 if t == 0 else 1
                    link(v.scalar_tensor_tensor(out=MIX[:, t, :], in0=X[:, t, :], scalar=small[:, 8 + t:9 + t],
                                                in1=MOD[:, g, 1, :], op0=ALU.mult, op1=ALU.mult))
                    feed(v.tensor_tensor(MIX[:, t, :], MIX[:, t, :], MOD[:, g, 0, :], ALU.add))
                dve.wait_ge(to_pe, fed[0])
                dve.sem_inc(pool_free, 1)
                to_features(kind, layer)

            def to_features(kind, layer):
                for t in range(NT):
                    b = filled(dve, (kind, layer, t, 1))
                    emptied_by_me(v.tensor_copy(hT[:, 4:8, t * P:(t + 1) * P], b[:, :].rearrange("p (c n) -> p c n", c=4)))

            def attention(layer):
                groups = attention_groups(layer)
                scale = 0.125 if layer == 0 else 96 ** -0.5

                def maxima(n):
                    g, t = groups[n]
                    nk = len(key_tiles(t)) * P
                    if layer == 1 and t == 0:
                        queries_keys(g)
                    sp_ = smallp[:, n % 3]
                    share = score_heads(layer, t)
                    for i, hs in enumerate(share):
                        b = filled(dve, ("score", layer, n, i))
                        link(v.tensor_reduce(out=sp_[:, 16 + i:20:len(share)],
                                             in_=b[:, 0:len(hs) * nk].rearrange("p (h k) -> p h k", k=nk), axis=AX, op=ALU.max))
                    if layer == 0:
                        sk = sink[:, 4 * g:4 * g + 4]
                        link(v.scalar_tensor_tensor(out=sp_[:, 16:20], in0=sp_[:, 16:20], scalar=scale, in1=sk,
                                                    op0=ALU.mult, op1=ALU.max))
                        link(v.tensor_tensor(sp_[:, 8:12], sk, sp_[:, 16:20], ALU.subtract))
                        give(v.tensor_scalar(sp_[:, 0:4], sp_[:, 16:20], -1.0, None, ALU.mult))
                    else:
                        give(v.tensor_scalar(sp_[:, 0:4], sp_[:, 16:20], -scale, None, ALU.mult))

                maxima(0)
                for n, (g, t) in enumerate(groups):
                    if n + 1 < len(groups):
                        maxima(n + 1)
                    sp_ = smallp[:, n % 3]
                    pt = (PT0 if layer == 0 else PT1)
                    for i in range(1, len(key_tiles(t))):
                        b = filled(dve, ("pT", layer, n, i))
                        if n >= len(pt):
                            dve.wait_ge(bank_filled, number[("pv", layer, n - len(pt))] + 1)
                        emptied_by_me(v.tensor_copy(pt[n % len(pt)][:, i, :], b[:, :]))
                    emptied_now(dve, ("score", layer, n, len(score_heads(layer, t)) - 1))
                    if layer == 0:
                        link(v.tensor_tensor(sp_[:, 4:8], sp_[:, 4:8], sp_[:, 12:16], ALU.add))
                    link(v.reciprocal(sp_[:, 20:24], sp_[:, 4:8]))
                    b = filled(dve, ("pv", layer, n))
                    emptied_by_me(v.tensor_tensor(MIX[:, t, 256 * g:256 * g + 256].rearrange("p (h e) -> p h e", h=4),
                                                  b[:, 0:256].rearrange("p (h e) -> p h e", h=4),
                                                  sp_[:, 20:24].unsqueeze(2).to_broadcast([P, 4, 64]), ALU.mult))

            def queries_keys(g):
                uq = block_view(("uq", g // 2)).rearrange("p c (h n) -> p c h n", h=8)
                hs = slice(4 * (g % 2), 4 * (g % 2) + 4)
                if g % 2 == 0:
                    weights_arrived(dve, ("uq", g // 2))
                wq = WQB[:].rearrange("p c (h n) -> p c h n", h=4)
                if g == 0:
                    dve.wait_ge(stored, 16 * 6)
                if g:
                    dve.wait_ge(bank_filled, number[("qT1", g - 1, 3)] + 1)
                for c in range(3):
                    v.tensor_copy(wq[:, c, :, 0:96], uq[:, c, hs, :])
                    for half in range(4):
                        to = 96 + 8 * half
                        fr = 64 + 8 * (half ^ 1)
                        last = v.tensor_copy(wq[:, c, :, to:to + 8], uq[:, c, hs, fr:fr + 8])
                feed(last)
                K, Q = K1[g % 2], Q1[g % 2]
                if g >= 2:
                    dve.wait_ge(bank_filled, number[("score", 1, 3 * (g - 2) + 2, 3)] + 1)
                for i in range(2):
                    b = filled(dve, ("kT", g, i))
                    v.tensor_copy(K[0:64, 2 * i, :], b[0:64, :])
                    emptied_by_me(v.tensor_copy(K[0:64, 2 * i + 1, :], b[64:128, :]))
                for i in range(4):
                    b = filled(dve, ("qT1", g, i))
                    v.tensor_copy(Q[0:64, i, :], b[0:64, 0:TOK])
                    v.tensor_copy(Q[64:96, i, 0:P], b[64:96, 0:P])
                    v.tensor_tensor(Q[64:96, i, P:TOK], b[64:96, P:TOK], ropeT[64:96, :], ALU.mult)
                    link(v.tensor_tensor(SQ[64:96, 0:2 * P], b[96:128, P:TOK], ropeT[96:128, :], ALU.mult))
                    emptied_by_me(v.tensor_tensor(Q[64:96, i, P:TOK], Q[64:96, i, P:TOK], SQ[64:96, 0:2 * P], ALU.add))
                    emptied_now(dve, ("qT1", g, i))
                feed(v.tensor_copy(K[64:96, :, :], KRT[64:96, :].unsqueeze(1).to_broadcast([32, 4, KEYT * P])))

            def residual(layer):
                for n in range(2):
                    for t in range(NT):
                        g = 0 if t == 0 else 1
                        cs = slice(n * 512, (n + 1) * 512)
                        b = filled(dve, ("proj", layer, n, t))
                        emptied_by_me(v.tensor_tensor(MIX[:, t, cs], b[:, :], MOD[:, g, 2, cs], ALU.mult))
                        emptied_now(dve, ("proj", layer, n, t))
                        link(v.tensor_tensor(X[:, t, cs], X[:, t, cs], MIX[:, t, cs], ALU.add))

            def first_hot(out, val, mx, tmp, n):
                io = iota[:, 0:n].unsqueeze(1).to_broadcast([P, NT, n])
                io64 = iota[:, 8:8 + n].unsqueeze(1).to_broadcast([P, NT, n])
                link(v.tensor_tensor(tmp, val, mx.to_broadcast([P, NT, n]), ALU.is_ge))
                link(v.scalar_tensor_tensor(out=tmp, in0=tmp, scalar=-64.0, in1=io64, op0=ALU.mult, op1=ALU.add))
                link(v.tensor_reduce(out=RT[:, 400:403], in_=tmp, axis=AX, op=ALU.min))
                link(v.tensor_tensor(out, RT[:, 400:403].unsqueeze(2).to_broadcast([P, NT, n]), io, ALU.is_equal))

            def route(layer):
                def cols(at, n):
                    return RT[:, at:at + NT * n].rearrange("p (t n) -> p t n", t=NT)

                L = cols(0, 36)
                b = filled(dve, ("router", layer))
                dve.wait_ge(router_in, 16 * 7 * (layer + 1))
                emptied_by_me(v.tensor_tensor(L, b[:, 0:108].rearrange("p (t n) -> p t n", t=NT),
                                              BR[:].unsqueeze(1).to_broadcast([P, NT, 36]), ALU.add))
                emptied_now(dve, ("router", layer))
                GL = L[:, :, 0:4]
                gm, gsum = cols(112, 1), cols(116, 1)
                eg = cols(128, 4)
                link(v.tensor_reduce(out=gm, in_=GL, axis=AX, op=ALU.max))
                give(v.tensor_tensor(eg, GL, gm.to_broadcast([P, NT, 4]), ALU.subtract))
                goh, tmp = cols(144, 4), cols(160, 8)
                first_hot(goh, GL, gm, tmp[:, :, 0:4], 4)
                prod = RT[:, 300:396].rearrange("p (t g e) -> p t g e", t=NT, g=4)
                for t in range(NT):
                    link(v.tensor_tensor(prod[:, t], L[:, t, 4:36].rearrange("p (g e) -> p g e", g=4),
                                         goh[:, t].unsqueeze(2).to_broadcast([P, 4, 8]), ALU.mult))
                esel = cols(224, 8)
                link(v.tensor_reduce(out=esel, in_=prod.rearrange("p t g e -> p t e g"), axis=AX, op=ALU.add))
                m1 = cols(120, 1)
                link(v.tensor_reduce(out=m1, in_=esel, axis=AX, op=ALU.max))
                e8 = cols(256, 8)
                get()
                give(v.tensor_tensor(e8, esel, m1.to_broadcast([P, NT, 8]), ALU.subtract))
                link(v.tensor_reduce(out=gsum, in_=eg, axis=AX, op=ALU.add))
                link(v.reciprocal(gsum, gsum))
                o1, o2 = cols(184, 8), cols(404 - 0, 8)
                first_hot(o1, esel, m1, tmp, 8)
                link(v.scalar_tensor_tensor(out=esel, in0=o1, scalar=-1e30, in1=esel, op0=ALU.mult, op1=ALU.add))
                link(v.tensor_reduce(out=m1, in_=esel, axis=AX, op=ALU.max))
                first_hot(o2, esel, m1, tmp, 8)
                get()
                link(v.tensor_tensor(o1, o1, o2, ALU.add))
                link(v.tensor_tensor(e8, e8, o1, ALU.mult))
                den = cols(124, 1)
                link(v.tensor_reduce(out=den, in_=e8, axis=AX, op=ALU.add))
                link(v.reciprocal(den, den))
                link(v.tensor_tensor(den, den, gsum, ALU.mult))
                link(v.tensor_tensor(e8, e8, den.to_broadcast([P, NT, 8]), ALU.mult))
                for t in range(NT):
                    last = v.tensor_tensor(COMB[:, t, :].rearrange("p (g e) -> p g e", g=4),
                                           goh[:, t].unsqueeze(2).to_broadcast([P, 4, 8]),
                                           e8[:, t].unsqueeze(1).to_broadcast([P, 4, 8]), ALU.mult)
                feed(last)
                dve.wait_ge(to_pe, fed[0])

            def experts(layer):
                link(v.memset(YACC, 0.0))
                dve.sem_inc(y_emptied, 4)
                dve.sem_inc(act_ready, 2)
                with dve.Fori(0, EXPERTS // 2) as i:
                    for q in range(2):
                        for f in range(2):
                            n = 2 * q + f
                            dve.wait_ge(gexp_done, layer * 2 * EXPERTS + n + 1 + 4 * i)
                            s0 = layer * 12 * (EXPERTS // 2) + 3 * n
                            v.tensor_scalar(EE[:, f, :], EE[:, f, :], 1.0, None, ALU.add).then_inc(v_loop, 1)
                            dve.wait_ge(v_loop, s0 + 1 + 12 * i)
                            v.reciprocal(EE[:, f, :], EE[:, f, :]).then_inc(v_loop, 1)
                            dve.wait_ge(v_loop, s0 + 2 + 12 * i)
                            v.tensor_tensor(EE[:, f, :], banks[f][:, 0:TOK], EE[:, f, :], ALU.mult).then_inc(v_loop, 1)
                            dve.wait_ge(v_loop, s0 + 3 + 12 * i)
                            v.tensor_tensor(AT[:, q, f, :], banks[2 + f][:, 0:TOK], EE[:, f, :], ALU.mult).then_inc(act_ready, 1)
                        for j in range(6):
                            h, t = divmod(j, NT)
                            k = 6 * q + j
                            dve.wait_ge(y_done, layer * 6 * EXPERTS + k + 1 + 12 * i)
                            ys = YACC[:, t, h * 512:(h + 1) * 512]
                            dve.wait_ge(y_emptied, layer * (6 * EXPERTS + 4) + 4 + k + 12 * i)
                            v.scalar_tensor_tensor(out=ys, in0=banks[4 + k % 4][:, :], scalar=COMB[:, t, bass.ds(2 * i + q, 1)],
                                                   in1=ys, op0=ALU.mult, op1=ALU.add).then_inc(y_emptied, 1)
                dve.wait_ge(y_emptied, (layer + 1) * (6 * EXPERTS + 4))
                for t in range(NT):
                    link(v.tensor_tensor(YACC[:, t, :], YACC[:, t, :], MOD[:, 0 if t == 0 else 1, 2, :], ALU.mult))
                    link(v.tensor_tensor(X[:, t, :], X[:, t, :], YACC[:, t, :], ALU.add))

            def modulation(layer):
                for b in range(12):
                    bk = filled(dve, ("mod", layer, b))
                    dve.wait_ge(modbias_in[b % 2], 32 * (6 * layer + b // 2 + 1))
                    if b >= 2:
                        dve.wait_ge(modrow_out[b % 2], 16 * (6 * layer + b // 2))
                    v.tensor_tensor(modrow[0:2, b % 2, :], bk[0:2, :], modbias[0:2, b % 2, :], ALU.add).then_inc(modrow_ready, 1)
                    dve.wait_ge(modrow_ready, 12 * layer + b + 1)
                    dve.sem_inc(emptied["v"], 1)

            v.memset(small[:, 62:63], EPS)
            for j in range(8):
                v.memset(iota[:, j:j + 1], float(j))
                v.memset(iota[:, 8 + j:9 + j], float(64 + j))
            get()
            link(v.tensor_scalar(cond[:], cond[:], 1.0, None, ALU.add))
            link(v.reciprocal(cond[:], cond[:]))
            v.tensor_tensor(cond[:], cond[:], cond2[:], ALU.mult).then_inc(cond_ready, 1)
            dve.wait_ge(tokens_in, 32)
            for layer in range(2):
                modulation(layer)
                adaln("hT", layer, CONSTS + 32 * layer, 2 * layer + 1)
                if layer == 0:
                    emptied_now(dve, ("qkv", 1, 2))
                    dve.wait_ge(l1params_in, 48)
                    for t in (1, 2):
                        x = QKVt[:, t, 0:640].rearrange("p (h r) -> p h r", r=HD)
                        link(v.tensor_tensor(ROT[:, 0, :].rearrange("p (h r) -> p h r", r=HD), x,
                                             rope_cs[:, t - 1, 0].unsqueeze(1).to_broadcast([P, 10, HD]), ALU.mult))
                        for half in range(4):
                            o = half ^ 1
                            r = ROT[:, 1, :].rearrange("p (h r) -> p h r", r=HD)
                            link(v.tensor_tensor(r[:, :, 16 * half:16 * half + 16], x[:, :, 16 * o:16 * o + 16],
                                                 rope_cs[:, t - 1, 1, 16 * half:16 * half + 16].unsqueeze(1).to_broadcast([P, 10, 16]),
                                                 ALU.mult))
                        link(v.tensor_tensor(QKVt[:, t, 0:640], ROT[:, 0, :], ROT[:, 1, :], ALU.add))
                    for kt in (0, 2, 3):
                        t = 0 if kt == 0 else kt - 1
                        for dup in range(2):
                            last = v.tensor_copy(KD[:, kt, :, dup * HD:dup * HD + HD],
                                                 QKVt[:, t, 512:640].rearrange("p (g d) -> p g d", g=2))
                    feed(last)
                    for t in range(NT):
                        b = filled(dve, ("qT", t))
                        emptied_by_me(v.tensor_copy(QT[:, :, t * P:(t + 1) * P], b[:, :].rearrange("p (j n) -> p j n", j=4)))
                    for k in range(2):
                        b = filled(dve, ("kT0", k))
                        for j in range(2):
                            ins = v.tensor_copy(KT[:, :, (2 * k + j) * P:(2 * k + j + 1) * P],
                                                b[:, 2 * j * P:(2 * j + 2) * P].rearrange("p (g n) -> p g n", g=2))
                        emptied_by_me(ins)
                    attention(0)
                    emptied_now(dve, ("pv", 0, 5))
                    emptied_now(dve, ("vg", 1, 2))
                    dve.wait_ge(stored, 32)
                    give(v.tensor_tensor(lbs[:, 1, :, :], lbc[:], lbc[:], ALU.subtract))
                    get()
                    link(v.reciprocal(lbs[:, 5, :, :], lbs[:, 0, :, :]))
                    link(v.tensor_tensor(lbs[:, 0, :, :], lbs[:, 0, :, :], lbs[:, 5, :, :], ALU.mult))
                    link(v.tensor_tensor(lbs[:, 1, :, :], lbs[:, 0, :, :], lbs[:, 0, :, :], ALU.subtract))
                    link(v.tensor_scalar(lbs[:, 1, :, :], lbs[:, 1, :, :], 0.0, 1.0 - 1e-6, ALU.max, ALU.min))
                    give(v.tensor_scalar(lbs[:, 2, :, :], lbs[:, 1, :, :], 1e-30, None, ALU.max))
                    QHf, GGf = QH.rearrange("p h t -> p (h t)"), GG.rearrange("p h t -> p (h t)")
                    link(v.tensor_scalar(BIG, BIG, 1.0, None, ALU.add))
                    link(v.reciprocal(BIG, BIG))
                    v.scalar_tensor_tensor(out=QHf, in0=QHf, scalar=HGRN_SCALE, in1=BIG[:, 0:1536], op0=ALU.mult, op1=ALU.mult)
                    link(v.tensor_tensor(GGf, GGf, BIG[:, 1536:3072], ALU.mult))
                    get()
                    link(v.tensor_scalar(lbs[:, 3, :, :], lbs[:, 3, :, :], -60 * LN2, None, ALU.add))
                    dve.sem_inc(to_act, 1)
                    get()
                    LFf = LF.rearrange("p d n -> p (d n)")
                    LF8 = LFf.rearrange("p (b n) -> p b n", b=8)
                    BIG8 = BIG.rearrange("p (b n) -> p b n", b=8)
                    A8 = lbs[:, 3, :, :].rearrange("p d h -> p (d h)").unsqueeze(2).to_broadcast([P, 8, TOK])
                    C8 = lbs[:, 4, :, :].rearrange("p d h -> p (d h)").unsqueeze(2).to_broadcast([P, 8, TOK])
                    link(v.scalar_tensor_tensor(out=LFf, in0=LFf, scalar=0.0, in1=BIG, op0=ALU.min, op1=ALU.subtract))
                    link(v.tensor_tensor(LF8, LF8, C8, ALU.add))
                    give(v.tensor_tensor(BIG8, LF8, A8, ALU.subtract))
                    link(v.tensor_tensor(LF8, LF8, A8, ALU.max))
                    get()
                    give(v.tensor_tensor(LFf, LFf, BIG, ALU.add))
                    get()
                    link(v.tensor_scalar(KK.rearrange("p d n -> p (d n)"), KK.rearrange("p d n -> p (d n)"), -1.0, 1.0, ALU.mult, ALU.add))
                    v.memset(BIG[:, 0:1536], 1.0).then_inc(v_step, 1)
                    step[0] += 1
                    dve.wait_ge(v_step, step[0])
                    link(v.memset(BIG[:, 0:1536].rearrange("p (n t) -> p n t", t=P)[:, :, 0:1], 0.0))
                    for d in range(2):
                        link(v.tensor_tensor_scan(out=BIG2[:, d * 1536:(d + 1) * 1536], data0=BIG[:, 0:1536],
                                                  data1=LF[:, d, :], initial=0.0, op0=ALU.mult, op1=ALU.add))
                    link(v.tensor_copy(LF[:, 0, :], BIG2[:, 0:1536]))
                    link(v.tensor_tensor(LF[:, 1, :], LF[:, 1, :], BIG2[:, 1536:3072], ALU.subtract))
                    b2 = BIG2[:, 1536:3072].rearrange("p (n t) -> p n t", t=P)
                    l2 = LF[:, 1, :].rearrange("p (n t) -> p n t", t=P)
                    link(v.tensor_tensor(l2, l2, b2[:, :, P - 1:P].to_broadcast([P, GH * NT, P]), ALU.add))
                    for lv, half in enumerate(LEVELS):
                        nb = GH * TOK // (2 * half)
                        for d in range(2):
                            b3 = LF[:, d, :].rearrange("p (n w) -> p n w", w=2 * half)
                            ref = half - 1 if d == 0 else half
                            if lv:
                                dve.wait_ge(bank_filled, number[("lvl", lv - 1, d, NT - 1)] + 1)
                            give(v.tensor_tensor(LE[d].rearrange("p (n w) -> p n w", w=2 * half), b3,
                                                 b3[:, :, ref:ref + 1].to_broadcast([P, nb, 2 * half]), ALU.subtract))
                        for d in range(2):
                            get()
                            link(v.tensor_tensor(LK[d], LE[d], KK[:, d, :], ALU.mult))
                            feed(v.tensor_tensor(LE[d], LE[d], QHf, ALU.mult))
                            for t in range(NT):
                                b = filled(dve, ("lvl", lv, d, t))
                                emptied_by_me(v.copy_predicated(ATT[:, t], MASK[:, 2 * lv + d].unsqueeze(1).to_broadcast([P, GH, P]),
                                                                b[:, :].rearrange("p (h n) -> p h n", h=GH)))
                    feed(v.tensor_tensor(LK[0], KK[:, 0, :], KK[:, 1, :], ALU.add))
                    dve.wait_ge(to_pe, fed[0])
                    for t in range(NT):
                        b = filled(dve, ("diag", t))
                        emptied_by_me(v.copy_predicated(ATT[:, t], MASK[:, 14].unsqueeze(1).to_broadcast([P, GH, P]),
                                                        b[:, :].rearrange("p (h n) -> p h n", h=GH)))
                    UNITS = ((0, 0), (1, 0), (0, 1), (1, 2))
                    for u, (d, t) in enumerate(UNITS):
                        b3 = LF[:, d, :].rearrange("p (h n) -> p h n", h=GH)[:, :, t * P:(t + 1) * P]
                        end = b3[:, :, P - 1:P] if d == 0 else b3[:, :, 0:1]
                        link(v.tensor_tensor(KD4[:, u, :].rearrange("p (h n) -> p h n", h=GH),
                                             end.to_broadcast([P, GH, P]), b3, ALU.subtract))
                        if u >= 2:
                            link(v.tensor_copy(smallp[:, u - 2, 0:4].unsqueeze(2), end))
                            link(v.tensor_copy(smallp[:, u - 2, 4:8].unsqueeze(2), end))
                    for d in range(2):
                        b3 = LF[:, d, :].rearrange("p (h n) -> p h n", h=GH)[:, :, P:TOK]
                        ins = v.tensor_copy(QI[:, d, :].rearrange("p (h n) -> p h n", h=GH), b3)
                    give(ins)
                    get()
                    for u, (d, t) in enumerate(UNITS):
                        k3 = KK[:, d, :].rearrange("p (h n) -> p h n", h=GH)[:, :, t * P:(t + 1) * P]
                        kd = KD4[:, u, :].rearrange("p (h n) -> p h n", h=GH)
                        ins = v.tensor_tensor(kd, kd, k3, ALU.mult)
                    for d in range(2):
                        qi = QI[:, d, :].rearrange("p (h n) -> p h n", h=GH)
                        ins = v.tensor_tensor(qi, qi, QH[:, :, P:TOK], ALU.mult)
                    ins.then_inc(out_ready, 1)
                    dve.wait_ge(out_ready, 1)
                    fed[0] += 1
                    dve.sem_inc(to_pe, 1)
                    for u in range(2):
                        b = filled(dve, ("state", u))
                        v.tensor_copy(ST[:, 2 + u, :], b[:, :]).then_inc(out_ready, 1)
                        dve.wait_ge(out_ready, 2 + u)
                        dve.sem_inc(emptied["v"], 1)
                    dve.wait_ge(l1params_in, 80)
                    for u in (2, 3):
                        b = filled(dve, ("state", u))
                        for h in range(GH):
                            hs = slice(h * P, (h + 1) * P)
                            ins = v.scalar_tensor_tensor(out=ST[:, 2 + u, hs], in0=ST[:, u - 2, hs], scalar=smallp[:, u - 2, h:h + 1],
                                                         in1=b[:, hs], op0=ALU.mult, op1=ALU.add)
                        emptied_by_me(ins)
                    emptied_now(dve, ("o", 2))
                    ob = OB.rearrange("p t n -> p (t n)")
                    link(v.tensor_tensor(OB2.rearrange("p t n -> p (t n)"), ob, ob, ALU.mult))
                    link(v.tensor_reduce(out=small[:, 16:28], in_=OB2.rearrange("p t (h n) -> p (t h) n", h=GH), axis=AX, op=ALU.add))
                    give(v.tensor_scalar(small[:, 16:28], small[:, 16:28], 1.0 / P, None, ALU.mult))
                    get()
                    o3 = OB.rearrange("p t (h n) -> p (t h) n", h=GH)
                    link(v.tensor_tensor(o3, o3, small[:, 48:60].unsqueeze(2).to_broadcast([P, 12, P]), ALU.mult))
                    link(v.tensor_tensor(o3, o3, gnw[:].unsqueeze(1).to_broadcast([P, 12, P]), ALU.mult))
                    for t in range(NT):
                        feed(v.tensor_tensor(MIX[:, t, 512:1024], OB[:, t, :], GG[:, t, :], ALU.mult))
                else:
                    emptied_now(dve, ("dqkv", 1, 2))
                    for t in range(NT):
                        for j, (lo, n) in enumerate(((0, QR), (QR, KVR))):
                            link(v.tensor_tensor_reduce(out=SQ[:, 0:n], in0=CQ[:, t, lo:lo + n], in1=CQ[:, t, lo:lo + n],
                                                        scale=1.0 / n, scalar=0.0, op0=ALU.mult, op1=ALU.add,
                                                        accum_out=small[:, 16 + 2 * t + j:17 + 2 * t + j]))
                    dve.sem_inc(to_act, 1)
                    v.memset(KR, 0.0).then_inc(out_ready, 1)
                    dve.wait_ge(out_ready, 4)
                    get()
                    dve.wait_ge(l1params_in, 16 * 9)
                    for t in range(NT):
                        for j, (lo, n) in enumerate(((0, QR), (QR, KVR))):
                            r = small[:, 48 + 2 * t + j:49 + 2 * t + j]
                            ins = v.scalar_tensor_tensor(out=CQ[:, t, lo:lo + n], in0=CQ[:, t, lo:lo + n], scalar=r,
                                                         in1=qnw[:, lo:lo + n], op0=ALU.mult, op1=ALU.mult)
                    ins.then_inc(out_ready, 1)
                    for t in (1, 2):
                        x = CQ[:, t, QR + KVR:]
                        link(v.tensor_tensor(KR[:, t + 1, 64:96], x, rope32[:, t - 1, 0], ALU.mult))
                        for half in range(4):
                            o = half ^ 1
                            link(v.tensor_tensor(SQ[:, 8 * half:8 * half + 8], x[:, 8 * o:8 * o + 8],
                                                 rope32[:, t - 1, 1, 8 * half:8 * half + 8], ALU.mult))
                        link(v.tensor_tensor(KR[:, t + 1, 64:96], KR[:, t + 1, 64:96], SQ[:, 0:32], ALU.add))
                    link(v.tensor_copy(KR[:, 0, 64:96], CQ[:, 0, QR + KVR:]))
                    fed[0] += 1
                    dve.sem_inc(to_pe, 1)
                    for t in range(NT):
                        b = filled(dve, ("cqT", t))
                        emptied_by_me(v.tensor_copy(CQT[:, :, t * P:(t + 1) * P], b[:, 0:TOK].rearrange("p (c n) -> p c n", c=3)))
                    for k in range(2):
                        b = filled(dve, ("ckvT", k))
                        for j in range(2):
                            ins = v.tensor_copy(CKVT[:, :, (2 * k + j) * P:(2 * k + j + 1) * P],
                                                b[:, 2 * j * P:(2 * j + 2) * P].rearrange("p (c n) -> p c n", c=2))
                        emptied_by_me(ins)
                    b = filled(dve, ("krT",))
                    emptied_by_me(v.tensor_copy(KRT[64:96, :], b[64:96, :]))
                    emptied_now(dve, ("krT",))
                    attention(1)
                    emptied_now(dve, ("pv", 1, 11))
                    for t in range(NT):
                        fed[0] += 1
                        dve.sem_inc(to_pe, 1)
                to_features("mixT", layer)
                residual(layer)
                dve.sem_inc(mod_free, 1)
                adaln("h2T", layer, CONSTS + 16 + 32 * layer, 2 * layer + 2)
                route(layer)
                experts(layer)
                dve.sem_inc(mod_free, 1)
            rstd(X, D)
            dve.wait_ge(consts_in, CONSTS + 64)
            for t in range(NT):
                ins = v.scalar_tensor_tensor(out=MIX[:, t, :], in0=X[:, t, :], scalar=small[:, 8 + t:9 + t],
                                             in1=normw[:], op0=ALU.mult, op1=ALU.mult)
            ins.then_inc(out_ready, 1)


_CONSTANTS = ("k_ident", "k_mask", "k_band", "k_rope64", "k_rope32", "k_ropeT")


def _constants():
    import numpy as np
    s, t = np.arange(P)[:, None], np.arange(P)[None, :]
    masks = []
    for h in LEVELS:
        same = s // (2 * h) == t // (2 * h)
        masks.append(same & (s % (2 * h) < h) & (t % (2 * h) >= h))
        masks.append(same & (s % (2 * h) >= h) & (t % (2 * h) < h))
    masks.append(s == t)
    band = np.zeros((P, 2, P), np.float32)
    band[:, 0, :][~(t <= s)] = -8e30
    band[:, 1, :][~(t >= s)] = -8e30

    def angles(dim):
        nf = dim // 4
        inv = np.exp(np.float32(-np.log(10000.0)) * np.arange(nf, dtype=np.float32) / np.float32(nf)).astype(np.float32)
        tok = np.arange(2 * P)
        ang = [(p.astype(np.float32)[:, None] * inv[None]).astype(np.float32) for p in (tok // 64, tok % 64)]
        cos = np.concatenate([np.cos(a) for a in (ang[0], ang[0], ang[1], ang[1])], 1)
        sin = np.concatenate([-np.sin(ang[0]), np.sin(ang[0]), -np.sin(ang[1]), np.sin(ang[1])], 1)
        return cos.astype(np.float32), sin.astype(np.float32)

    out = {"k_ident": np.eye(P, dtype=np.float32), "k_mask": np.stack(masks, 1).astype(np.int32), "k_band": band}
    for dim in (64, 32):
        cos, sin = angles(dim)
        out[f"k_rope{dim}"] = np.ascontiguousarray(np.stack([cos, sin]).reshape(2, 2, P, dim).transpose(2, 1, 0, 3))
    ropeT = np.zeros((P, 2 * P), np.float32)
    ropeT[64:96], ropeT[96:128] = cos.T, sin.T
    out["k_ropeT"] = ropeT
    return out


_INS = ['x_prompt', 'x_sample', 'c', 'cache_swa_k', 'cache_swa_v', 'state_hgrn', 'cache_mla_ckv',
        'cache_mla_krope', 'c_ctx', 'mod_w', 'mod_b', 'norm1_w', 'norm2_w', 'final_norm_w',
        'even_w_in', 'even_w_out', 'swa_sink', 'hgrn_lb_fwd', 'hgrn_lb_bwd', 'hgrn_gnorm_w',
        'mla_w_dq', 'mla_qnorm_w', 'mla_w_uq', 'mla_w_dkv', 'mla_kvnorm_w', 'mla_w_ukv', 'mla_w_o',
        'moe_router_group_w', 'moe_router_group_b', 'moe_router_expert_w', 'moe_router_expert_b',
        'moe_w_gate', 'moe_w_up', 'moe_w_down']
_OUTS = [(1, 128, 1024), (1, 256, 1024), (1, 1, 128, 2, 64), (1, 1, 128, 2, 64), (1, 1, 2, 4, 128, 128),
         (1, 1, 128, 256), (1, 1, 128, 32)]


def kernel(**inputs):
    import numpy as np
    import concourse.bacc as bacc
    from concourse.bass_utils import run_bass_kernel_spmd

    nc = bacc.Bacc("TRN2", target_bir_lowering=False, num_devices=1)
    given = {name: np.ascontiguousarray(inputs[name]) for name in _INS}
    given.update(_constants())
    arrays, I, O = {}, {}, []
    for name, a in given.items():
        arrays[f"in_{name}"] = a
        I[name] = nc.dram_tensor(f"in_{name}", a.shape, mybir.dt.from_np(a.dtype), kind="ExternalInput").ap()
    for i, shape in enumerate(_OUTS):
        O.append(nc.dram_tensor(f"out_{i}", shape, mybir.dt.float32, kind="ExternalOutput").ap())
    mod_dram = nc.dram_tensor("mod_dram", (2, 2, 6 * D), mybir.dt.float32, kind="Internal").ap()
    build(nc, I, O, mod_dram)
    r = run_bass_kernel_spmd(nc, [arrays], core_ids=[0])
    return tuple(r.results[0][f"out_{i}"] for i in range(len(_OUTS)))
```

```python
import concourse.bass as bass
from concourse import mybir
from contextlib import ExitStack

P = 128
D = 1024
DC = D // P
NT = 3
TOK = NT * P
HEADS, KVH, HD = 8, 2, 64
GH = 4
QKV = (HEADS + 2 * KVH) * HD
MH, QR, KVR, RD, ND, VD = 16, 384, 256, 32, 64, 64
EXPERTS, GROUPS, PER = 32, 4, 8
FF = 256
BANKS = 8
PAIRS = EXPERTS // 2
HALF = PAIRS // 2
CAP = 64
RING = 3
SLOT = 4096
LEVELS = [64, 32, 16, 8, 4, 2, 1]
EPS = 1e-6
WORK = 25312
HGRN_SCALE = P ** -0.5
LN2 = 0.6931471805599453
KEYT = 4


def attention_groups(layer):
    return [(g, t) for g in range(2 if layer == 0 else 4) for t in range(NT)]


def key_tiles(t):
    return [0] if t == 0 else [1, 2, 3]


def score_heads(layer, t):
    if t == 0:
        return [[0, 1, 2, 3]] if layer else [[0, 2], [1, 3]]
    return [[0], [1], [2], [3]]


def matmul_jobs():
    jobs = []

    def add(key, eng):
        jobs.append((key, eng))

    def attention(layer):
        groups = attention_groups(layer)

        def scores(n):
            g, t = groups[n]
            if layer == 1 and t == 0:
                for i in range(2):
                    add(("kT", g, i), "v")
                for i in range(4):
                    add(("qT1", g, i), "v")
            for i in range(len(score_heads(layer, t))):
                add(("score", layer, n, i), "a")
        scores(0)
        for n in range(len(groups)):
            if n + 1 < len(groups):
                scores(n + 1)
            for i in range(len(key_tiles(groups[n][1]))):
                add(("pT", layer, n, i), "a" if i == 0 else "v")
            add(("pv", layer, n), "v")

    def to_features(kind, layer):
        for t in range(NT):
            for k in range(2):
                add((kind, layer, t, k), "v" if k else "a")

    for layer in range(2):
        for b in range(12):
            add(("mod", layer, b), "v")
        to_features("hT", layer)
        if layer == 0:
            for b in (0, 1):
                for t in range(NT):
                    add(("qkv", b, t), "a")
            for b in range(3):
                for h in range(GH):
                    add(("qff", b, h), "a")
            for b in range(2):
                for t in range(NT):
                    add(("vg", b, t), "a")
            for t in range(NT):
                add(("qT", t), "v")
            for k in range(2):
                add(("kT0", k), "v")
            attention(0)
            for lv in range(len(LEVELS)):
                for d in range(2):
                    for t in range(NT):
                        add(("lvl", lv, d, t), "v")
            for t in range(NT):
                add(("diag", t), "v")
            for u in range(4):
                add(("kdT", u), "a")
                add(("state", u), "v")
            for t in range(NT):
                add(("o", t), "a")
        else:
            for b in range(2):
                for t in range(NT):
                    add(("dqkv", b, t), "a")
            for t in range(NT):
                add(("cqT", t), "v")
            for k in range(2):
                add(("ckvT", k), "v")
            add(("krT",), "v")
            for kt in range(KEYT):
                for k in range(2):
                    add(("val", kt, k), "a")
            attention(1)
        to_features("mixT", layer)
        for n in range(2):
            for t in range(NT):
                add(("proj", layer, n, t), "v")
        to_features("h2T", layer)
        add(("router", layer), "v")
        add(("pos", layer), "v")
        add(("slot", layer), "v")
    return jobs


def build(nc, I, O, mod_dram, h2_dram, y_dram):
    f32, i32 = mybir.dt.float32, mybir.dt.int32
    ALU, ACT = mybir.AluOpType, mybir.ActivationFunctionType
    AX = mybir.AxisListType.X

    jobs = matmul_jobs()
    number = {key: n for n, (key, _) in enumerate(jobs)}
    drains = []
    count = {"v": 0, "a": 0}
    for _, e in jobs:
        count[e] += 1
        drains.append(count[e])

    with ExitStack() as ctx:
        def sb(name, shape, dt=f32):
            return ctx.enter_context(nc.sbuf_tensor(name, shape, dt))

        def sem(name):
            return ctx.enter_context(nc.semaphore(name))

        X = sb("X", [P, NT, D])
        hT = sb("hT", [P, DC, TOK])
        MOD = sb("MOD", [P, 2, 3, D])
        RINGB = sb("RINGB", [P, RING, SLOT])
        W = sb("W", [P, WORK])
        ident = sb("ident", [P, P])
        normw = sb("normw", [P, D])
        WR = sb("WR", [P, DC, 36])
        BR = sb("BR", [P, 36])
        cond = sb("cond", [P, 2, DC])
        cond2 = sb("cond2", [P, 2, DC])
        small = sb("small", [P, 64])
        banks = [ctx.enter_context(nc.psum_tensor(f"bank{i}", [P, 512], f32)) for i in range(BANKS)]

        def cut(at, shape, dt=None):
            n = 1
            for s in shape:
                n *= s
            v = W[:, at:at + n]
            if dt is not None:
                v = v.bitcast(dt)
            if len(shape) == 2:
                v = v.rearrange("p (a b) -> p a b", a=shape[0])
            if len(shape) == 3:
                v = v.rearrange("p (a b c) -> p a b c", a=shape[0], b=shape[1])
            return v

        modbias = cut(0, (2, 512))
        modrow = cut(1024, (2, 512))
        MIX = cut(0, (NT, D))
        ATT = cut(3072, (NT, GH, P))
        QH = cut(4608, (GH, TOK))
        LF = cut(6144, (2, GH * TOK))
        KK = cut(9216, (2, GH * TOK))
        VV = cut(12288, (NT, GH * P))
        GG = cut(13824, (NT, GH * P))
        MASK = cut(15360, (15, P), i32)
        T0 = 17280
        QKVt = cut(T0, (NT, QKV))
        QT = cut(T0 + 2304, (4, TOK))
        KT = cut(T0 + 3840, (2, KEYT * P))
        KD = cut(T0 + 4864, (KEYT, KVH, 2 * HD))
        ROT = cut(T0 + 5888, (2, 640))
        VC = cut(T0 + 7424, (P,))
        band = cut(T0 + 7552, (2, P))
        P0 = [cut(9216 + 1536 * i, (4, TOK)) for i in range(2)]
        PT0 = [cut(3072, (NT, 4 * P)), cut(T0 + 5888, (NT, 4 * P))]
        LE = [cut(T0 + 3072 * i, (GH * TOK,)) for i in range(2)]
        LK = [cut(T0 + 3072 * i + 1536, (GH * TOK,)) for i in range(2)]
        BIG = cut(T0, (2 * GH * TOK,))
        BIG2 = cut(T0 + 3072, (2 * GH * TOK,))
        KD4 = cut(T0, (4, GH * P))
        KDT = cut(T0 + 2048, (4, GH * P))
        QI = cut(T0 + 4096, (2, GH * 2 * P))
        ST = cut(9216, (6, GH * P))
        OB = cut(T0, (NT, GH * P))
        OB2 = cut(T0 + 1536, (NT, GH * P))
        CQ = cut(3072, (NT, QR + KVR + RD))
        CACHE = cut(5088, (KVR,))
        KR = cut(5344, (KEYT, 96))
        CQT = cut(5728, (3, TOK))
        CKVT = cut(6880, (2, KEYT * P))
        VAL = cut(7904, (KEYT, MH * VD))
        Q1 = [cut(12000 + 1536 * i, (4, TOK)) for i in range(2)]
        K1 = [cut(15072 + 2048 * i, (4, KEYT * P)) for i in range(2)]
        P1 = [cut(19168 + 1536 * i, (4, TOK)) for i in range(2)]
        PT1 = [cut(22240, (NT, 4 * P))]
        KRT = cut(23776, (KEYT * P,))
        SQ = cut(24288, (QR,))
        qnw = cut(24672, (QR + KVR,))
        WQB = cut(3072, (3, 4 * P))
        RINGF = RINGB[:].rearrange("p s n -> p (s n)")
        WSET = [RINGF, cut(0, (3 * SLOT,))]
        XG = [cut(12288 + 1024 * i, (D,)) for i in range(2)]
        XGT = [cut(14336 + 1024 * i, (DC, P)) for i in range(2)]
        YS = [cut(16384 + 1024 * i, (D,)) for i in range(2)]
        ACTV = [cut(18432 + 256 * i, (FF,)) for i in range(2)]
        GE = [cut(18944 + 256 * i, (FF,)) for i in range(2)]
        ACTT = [cut(19456 + 256 * i, (2, P)) for i in range(2)]
        RT = cut(19968, (NT * 36 * 4,))
        COMB = cut(20400, (NT, EXPERTS))
        OVER = cut(20496, (NT, EXPERTS))
        S12 = cut(20592, (2 * NT, EXPERTS))
        SEL = cut(20784, (NT, EXPERTS))
        POS = cut(20880, (NT, EXPERTS))
        PROD = cut(20976, (2 * NT, EXPERTS))
        LOHI = cut(21168, (8, 2 * NT))
        OHLO = cut(21216, (2 * NT, P))
        OHHI = cut(21984, (2 * NT, PAIRS))
        SEL2 = cut(22112, (NT, EXPERTS))
        IDX = cut(22080, (PAIRS,), i32)
        ROWI = cut(22096, (2 * NT,), i32)
        FULL = cut(22106, (1,), i32)
        FULLF = cut(22107, (1,))
        YG = cut(0, (2 * NT, D))
        YACC = cut(0, (NT, D))
        EE = cut(3200, (2, TOK))
        AT = cut(5000, (2, 2, TOK))

        rope_cs = sb("rope_cs", [P, 2, 2, HD])
        rope32 = sb("rope32", [P, 2, 2, RD])
        ropeT = sb("ropeT", [P, 2 * P])
        smallp = sb("smallp", [P, 3, 32])
        sink = sb("sink", [P, HEADS])
        lbc = sb("lbc", [P, 2, GH])
        lbs = sb("lbs", [P, 6, 2, GH])
        gnw = sb("gnw", [P, P])
        iota = sb("iota", [P, 16])
        tri = sb("tri", [P, 2, P])
        ktab = sb("ktab", [P, P + PAIRS + 2 * EXPERTS + NT])

        consts_in = sem("consts_in")
        cond_in = sem("cond_in")
        tokens_in = sem("tokens_in")
        weight_in = [sem(f"weight_in{i}") for i in range(RING)]
        modbias_in = [sem(f"modbias_in{i}") for i in range(2)]
        block_used = sem("block_used")
        bank_filled = sem("bank_filled")
        emptied = {"v": sem("emptied_by_vector"), "a": sem("emptied_by_scalar")}
        v_step = sem("v_step")
        a_step = sem("a_step")
        to_act = sem("input_for_scalar")
        from_act = sem("output_of_scalar")
        to_pe = sem("input_for_tensor")
        cond_ready = sem("cond_ready")
        modrow_ready = sem("modrow_ready")
        modrow_out = [sem(f"modrow_out{i}") for i in range(2)]
        mod_in = sem("mod_in")
        mod_free = sem("mod_free")
        router_in = sem("router_in")
        l1params_in = sem("l1params_in")
        pool_free = sem("pool_free")
        stored = sem("stored")
        out_ready = sem("out_ready")
        experts_over = sem("experts_over")
        h2_made = sem("h2_made")
        h2_out = sem("h2_out")
        pair_gu_in = [sem(f"pair_gu_in{i}") for i in range(2)]
        pair_dn_in = [sem(f"pair_down_in{i}") for i in range(2)]
        gathered = [sem(f"gathered{i}") for i in range(2)]
        idx_ready = sem("idx_ready")
        xt_filled = sem("xt_filled")
        xt_ready = {"v": sem("xt_ready_v"), "a": sem("xt_ready_a")}
        gu_filled = sem("gu_filled")
        gexp_ready = sem("gexp_ready")
        act_made = sem("act_made")
        actt_filled = sem("actt_filled")
        actt_ready = sem("actt_ready")
        y_filled = sem("y_filled")
        y_copied = {"v": sem("y_copied_v"), "a": sem("y_copied_a")}
        y_out = [sem(f"y_out{i}") for i in range(2)]
        y_back = [sem(f"y_back{i}") for i in range(NT)]
        p_step = sem("v_step_in_pairs")
        combined = sem("combined")
        fb = [{k: sem(f"every{layer}_{k}") for k in ("gu_in0", "gu_in1", "dn_in0", "dn_in1", "gu_done", "gexp_done",
                                                     "act_ready", "y_done", "y_emptied", "step", "chain")}
              for layer in range(2)]

        blocks = []

        def rows(ap, chunks):
            return ap.rearrange("(p c) n -> p c n", c=chunks)

        for layer in range(2):
            for b in range(12):
                blocks.append((("mod", layer, b), rows(I["mod_w"][layer], DC)[:, :, b * 512:b * 512 + 512], (DC, 512)))
            if layer == 0:
                win = rows(I["even_w_in"][0], DC)
                for b, (lo, hi) in enumerate([(0, 512), (512, 768), (768, 1280), (1280, 1792), (1792, 2304),
                                              (2304, 2816), (2816, 3328)]):
                    blocks.append((("win", b), win[:, :, lo:hi], (DC, hi - lo)))
                for n in range(2):
                    blocks.append((("wout", 0, n), rows(I["even_w_out"][0], DC)[:, :, n * 512:n * 512 + 512], (DC, 512)))
            else:
                blocks.append((("dq",), rows(I["mla_w_dq"][0], DC), (DC, QR)))
                blocks.append((("dkv",), rows(I["mla_w_dkv"][0], DC), (DC, KVR + RD)))
                blocks.append((("ukv",), rows(I["mla_w_ukv"][0], 2), (2, 2048)))
                for n in range(2):
                    blocks.append((("uq", n), rows(I["mla_w_uq"][0], 3)[:, :, n * 768:n * 768 + 768], (3, 768)))
                for n in range(2):
                    blocks.append((("wout", 1, n), rows(I["mla_w_o"][0], DC)[:, :, n * 512:n * 512 + 512], (DC, 512)))
        blockno = {key: n for n, (key, _, _) in enumerate(blocks)}
        first1 = blockno[("mod", 1, 0)]

        def block_view(key):
            n = blockno[key]
            c, w = blocks[n][2]
            return RINGB[:, n % RING, 0:c * w].rearrange("p (c n) -> p c n", c=c)

        def weights_arrived(eng, key):
            n = blockno[key]
            eng.wait_ge(weight_in[n % RING], 16 * (n // RING + 1))

        def filled(eng, key):
            n = number[key]
            eng.wait_ge(bank_filled, n + 1)
            return banks[n % BANKS]

        def emptied_now(eng, key):
            n = number[key]
            eng.wait_ge(emptied[jobs[n][1]], drains[n])

        block = ctx.enter_context(nc.Block())

        wg = lambda layer, e: I["moe_w_gate"][layer, e, :, :].rearrange("(p c) n -> p c n", c=DC)
        wu = lambda layer, e: I["moe_w_up"][layer, e, :, :].rearrange("(p c) n -> p c n", c=DC)
        wd = lambda layer, e: I["moe_w_down"][layer, e, :, :].rearrange("(p c) n -> p c n", c=2)

        def gu_slot(q):
            return RINGB[:, q, :].rearrange("p (g c n) -> p g c n", g=2, c=DC)

        def dn_slot(q):
            return RINGB[:, 2, q * 2048:q * 2048 + 2048].rearrange("p (c n) -> p c n", c=2)

        def pair_gu(sset):
            return WSET[sset][:, 0:8192].rearrange("p (e g n) -> p e g n", e=2, g=2)

        def pair_dn(sset):
            return WSET[sset][:, 8192:12288].rearrange("p (e n) -> p e n", e=2)

        def at_least(eng, semaphore, value):
            if not isinstance(value, int) or value > 0:
                eng.wait_ge(semaphore, value)

        def overflow(eng):
            return eng.value_load(FULL[0:1, 0:1], min_val=0, max_val=TOK) > CAP

        def over_pairs(eng, step):
            with eng.Fori(0, HALF - 1) as k:
                for j in range(2):
                    step(2 * k + 1 + j, (1 + j) % 2)

        @block.sync
        def _(sp):
            def load(n):
                if n >= RING:
                    sp.wait_ge(block_used, n - RING + 1)
                key, src, (c, w) = blocks[n]
                sp.dma_start(block_view(key), src).then_inc(weight_in[n % RING], 16)
                if key[0] == "mod":
                    b = key[2]
                    if key[1] and b == 0:
                        sp.wait_ge(mod_free, 2)
                    if b >= 2:
                        sp.wait_ge(modrow_ready, 12 * key[1] + b - 1)
                    for g in range(2):
                        sp.dma_start(modbias[g:g + 1, b % 2, :],
                                     I["mod_b"][key[1]:key[1] + 1, b * 512:b * 512 + 512]).then_inc(modbias_in[b % 2], 16)

            def pairs(layer):
                B = PAIRS * layer

                def load_pair(i, q):
                    def part(name):
                        if isinstance(i, int):
                            return I[name][layer, 2 * i:2 * i + 2]
                        return I[name][layer, bass.ds(2 * i, 2)]
                    gu, dn = pair_gu(q), pair_dn(q)
                    if not (isinstance(i, int) and i < 2):
                        sp.wait_ge(gu_filled, B + i - 1)
                    for g, name in enumerate(("moe_w_gate", "moe_w_up")):
                        sp.dma_start(gu[:, :, g, :], part(name).rearrange("e (p c) n -> p e (c n)", c=DC)).then_inc(pair_gu_in[q], 16)
                    if not (isinstance(i, int) and i < 2):
                        sp.wait_ge(y_filled, B + i - 1)
                    sp.dma_start(dn, part("moe_w_down").rearrange("e (p c) n -> p e (c n)", c=2)).then_inc(pair_dn_in[q], 16)

                sp.wait_ge(block_used, first1 if layer == 0 else len(blocks))
                load_pair(0, 0)
                sp.wait_ge(h2_out, 16 * (layer + 1))
                sp.wait_ge(bank_filled, number[("h2T", layer, NT - 1, 1)] + 1)
                load_pair(1, 1)
                with sp.Fori(0, HALF - 1) as k:
                    for q in range(2):
                        load_pair(2 * k + 2 + q, q)

            def every_expert(layer):
                F = fb[layer]

                def load_expert(e, q, after):
                    if after is not None:
                        sp.wait_ge(F["gu_done"], after)
                    sp.dma_start(gu_slot(q)[:, 0], wg(layer, e)).then_inc(F[f"gu_in{q}"], 16)
                    sp.dma_start(gu_slot(q)[:, 1], wu(layer, e)).then_inc(F[f"gu_in{q}"], 16)
                    if after is not None:
                        sp.wait_ge(F["y_done"], after * 3)
                    sp.dma_start(dn_slot(q), wd(layer, e)).then_inc(F[f"dn_in{q}"], 16)

                sp.wait_ge(combined, layer + 1)
                with sp.If(overflow(sp)):
                    for q in range(2):
                        load_expert(q, q, None)
                    with sp.Fori(0, EXPERTS // 2 - 1) as i:
                        for q in range(2):
                            load_expert(2 * i + 2 + q, q, 4 * i + 2 * q + 2)

            for n in range(first1):
                load(n)
            pairs(0)
            every_expert(0)
            sp.wait_ge(experts_over, 1)
            for n in range(first1, len(blocks)):
                load(n)
            pairs(1)
            every_expert(1)

        @block.gpsimd
        def _(pool):
            def dma(out, src, s):
                pool.dma_start(out, src).then_inc(s, 16)
            dma(cond2[:, 0, :], I["c_ctx"].rearrange("(p c) -> p c", c=DC), cond_in)
            dma(cond2[:, 1, :], I["c"][0].rearrange("(p c) -> p c", c=DC), cond_in)
            dma(X[:, 0, :], I["x_prompt"][0], tokens_in)
            dma(X[:, 1:3, :], I["x_sample"][0].rearrange("(t p) d -> p t d", p=P), tokens_in)
            dma(ident[:], I["k_ident"], consts_in)
            dma(MASK, I["k_mask"], consts_in)
            dma(rope_cs[:], I["k_rope64"], consts_in)
            dma(rope32[:], I["k_rope32"], consts_in)
            dma(ropeT[:], I["k_ropeT"], consts_in)
            dma(sink[:], I["swa_sink"][0:1, :].to_broadcast([P, HEADS]), consts_in)
            dma(gnw[:], I["hgrn_gnorm_w"][0:1, :].to_broadcast([P, P]), consts_in)
            dma(band, I["k_band"], consts_in)
            dma(tri[:], I["k_tri"], consts_in)
            dma(ktab[:], I["k_tab"], consts_in)
            dma(normw[:], I["norm1_w"][0:1, :].to_broadcast([P, D]), consts_in)
            for d, nm in enumerate(("hgrn_lb_fwd", "hgrn_lb_bwd")):
                with nc.allow_non_contiguous_dma(reason="512 values, once"):
                    dma(lbc[:, d, :], I[nm][0].rearrange("(h p) -> p h", p=P), consts_in)

            def modulation(layer, part, nth):
                if nth:
                    pool.wait_ge(mod_free, nth)
                for par in range(2):
                    pool.wait_ge(modrow_out[par], 16 * 6 * (layer + 1))
                for g in range(2):
                    src = mod_dram[layer, g:g + 1, part * 3 * D:(part + 1) * 3 * D]
                    dma(MOD[:, g, :, :].rearrange("p v d -> p (v d)"), src.to_broadcast([P, 3 * D]), mod_in)

            def rowblocks(layer):
                for b in range(12):
                    pool.wait_ge(modrow_ready, 12 * layer + b + 1)
                    dma(mod_dram[layer, :, b * 512:b * 512 + 512], modrow[0:2, b % 2, :], modrow_out[b % 2])

            def router(layer):
                if layer:
                    emptied_now(pool, ("router", 0))
                dma(WR[:, :, 0:4], I["moe_router_group_w"][layer].rearrange("(p c) n -> p c n", c=DC), router_in)
                for g in range(GROUPS):
                    dma(WR[:, :, 4 + 8 * g:12 + 8 * g],
                        I["moe_router_expert_w"][layer, g].rearrange("(p c) n -> p c n", c=DC), router_in)
                dma(BR[:, 0:4], I["moe_router_group_b"][layer:layer + 1, :].to_broadcast([P, 4]), router_in)
                dma(BR[:, 4:36], I["moe_router_expert_b"][layer].rearrange("g e -> (g e)").unsqueeze(0).to_broadcast([P, 32]), router_in)

            def pairs(layer):
                B = PAIRS * layer
                pool.wait_ge(h2_made, layer + 1)
                dma(h2_dram.rearrange("(t p) d -> p t d", p=P), MIX, h2_out)
                pool.wait_ge(h2_out, 16 * (layer + 1))
                pool.wait_ge(idx_ready, layer + 1)

                def gather(i, q):
                    if i >= 2:
                        pool.wait_ge(xt_filled, B + i - 1)
                    pool.indirect_dma_start(XG[q], None, h2_dram, bass.IndirectOffsetOnAxis(ap=IDX[:, i:i + 1], axis=0))\
                        .then_inc(gathered[q], 16)

                def store(i, q):
                    pool.wait_ge(y_copied["v"], B + i + 1)
                    pool.wait_ge(y_copied["a"], B + i + 1)
                    dma(y_dram[i], YS[q], y_out[q])

                gather(0, 0)
                gather(1, 1)
                for i in range(PAIRS):
                    if i + 2 < PAIRS:
                        gather(i + 2, i % 2)
                    store(i, i % 2)
                for q in range(2):
                    pool.wait_ge(y_out[q], 16 * HALF * (layer + 1))
                for t in range(NT):
                    for j in range(2):
                        pool.indirect_dma_start(YG[:, j * NT + t, :], None, y_dram.rearrange("a p d -> (a p) d"),
                                                bass.IndirectOffsetOnAxis(ap=ROWI[:, j * NT + t:j * NT + t + 1], axis=0))\
                            .then_inc(y_back[t], 16)

            router(0)
            rowblocks(0)
            modulation(0, 0, 0)
            for dup in range(2):
                dma(KD[:, 1, :, dup * HD:dup * HD + HD], I["cache_swa_k"][0, 0], l1params_in)
            dma(VC, I["cache_swa_v"][0, 0].rearrange("s h d -> s (h d)"), l1params_in)
            emptied_now(pool, ("qkv", 1, 0))
            dma(O[2][0, 0].rearrange("s h d -> s (h d)"), QKVt[:, 0, 512:640], stored)
            dma(O[3][0, 0].rearrange("s h d -> s (h d)"), QKVt[:, 0, 640:768], stored)
            pool.wait_ge(out_ready, 1)
            dma(ST[:, 0, :].rearrange("p (h e) -> p h e", h=GH), I["state_hgrn"][0, 0, 0].rearrange("h k v -> k h v"), l1params_in)
            dma(ST[:, 1, :].rearrange("p (h e) -> p h e", h=GH), I["state_hgrn"][0, 0, 1].rearrange("h k v -> k h v"), l1params_in)
            for d in range(2):
                pool.wait_ge(out_ready, 2 + d)
                dma(O[4][0, 0, d].rearrange("h k v -> k h v"), ST[:, 2 + d, :].rearrange("p (h e) -> p h e", h=GH), stored)
            modulation(0, 1, 1)
            pool.wait_ge(pool_free, 1)
            dma(normw[:], I["norm2_w"][0:1, :].to_broadcast([P, D]), consts_in)
            pairs(0)
            dma(normw[:], I["norm1_w"][1:2, :].to_broadcast([P, D]), consts_in)
            router(1)
            rowblocks(1)
            modulation(1, 0, 2)
            dma(qnw[:, 0:QR], I["mla_qnorm_w"][0:1, :].to_broadcast([P, QR]), l1params_in)
            dma(qnw[:, QR:QR + KVR], I["mla_kvnorm_w"][0:1, :].to_broadcast([P, KVR]), l1params_in)
            dma(CACHE, I["cache_mla_ckv"][0, 0], l1params_in)
            pool.wait_ge(out_ready, 4)
            dma(KR[:, 1, 64:96], I["cache_mla_krope"][0, 0], l1params_in)
            pool.wait_ge(out_ready, 5)
            dma(O[5][0, 0], CQ[:, 0, QR:QR + KVR], stored)
            dma(O[6][0, 0], CQ[:, 0, QR + KVR:], stored)
            modulation(1, 1, 3)
            pool.wait_ge(pool_free, 3)
            dma(normw[:], I["norm2_w"][1:2, :].to_broadcast([P, D]), consts_in)
            pairs(1)
            dma(normw[:], I["final_norm_w"].unsqueeze(0).to_broadcast([P, D]), consts_in)
            pool.wait_ge(out_ready, 6)
            dma(O[0][0], MIX[:, 0, :], stored)
            dma(O[1][0].rearrange("(t p) d -> p t d", p=P), MIX[:, 1:3, :], stored)
            pool.wait_ge(stored, 16 * 8)

        CONSTS = 16 * 13

        @block.tensor
        def _(pe):
            inputs = [0]

            def new_input():
                inputs[0] += 1
                pe.wait_ge(to_pe, inputs[0])

            def bank(key):
                n = number[key]
                if n >= BANKS:
                    pe.wait_ge(emptied[jobs[n - BANKS][1]], drains[n - BANKS])
                return banks[n % BANKS]

            def contract(out, lhs, rhs, chunks):
                for c in range(chunks):
                    last = nc.tensor.matmul(out, lhs(c), rhs(c), start=(c == 0), stop=(c == chunks - 1))
                return last

            def transposed(kind, layer, src):
                for t in range(NT):
                    new_input()
                    for k in range(2):
                        b = bank((kind, layer, t, k))
                        for j in range(4):
                            last = nc.tensor.transpose(b[:, j * P:(j + 1) * P], src[:, t, 4 * k + j::DC], ident[:])
                        last.then_inc(bank_filled, 1)

            def modulation(layer):
                for b in range(12):
                    key = ("mod", layer, b)
                    weights_arrived(pe, key)
                    w = block_view(key)
                    out = bank(key)
                    contract(out[0:2, :], lambda c: cond[:, :, c], lambda c: w[:, c, :], DC).then_inc(bank_filled, 1)
                    used(key)

            def used(key):
                pe.wait_ge(bank_filled, number[key] + 1)
                pe.sem_inc(block_used, 1)

            def attention(layer):
                groups = attention_groups(layer)

                def scores(n):
                    g, t = groups[n]
                    if layer == 1 and t == 0:
                        if g == 0:
                            weights_arrived(pe, ("uq", 0))
                        if g == 2:
                            weights_arrived(pe, ("uq", 1))
                        kv = block_view(("ukv",)).rearrange("p c (h n) -> p c h n", h=MH)
                        for i in range(2):
                            key = ("kT", g, i)
                            out = bank(key)
                            h = 4 * g + 2 * i
                            for j in range(2):
                                last = contract(out[64 * j:64 * j + 64, :], lambda c: kv[:, c, h + j, 0:ND],
                                                lambda c: CKVT[:, c, :], 2)
                            last.then_inc(bank_filled, 1)
                        new_input()
                        for i in range(4):
                            out = bank(("qT1", g, i))
                            contract(out[:, 0:TOK], lambda c: WQB[:, c, i * P:(i + 1) * P], lambda c: CQT[:, c, :], 3)\
                                .then_inc(bank_filled, 1)
                        if g == 3:
                            for _ in range(3):
                                used(("qT1", g, 3))
                        new_input()
                    kts = key_tiles(t)
                    nk = len(kts) * P
                    for i, hs in enumerate(score_heads(layer, t)):
                        out = bank(("score", layer, n, i))
                        for j, h in enumerate(hs):
                            o = out[:, j * nk:(j + 1) * nk]
                            if layer == 0:
                                hh = (4 * g + h) % 2
                                q = QT[64 * hh:64 * hh + 64, (4 * g + h) // 2, t * P:(t + 1) * P]
                                k = KT[64 * hh:64 * hh + 64, g, kts[0] * P:kts[0] * P + nk]
                            else:
                                q = Q1[g % 2][0:96, h, t * P:(t + 1) * P]
                                k = K1[g % 2][0:96, h, kts[0] * P:kts[0] * P + nk]
                            masked = layer == 0 and t > 0
                            last = nc.tensor.matmul(o, q, k, start=True, stop=not masked)
                            if masked:
                                far = 3 if t == 1 else 2
                                last = nc.tensor.matmul(out[:, (far - 1) * P:far * P], ident[:], band[:, t - 1, :],
                                                        start=False, stop=True)
                        last.then_inc(bank_filled, 1)

                scores(0)
                for n, (g, t) in enumerate(groups):
                    if n + 1 < len(groups):
                        scores(n + 1)
                    kts = key_tiles(t)
                    prob = (P0 if layer == 0 else P1)[n % 2]
                    pt = (PT0 if layer == 0 else PT1)
                    pt = pt[n % len(pt)]
                    emptied_now(pe, ("score", layer, n, len(score_heads(layer, t)) - 1))
                    pr = prob.rearrange("p h k -> p (h k)")[:, 0:4 * P * len(kts)].rearrange("p (h k) -> p h k", h=4)
                    for i in range(len(kts)):
                        out = bank(("pT", layer, n, i))
                        for h in range(4):
                            last = nc.tensor.transpose(out[:, h * P:(h + 1) * P], pr[:, h, i * P:(i + 1) * P], ident[:])
                        last.then_inc(bank_filled, 1)
                    out = bank(("pv", layer, n))
                    emptied_now(pe, ("pT", layer, n, 0))
                    emptied_now(pe, ("pT", layer, n, len(kts) - 1))
                    for h in range(4):
                        for i, kt in enumerate(kts):
                            if layer == 0:
                                v = VC[:, g * HD:(g + 1) * HD] if kt == 1 else \
                                    QKVt[:, 0 if kt == 0 else kt - 1, 640 + g * HD:640 + (g + 1) * HD]
                            else:
                                v = VAL[:, kt, (4 * g + h) * VD:(4 * g + h + 1) * VD]
                            last = nc.tensor.matmul(out[:, h * 64:(h + 1) * 64], pt[:, i, h * P:(h + 1) * P], v,
                                                    start=(i == 0), stop=(i == len(kts) - 1))
                    last.then_inc(bank_filled, 1)

            def project(layer):
                transposed("mixT", layer, MIX)
                for n in range(2):
                    weights_arrived(pe, ("wout", layer, n))
                    w = block_view(("wout", layer, n))
                    for t in range(NT):
                        if n == 0:
                            emptied_now(pe, ("mixT", layer, t, 0))
                            emptied_now(pe, ("mixT", layer, t, 1))
                        out = bank(("proj", layer, n, t))
                        contract(out[:, :], lambda c: hT[:, c, t * P:(t + 1) * P], lambda c: w[:, c, :], DC)\
                            .then_inc(bank_filled, 1)
                    used(("proj", layer, n, NT - 1))

            def router(layer):
                transposed("h2T", layer, MIX)
                pe.wait_ge(router_in, 16 * 7 * (layer + 1))
                out = bank(("router", layer))
                for t in range(NT):
                    emptied_now(pe, ("h2T", layer, t, 0))
                    emptied_now(pe, ("h2T", layer, t, 1))
                    last = contract(out[:, t * 36:t * 36 + 36], lambda c: hT[:, c, t * P:(t + 1) * P],
                                    lambda c: WR[:, c, :], DC)
                last.then_inc(bank_filled, 1)

            def assign(layer):
                new_input()
                out = bank(("pos", layer))
                for t in range(NT):
                    cols = out[:, t * EXPERTS:(t + 1) * EXPERTS]
                    last = nc.tensor.matmul(cols, tri[:, 0, :], SEL[:, t, :], start=True, stop=(t == 0))
                    for u in range(t):
                        last = nc.tensor.matmul(cols, tri[:, 1, :], SEL[:, u, :], start=False, stop=(u == t - 1))
                for t in range(NT):
                    last = nc.tensor.matmul(out[:, NT * EXPERTS:(NT + 1) * EXPERTS], tri[:, 1, :], SEL[:, t, :],
                                            start=(t == 0), stop=(t == NT - 1))
                last.then_inc(bank_filled, 1)
                new_input()
                out = bank(("slot", layer))
                for j in range(2 * NT):
                    last = nc.tensor.matmul(out[:, 0:PAIRS], OHLO[:, j, :], OHHI[:, j, :], start=(j == 0), stop=(j == 2 * NT - 1))
                last.then_inc(bank_filled, 1)
                emptied_now(pe, ("slot", layer))

            def pairs(layer):
                B = PAIRS * layer

                def turn(i, q):
                    pe.wait_ge(gathered[q], 16 * (HALF * layer + 1) + 8 * (i - q))
                    for e in ("v", "a"):
                        at_least(pe, xt_ready[e], B + i)
                    for c in range(DC):
                        last = nc.tensor.transpose(banks[c // 4][:, (c % 4) * P:(c % 4 + 1) * P], XG[q][:, c::DC], ident[:])
                    last.then_inc(xt_filled, 1)

                def gate_up(i, q):
                    for e in ("v", "a"):
                        pe.wait_ge(xt_ready[e], B + i + 1)
                    at_least(pe, act_made, B + i - 1)
                    pe.wait_ge(pair_gu_in[q], 32 * (HALF * layer + 1) + 16 * (i - q))
                    w = pair_gu(q).rearrange("p e g (c n) -> p e g c n", c=DC)
                    for c in range(DC):
                        for e in range(2):
                            last = nc.tensor.matmul(banks[2 + q][64 * e:64 * e + 64, :], XGT[q][:, c, 64 * e:64 * e + 64],
                                                    w[:, e, :, c, :], start=(c == 0), stop=(c == DC - 1))
                    last.then_inc(gu_filled, 1)

                def turn_act(i, q):
                    pe.wait_ge(act_made, B + i + 1)
                    at_least(pe, actt_ready, B + i)
                    for f in range(2):
                        last = nc.tensor.transpose(banks[4][:, f * P:(f + 1) * P], ACTV[q][:, f::2], ident[:])
                    last.then_inc(actt_filled, 1)

                def down(i, q):
                    pe.wait_ge(actt_ready, B + i + 1)
                    pe.wait_ge(pair_dn_in[q], 16 * (HALF * layer + 1) + 8 * (i - q))
                    for e in ("v", "a"):
                        at_least(pe, y_copied[e], B + i)
                    w = pair_dn(q).rearrange("p e (c n) -> p e c n", c=2)
                    for n in range(2):
                        for c in range(2):
                            for e in range(2):
                                last = nc.tensor.matmul(banks[5 + n][64 * e:64 * e + 64, :], ACTT[q][:, c, 64 * e:64 * e + 64],
                                                        w[:, e, c, n * 512:(n + 1) * 512], start=(c == 0), stop=(c == 1))
                    last.then_inc(y_filled, 1)

                def step(i, q):
                    gate_up(i, q)
                    down(i - 1, 1 - q)
                    turn(i + 1, 1 - q)
                    turn_act(i, q)

                turn(0, 0)
                gate_up(0, 0)
                turn(1, 1)
                turn_act(0, 0)
                over_pairs(pe, step)
                gate_up(PAIRS - 1, 1)
                down(PAIRS - 2, 0)
                turn_act(PAIRS - 1, 1)
                down(PAIRS - 1, 1)

            def every_expert(layer):
                F = fb[layer]
                pe.wait_ge(combined, layer + 1)
                with pe.If(overflow(pe)):
                    with pe.Fori(0, EXPERTS // 2) as i:
                        for q in range(2):
                            pe.wait_ge(F[f"gu_in{q}"], 32 + 32 * i)
                            for f in range(2):
                                pe.wait_ge(F["act_ready"], 2 * q + f + 1 + 4 * i)
                                for g in range(2):
                                    last = contract(banks[2 * g + f][:, 0:TOK], lambda c: gu_slot(q)[:, g, c, f::2],
                                                    lambda c: hT[:, c, :], DC)
                                last.then_inc(F["gu_done"], 1)
                            pe.wait_ge(F[f"dn_in{q}"], 16 + 16 * i)
                            pe.wait_ge(F["act_ready"], 2 * q + 4 + 4 * i)
                            for j in range(6):
                                n, t = divmod(j, NT)
                                k = 6 * q + j
                                pe.wait_ge(F["y_emptied"], k + 1 + 12 * i)
                                contract(banks[4 + k % 4][:, :], lambda c: AT[:, q, c, t * P:(t + 1) * P],
                                         lambda c: dn_slot(q)[:, c, n * 512:(n + 1) * 512], 2).then_inc(F["y_done"], 1)
                pe.wait_ge(experts_over, layer + 1)

            pe.wait_ge(cond_ready, 1)
            for layer in range(2):
                modulation(layer)
                if layer == 0:
                    pe.wait_ge(consts_in, CONSTS)
                transposed("hT", layer, MIX)
                for t in range(NT):
                    for k in range(2):
                        emptied_now(pe, ("hT", layer, t, k))
                if layer == 0:
                    for b in range(7):
                        weights_arrived(pe, ("win", b))
                        w = block_view(("win", b))
                        if b in (0, 1, 5, 6):
                            for t in range(NT):
                                key = ("qkv", b, t) if b < 2 else ("vg", b - 5, t)
                                out = bank(key)
                                contract(out[:, 0:blocks[blockno[("win", b)]][2][1]],
                                         lambda c: hT[:, c, t * P:(t + 1) * P], lambda c: w[:, c, :], DC)\
                                    .then_inc(bank_filled, 1)
                        else:
                            for h in range(GH):
                                key = ("qff", b - 2, h)
                                out = bank(key)
                                contract(out[:, 0:TOK], lambda c: w[:, c, h * P:(h + 1) * P], lambda c: hT[:, c, :], DC)\
                                    .then_inc(bank_filled, 1)
                        used(key)
                    new_input()
                    for t in range(NT):
                        out = bank(("qT", t))
                        for j in range(4):
                            last = nc.tensor.transpose(out[:, j * P:(j + 1) * P], QKVt[:, t, j * P:(j + 1) * P], ident[:])
                        last.then_inc(bank_filled, 1)
                    for k in range(2):
                        out = bank(("kT0", k))
                        for j in range(4):
                            last = nc.tensor.transpose(out[:, j * P:(j + 1) * P], KD[:, 2 * k + j // 2, j % 2, :], ident[:])
                        last.then_inc(bank_filled, 1)
                    emptied_now(pe, ("qT", 2))
                    emptied_now(pe, ("kT0", 1))
                    attention(0)
                    for lv in range(len(LEVELS)):
                        for d in range(2):
                            new_input()
                            for t in range(NT):
                                out = bank(("lvl", lv, d, t))
                                for h in range(GH):
                                    at = h * TOK + t * P
                                    last = nc.tensor.matmul(out[:, h * P:(h + 1) * P], LK[d][:, at:at + P],
                                                            LE[d][:, at:at + P], start=True, stop=True)
                                last.then_inc(bank_filled, 1)
                    new_input()
                    for t in range(NT):
                        out = bank(("diag", t))
                        for h in range(GH):
                            at = h * TOK + t * P
                            last = nc.tensor.matmul(out[:, h * P:(h + 1) * P], LK[0][:, at:at + P],
                                                    QH[:, h, t * P:(t + 1) * P], start=True, stop=True)
                        last.then_inc(bank_filled, 1)
                    new_input()
                    for u, (d, t) in enumerate(((0, 0), (1, 0), (0, 1), (1, 2))):
                        out = bank(("kdT", u))
                        for h in range(GH):
                            last = nc.tensor.transpose(out[:, h * P:(h + 1) * P], KD4[:, u, h * P:(h + 1) * P], ident[:])
                        last.then_inc(bank_filled, 1)
                        out = bank(("state", u))
                        emptied_now(pe, ("kdT", u))
                        for h in range(GH):
                            last = nc.tensor.matmul(out[:, h * P:(h + 1) * P], KDT[:, u, h * P:(h + 1) * P],
                                                    VV[:, t, h * P:(h + 1) * P], start=True, stop=True)
                        last.then_inc(bank_filled, 1)
                    emptied_now(pe, ("state", 3))
                    emptied_now(pe, ("diag", 2))
                    for t in range(NT):
                        out = bank(("o", t))
                        for h in range(GH):
                            hs = slice(h * P, (h + 1) * P)
                            last = nc.tensor.matmul(out[:, hs], ATT[:, t, h, :], VV[:, t, hs], start=True, stop=(t == 0))
                            if t:
                                at = (h * 2 + t - 1) * P
                                for d in range(2):
                                    s = (0 if t == 1 else 4) if d == 0 else (1 if t == 2 else 5)
                                    last = nc.tensor.matmul(out[:, hs], QI[:, d, at:at + P], ST[:, s, hs],
                                                            start=False, stop=(d == 1))
                        last.then_inc(bank_filled, 1)
                else:
                    for b, (nm, n) in enumerate((("dq", QR), ("dkv", KVR + RD))):
                        weights_arrived(pe, (nm,))
                        w = block_view((nm,))
                        for t in range(NT):
                            out = bank(("dqkv", b, t))
                            contract(out[:, 0:n], lambda c: hT[:, c, t * P:(t + 1) * P], lambda c: w[:, c, :], DC)\
                                .then_inc(bank_filled, 1)
                        used(("dqkv", b, NT - 1))
                    new_input()
                    for t in range(NT):
                        out = bank(("cqT", t))
                        for c in range(3):
                            last = nc.tensor.transpose(out[:, c * P:(c + 1) * P], CQ[:, t, c:QR:3], ident[:])
                        last.then_inc(bank_filled, 1)
                    for k in range(2):
                        out = bank(("ckvT", k))
                        for j in range(4):
                            kt, c = 2 * k + j // 2, j % 2
                            src = CACHE[:, c::2] if kt == 1 else CQ[:, 0 if kt == 0 else kt - 1, QR + c:QR + KVR:2]
                            last = nc.tensor.transpose(out[:, j * P:(j + 1) * P], src, ident[:])
                        last.then_inc(bank_filled, 1)
                    out = bank(("krT",))
                    for kt in range(KEYT):
                        last = nc.tensor.transpose(out[0:96, kt * P:(kt + 1) * P], KR[:, kt, :], ident[:])
                    last.then_inc(bank_filled, 1)
                    emptied_now(pe, ("krT",))
                    weights_arrived(pe, ("ukv",))
                    kv = block_view(("ukv",)).rearrange("p c (h n) -> p c h n", h=MH)
                    for kt in range(KEYT):
                        for k in range(2):
                            out = bank(("val", kt, k))
                            contract(out[:, :], lambda c: CKVT[:, c, kt * P:(kt + 1) * P],
                                     lambda c: kv[:, c, 8 * k:8 * k + 8, ND:], 2).then_inc(bank_filled, 1)
                    for kt in range(KEYT):
                        emptied_now(pe, ("val", kt, 1))
                    attention(1)
                project(layer)
                router(layer)
                assign(layer)
                pairs(layer)
                every_expert(layer)

        @block.scalar
        def _(act):
            step = [0]
            given = [0]

            def link(ins):
                step[0] += 1
                ins.then_inc(a_step, 1)
                act.wait_ge(a_step, step[0])

            def go():
                given[0] += 1
                act.wait_ge(to_act, given[0])

            def done(ins):
                ins.then_inc(from_act, 1)

            def emptied_by_me(ins):
                ins.then_inc(emptied["a"], 1)

            nc.scalar.preload_act_table_set("natural_log_exp_and_others")

            def norm():
                go()
                link(nc.scalar.activation(small[:, 4:7], small[:, 0:3], ACT.Ln, bias=small[:, 62:63]))
                done(nc.scalar.activation(small[:, 8:11], small[:, 4:7], ACT.Exp, scale=-0.5))

            def to_features(kind, layer):
                for t in range(NT):
                    b = filled(act, (kind, layer, t, 0))
                    emptied_by_me(nc.scalar.activation(hT[:, 0:4, t * P:(t + 1) * P],
                                                       b[:, :].rearrange("p (c n) -> p c n", c=4), ACT.Copy))

            def attention(layer):
                groups = attention_groups(layer)
                scale = 0.125 if layer == 0 else 96 ** -0.5

                def exps(n):
                    g, t = groups[n]
                    nk = len(key_tiles(t)) * P
                    prob = (P0 if layer == 0 else P1)[n % 2]
                    pr = prob.rearrange("p h k -> p (h k)")[:, 0:4 * nk].rearrange("p (h k) -> p h k", h=4)
                    go()
                    if n >= 2:
                        gp, tp = groups[n - 2]
                        act.wait_ge(bank_filled, number[("pT", layer, n - 2, len(key_tiles(tp)) - 1)] + 1)
                    nb = smallp[:, n % 3, 0:4]
                    rs = smallp[:, n % 3, 4:8]
                    if layer == 0:
                        nc.scalar.activation(smallp[:, n % 3, 12:16], smallp[:, n % 3, 8:12], ACT.Exp)
                    share = score_heads(layer, t)
                    for h in range(4):
                        i = [h in hs for hs in share].index(True)
                        j = share[i].index(h)
                        b = banks[number[("score", layer, n, i)] % BANKS]
                        src = b[:, j * nk:(j + 1) * nk]
                        ins = nc.scalar.activation(pr[:, h, :], src, ACT.Exp, bias=nb[:, h:h + 1], scale=scale,
                                                   accum_out=rs[:, h:h + 1])
                        if h == share[i][-1]:
                            emptied_by_me(ins)

                exps(0)
                for n, (g, t) in enumerate(groups):
                    if n + 1 < len(groups):
                        exps(n + 1)
                    pt = (PT0 if layer == 0 else PT1)
                    b = filled(act, ("pT", layer, n, 0))
                    if n >= len(pt):
                        act.wait_ge(bank_filled, number[("pv", layer, n - len(pt))] + 1)
                    emptied_by_me(nc.scalar.activation(pt[n % len(pt)][:, 0, :], b[:, :], ACT.Copy))

            def pairs(layer):
                B = PAIRS * layer

                def gate_exp(i, q):
                    act.wait_ge(gu_filled, B + i + 1)
                    at_least(act, act_made, B + i - 1)
                    nc.scalar.activation(GE[q], banks[2 + q][:, 0:FF], ACT.Exp, scale=-1.0).then_inc(gexp_ready, 1)

                def copy_y(i, q):
                    act.wait_ge(y_filled, B + i + 1)
                    at_least(act, y_out[q], 16 * HALF * layer + 8 * (i - q))
                    nc.scalar.activation(YS[q][:, 512:1024], banks[6][:, :], ACT.Copy).then_inc(y_copied["a"], 1)

                def copy_x(i, q):
                    act.wait_ge(xt_filled, B + i + 1)
                    at_least(act, gu_filled, B + i - 1)
                    nc.scalar.activation(XGT[q][:, 0:4, :], banks[0][:, :].rearrange("p (c n) -> p c n", c=4), ACT.Copy)\
                        .then_inc(xt_ready["a"], 1)

                def copy_act(i, q):
                    act.wait_ge(actt_filled, B + i + 1)
                    at_least(act, y_filled, B + i - 1)
                    nc.scalar.activation(ACTT[q], banks[4][:, 0:2 * P].rearrange("p (f n) -> p f n", f=2), ACT.Copy)\
                        .then_inc(actt_ready, 1)

                def step(i, q):
                    gate_exp(i, q)
                    copy_y(i - 1, 1 - q)
                    copy_x(i + 1, 1 - q)
                    copy_act(i, q)

                copy_x(0, 0)
                gate_exp(0, 0)
                copy_x(1, 1)
                copy_act(0, 0)
                over_pairs(act, step)
                gate_exp(PAIRS - 1, 1)
                copy_y(PAIRS - 2, 0)
                copy_act(PAIRS - 1, 1)
                copy_y(PAIRS - 1, 1)

            def every_expert(layer):
                F = fb[layer]
                act.wait_ge(combined, layer + 1)
                with act.If(overflow(act)):
                    with act.Fori(0, EXPERTS // 2) as i:
                        for q in range(2):
                            for f in range(2):
                                act.wait_ge(F["gu_done"], 2 * q + f + 1 + 4 * i)
                                act.wait_ge(F["act_ready"], 2 * q + f + 1 + 4 * i)
                                nc.scalar.activation(EE[:, f, :], banks[f][:, 0:TOK], ACT.Exp, scale=-1.0)\
                                    .then_inc(F["gexp_done"], 1)

            act.wait_ge(cond_in, 32)
            done(nc.scalar.activation(cond[:], cond2[:], ACT.Exp, scale=-1.0))
            for layer in range(2):
                norm()
                to_features("hT", layer)
                if layer == 0:
                    for b in range(2):
                        for t in range(NT):
                            bk = filled(act, ("qkv", b, t))
                            w = 512 if b == 0 else 256
                            emptied_by_me(nc.scalar.activation(QKVt[:, t, 512 * b:512 * b + w], bk[:, 0:w], ACT.Copy))
                    for b in range(3):
                        for h in range(GH):
                            bk = filled(act, ("qff", b, h))
                            dst = QH[:, h, :] if b == 0 else LF[:, b - 1, h * TOK:(h + 1) * TOK]
                            emptied_by_me(nc.scalar.activation(dst, bk[:, 0:TOK], ACT.Copy))
                    for b in range(2):
                        for t in range(NT):
                            bk = filled(act, ("vg", b, t))
                            emptied_by_me(nc.scalar.activation((VV, GG)[b][:, t, :], bk[:, :], ACT.Copy))
                    attention(0)
                    go()
                    nc.scalar.activation(BIG[:, 0:1536], QH.rearrange("p h t -> p (h t)"), ACT.Exp, scale=-1.0)
                    nc.scalar.activation(BIG[:, 1536:3072], GG.rearrange("p h t -> p (h t)"), ACT.Exp, scale=-1.0)
                    done(nc.scalar.activation(lbs[:, 0, :, :], lbs[:, 1, :, :], ACT.Exp))
                    go()
                    nc.scalar.activation(lbs[:, 3, :, :], lbs[:, 2, :, :], ACT.Ln, scale=float(2.0 ** 60))
                    done(nc.scalar.activation(lbs[:, 4, :, :], lbs[:, 1, :, :], ACT.Ln, scale=-1.0, bias=1.0))
                    go()
                    LFf = LF.rearrange("p d n -> p (d n)")
                    link(nc.scalar.activation(BIG, LFf, ACT.Abs))
                    link(nc.scalar.activation(BIG, BIG, ACT.Exp, scale=-1.0))
                    done(nc.scalar.activation(BIG, BIG, ACT.Ln, bias=1.0))
                    go()
                    link(nc.scalar.activation(BIG, BIG, ACT.Abs))
                    link(nc.scalar.activation(BIG, BIG, ACT.Exp, scale=-1.0))
                    done(nc.scalar.activation(BIG, BIG, ACT.Ln, bias=1.0))
                    go()
                    done(nc.scalar.activation(KK.rearrange("p d n -> p (d n)"), LFf, ACT.Exp))
                    for lv in range(len(LEVELS)):
                        for d in range(2):
                            go()
                            link(nc.scalar.activation(LE[d], LE[d], ACT.Abs))
                            done(nc.scalar.activation(LE[d], LE[d], ACT.Exp, scale=-1.0))
                    go()
                    nc.scalar.activation(KD4.rearrange("p u n -> p (u n)"), KD4.rearrange("p u n -> p (u n)"), ACT.Exp)
                    nc.scalar.activation(QI[:, 0, :], QI[:, 0, :], ACT.Exp)
                    nc.scalar.activation(QI[:, 1, :], QI[:, 1, :], ACT.Exp)
                    done(nc.scalar.activation(smallp[:, 0:2, 0:8], smallp[:, 0:2, 0:8], ACT.Exp))
                    for u in range(4):
                        bk = filled(act, ("kdT", u))
                        emptied_by_me(nc.scalar.activation(KDT[:, u, :], bk[:, :], ACT.Copy))
                    for t in range(NT):
                        bk = filled(act, ("o", t))
                        emptied_by_me(nc.scalar.activation(OB[:, t, :], bk[:, :], ACT.Copy))
                    go()
                    link(nc.scalar.activation(small[:, 32:44], small[:, 16:28], ACT.Ln, bias=small[:, 62:63]))
                    done(nc.scalar.activation(small[:, 48:60], small[:, 32:44], ACT.Exp, scale=-0.5))
                else:
                    for b in range(2):
                        for t in range(NT):
                            bk = filled(act, ("dqkv", b, t))
                            lo, w = (0, QR) if b == 0 else (QR, KVR + RD)
                            emptied_by_me(nc.scalar.activation(CQ[:, t, lo:lo + w], bk[:, 0:w], ACT.Copy))
                    go()
                    link(nc.scalar.activation(small[:, 32:38], small[:, 16:22], ACT.Ln, bias=small[:, 62:63]))
                    done(nc.scalar.activation(small[:, 48:54], small[:, 32:38], ACT.Exp, scale=-0.5))
                    for kt in range(KEYT):
                        for k in range(2):
                            bk = filled(act, ("val", kt, k))
                            emptied_by_me(nc.scalar.activation(VAL[:, kt, k * 512:(k + 1) * 512], bk[:, :], ACT.Copy))
                    attention(1)
                to_features("mixT", layer)
                norm()
                to_features("h2T", layer)
                go()
                done(nc.scalar.activation(RT[:, 128:140], RT[:, 128:140], ACT.Exp))
                go()
                done(nc.scalar.activation(RT[:, 256:280], RT[:, 256:280], ACT.Exp))
                pairs(layer)
                every_expert(layer)
            norm()

        @block.vector
        def _(dve):
            v = nc.vector
            step = [0]
            waited = [0]

            def link(ins):
                step[0] += 1
                ins.then_inc(v_step, 1)
                dve.wait_ge(v_step, step[0])

            def give(ins):
                ins.then_inc(to_act, 1)

            def get():
                waited[0] += 1
                dve.wait_ge(from_act, waited[0])

            fed = [0]

            def feed(ins):
                fed[0] += 1
                ins.then_inc(to_pe, 1)

            def emptied_by_me(ins):
                ins.then_inc(emptied["v"], 1)

            def rstd(src, n):
                for t in range(NT):
                    link(v.tensor_tensor_reduce(out=MIX[:, t, 0:n], in0=src[:, t, :], in1=src[:, t, :], scale=1.0 / n,
                                                scalar=0.0, op0=ALU.mult, op1=ALU.add, accum_out=small[:, t:t + 1]))
                dve.sem_inc(to_act, 1)
                get()

            def adaln(kind, layer, consts, nth):
                dve.wait_ge(mod_in, 32 * nth)
                rstd(X, D)
                dve.wait_ge(consts_in, consts)
                for g in range(2):
                    link(v.scalar_tensor_tensor(out=MOD[:, g, 1, :], in0=MOD[:, g, 1, :], scalar=1.0, in1=normw[:],
                                                op0=ALU.add, op1=ALU.mult))
                for t in range(NT):
                    g = 0 if t == 0 else 1
                    link(v.scalar_tensor_tensor(out=MIX[:, t, :], in0=X[:, t, :], scalar=small[:, 8 + t:9 + t],
                                                in1=MOD[:, g, 1, :], op0=ALU.mult, op1=ALU.mult))
                    feed(v.tensor_tensor(MIX[:, t, :], MIX[:, t, :], MOD[:, g, 0, :], ALU.add))
                dve.wait_ge(to_pe, fed[0])
                if kind == "h2T":
                    dve.sem_inc(h2_made, 1)
                dve.sem_inc(pool_free, 1)
                to_features(kind, layer)

            def to_features(kind, layer):
                for t in range(NT):
                    b = filled(dve, (kind, layer, t, 1))
                    emptied_by_me(v.tensor_copy(hT[:, 4:8, t * P:(t + 1) * P], b[:, :].rearrange("p (c n) -> p c n", c=4)))

            def attention(layer):
                groups = attention_groups(layer)
                scale = 0.125 if layer == 0 else 96 ** -0.5

                def maxima(n):
                    g, t = groups[n]
                    nk = len(key_tiles(t)) * P
                    if layer == 1 and t == 0:
                        queries_keys(g)
                    sp_ = smallp[:, n % 3]
                    share = score_heads(layer, t)
                    for i, hs in enumerate(share):
                        b = filled(dve, ("score", layer, n, i))
                        link(v.tensor_reduce(out=sp_[:, 16 + i:20:len(share)],
                                             in_=b[:, 0:len(hs) * nk].rearrange("p (h k) -> p h k", k=nk), axis=AX, op=ALU.max))
                    if layer == 0:
                        sk = sink[:, 4 * g:4 * g + 4]
                        link(v.scalar_tensor_tensor(out=sp_[:, 16:20], in0=sp_[:, 16:20], scalar=scale, in1=sk,
                                                    op0=ALU.mult, op1=ALU.max))
                        link(v.tensor_tensor(sp_[:, 8:12], sk, sp_[:, 16:20], ALU.subtract))
                        give(v.tensor_scalar(sp_[:, 0:4], sp_[:, 16:20], -1.0, None, ALU.mult))
                    else:
                        give(v.tensor_scalar(sp_[:, 0:4], sp_[:, 16:20], -scale, None, ALU.mult))

                maxima(0)
                for n, (g, t) in enumerate(groups):
                    if n + 1 < len(groups):
                        maxima(n + 1)
                    sp_ = smallp[:, n % 3]
                    pt = (PT0 if layer == 0 else PT1)
                    for i in range(1, len(key_tiles(t))):
                        b = filled(dve, ("pT", layer, n, i))
                        if n >= len(pt):
                            dve.wait_ge(bank_filled, number[("pv", layer, n - len(pt))] + 1)
                        emptied_by_me(v.tensor_copy(pt[n % len(pt)][:, i, :], b[:, :]))
                    emptied_now(dve, ("score", layer, n, len(score_heads(layer, t)) - 1))
                    if layer == 0:
                        link(v.tensor_tensor(sp_[:, 4:8], sp_[:, 4:8], sp_[:, 12:16], ALU.add))
                    link(v.reciprocal(sp_[:, 20:24], sp_[:, 4:8]))
                    b = filled(dve, ("pv", layer, n))
                    emptied_by_me(v.tensor_tensor(MIX[:, t, 256 * g:256 * g + 256].rearrange("p (h e) -> p h e", h=4),
                                                  b[:, 0:256].rearrange("p (h e) -> p h e", h=4),
                                                  sp_[:, 20:24].unsqueeze(2).to_broadcast([P, 4, 64]), ALU.mult))

            def queries_keys(g):
                uq = block_view(("uq", g // 2)).rearrange("p c (h n) -> p c h n", h=8)
                hs = slice(4 * (g % 2), 4 * (g % 2) + 4)
                if g % 2 == 0:
                    weights_arrived(dve, ("uq", g // 2))
                wq = WQB[:].rearrange("p c (h n) -> p c h n", h=4)
                if g == 0:
                    dve.wait_ge(stored, 16 * 6)
                if g:
                    dve.wait_ge(bank_filled, number[("qT1", g - 1, 3)] + 1)
                for c in range(3):
                    v.tensor_copy(wq[:, c, :, 0:96], uq[:, c, hs, :])
                    for half in range(4):
                        to = 96 + 8 * half
                        fr = 64 + 8 * (half ^ 1)
                        last = v.tensor_copy(wq[:, c, :, to:to + 8], uq[:, c, hs, fr:fr + 8])
                feed(last)
                K, Q = K1[g % 2], Q1[g % 2]
                if g >= 2:
                    dve.wait_ge(bank_filled, number[("score", 1, 3 * (g - 2) + 2, 3)] + 1)
                for i in range(2):
                    b = filled(dve, ("kT", g, i))
                    v.tensor_copy(K[0:64, 2 * i, :], b[0:64, :])
                    emptied_by_me(v.tensor_copy(K[0:64, 2 * i + 1, :], b[64:128, :]))
                for i in range(4):
                    b = filled(dve, ("qT1", g, i))
                    v.tensor_copy(Q[0:64, i, :], b[0:64, 0:TOK])
                    v.tensor_copy(Q[64:96, i, 0:P], b[64:96, 0:P])
                    v.tensor_tensor(Q[64:96, i, P:TOK], b[64:96, P:TOK], ropeT[64:96, :], ALU.mult)
                    link(v.tensor_tensor(SQ[64:96, 0:2 * P], b[96:128, P:TOK], ropeT[96:128, :], ALU.mult))
                    emptied_by_me(v.tensor_tensor(Q[64:96, i, P:TOK], Q[64:96, i, P:TOK], SQ[64:96, 0:2 * P], ALU.add))
                    emptied_now(dve, ("qT1", g, i))
                feed(v.tensor_copy(K[64:96, :, :], KRT[64:96, :].unsqueeze(1).to_broadcast([32, 4, KEYT * P])))

            def residual(layer):
                for n in range(2):
                    for t in range(NT):
                        g = 0 if t == 0 else 1
                        cs = slice(n * 512, (n + 1) * 512)
                        b = filled(dve, ("proj", layer, n, t))
                        emptied_by_me(v.tensor_tensor(MIX[:, t, cs], b[:, :], MOD[:, g, 2, cs], ALU.mult))
                        emptied_now(dve, ("proj", layer, n, t))
                        link(v.tensor_tensor(X[:, t, cs], X[:, t, cs], MIX[:, t, cs], ALU.add))

            def first_hot(out, val, mx, tmp, n):
                io = iota[:, 0:n].unsqueeze(1).to_broadcast([P, NT, n])
                io64 = iota[:, 8:8 + n].unsqueeze(1).to_broadcast([P, NT, n])
                link(v.tensor_tensor(tmp, val, mx.to_broadcast([P, NT, n]), ALU.is_ge))
                link(v.scalar_tensor_tensor(out=tmp, in0=tmp, scalar=-64.0, in1=io64, op0=ALU.mult, op1=ALU.add))
                link(v.tensor_reduce(out=RT[:, 400:403], in_=tmp, axis=AX, op=ALU.min))
                link(v.tensor_tensor(out, RT[:, 400:403].unsqueeze(2).to_broadcast([P, NT, n]), io, ALU.is_equal))

            def route(layer):
                def cols(at, n):
                    return RT[:, at:at + NT * n].rearrange("p (t n) -> p t n", t=NT)

                L = cols(0, 36)
                b = filled(dve, ("router", layer))
                dve.wait_ge(router_in, 16 * 7 * (layer + 1))
                emptied_by_me(v.tensor_tensor(L, b[:, 0:108].rearrange("p (t n) -> p t n", t=NT),
                                              BR[:].unsqueeze(1).to_broadcast([P, NT, 36]), ALU.add))
                emptied_now(dve, ("router", layer))
                GL = L[:, :, 0:4]
                gm, gsum = cols(112, 1), cols(116, 1)
                eg = cols(128, 4)
                link(v.tensor_reduce(out=gm, in_=GL, axis=AX, op=ALU.max))
                give(v.tensor_tensor(eg, GL, gm.to_broadcast([P, NT, 4]), ALU.subtract))
                goh, tmp = cols(144, 4), cols(160, 8)
                first_hot(goh, GL, gm, tmp[:, :, 0:4], 4)
                prod = RT[:, 300:396].rearrange("p (t g e) -> p t g e", t=NT, g=4)
                for t in range(NT):
                    link(v.tensor_tensor(prod[:, t], L[:, t, 4:36].rearrange("p (g e) -> p g e", g=4),
                                         goh[:, t].unsqueeze(2).to_broadcast([P, 4, 8]), ALU.mult))
                esel = cols(224, 8)
                link(v.tensor_reduce(out=esel, in_=prod.rearrange("p t g e -> p t e g"), axis=AX, op=ALU.add))
                m1 = cols(120, 1)
                link(v.tensor_reduce(out=m1, in_=esel, axis=AX, op=ALU.max))
                e8 = cols(256, 8)
                get()
                give(v.tensor_tensor(e8, esel, m1.to_broadcast([P, NT, 8]), ALU.subtract))
                link(v.tensor_reduce(out=gsum, in_=eg, axis=AX, op=ALU.add))
                link(v.reciprocal(gsum, gsum))
                o1, o2 = cols(184, 8), cols(404 - 0, 8)
                first_hot(o1, esel, m1, tmp, 8)
                link(v.scalar_tensor_tensor(out=esel, in0=o1, scalar=-1e30, in1=esel, op0=ALU.mult, op1=ALU.add))
                link(v.tensor_reduce(out=m1, in_=esel, axis=AX, op=ALU.max))
                first_hot(o2, esel, m1, tmp, 8)
                get()
                o12 = tmp
                link(v.tensor_tensor(o12, o1, o2, ALU.add))
                link(v.tensor_tensor(e8, e8, o12, ALU.mult))
                den = cols(124, 1)
                link(v.tensor_reduce(out=den, in_=e8, axis=AX, op=ALU.add))
                link(v.reciprocal(den, den))
                link(v.tensor_tensor(den, den, gsum, ALU.mult))
                link(v.tensor_tensor(e8, e8, den.to_broadcast([P, NT, 8]), ALU.mult))
                for t in range(NT):
                    last = v.tensor_tensor(COMB[:, t, :].rearrange("p (g e) -> p g e", g=4),
                                           goh[:, t].unsqueeze(2).to_broadcast([P, 4, 8]),
                                           e8[:, t].unsqueeze(1).to_broadcast([P, 4, 8]), ALU.mult)
                    for j, o in enumerate((o1, o2)):
                        last = v.tensor_tensor(S12[:, j * NT + t, :].rearrange("p (g e) -> p g e", g=4),
                                               goh[:, t].unsqueeze(2).to_broadcast([P, 4, 8]),
                                               o[:, t].unsqueeze(1).to_broadcast([P, 4, 8]), ALU.mult)
                link(last)
                feed(v.tensor_tensor(SEL, S12[:, 0:NT, :], S12[:, NT:, :], ALU.add))
                b = filled(dve, ("pos", layer))
                v.tensor_copy(POS, b[:, 0:96].rearrange("p (t n) -> p t n", t=NT))
                link(v.tensor_reduce(out=FULLF, in_=b[:, 96:128], axis=AX, op=ALU.max))
                emptied_by_me(v.tensor_copy(FULL, FULLF))
                emptied_now(dve, ("pos", layer))
                link(v.tensor_scalar(OVER, POS, float(CAP), None, ALU.is_ge))
                link(v.tensor_scalar(SEL2, OVER, -1.0, 1.0, ALU.mult, ALU.add))
                link(v.tensor_tensor(OVER, OVER, COMB, ALU.mult))
                link(v.tensor_tensor(POS, POS, ktab[:, P + PAIRS:P + PAIRS + EXPERTS].unsqueeze(1).to_broadcast([P, NT, EXPERTS]), ALU.add))
                higher = ktab[:, P + PAIRS + EXPERTS:P + PAIRS + 2 * EXPERTS].unsqueeze(1).to_broadcast([P, NT, EXPERTS])
                for row, val in enumerate((POS, higher, SEL2, COMB)):
                    for j in range(2):
                        last = v.tensor_tensor(PROD[:, j * NT:(j + 1) * NT, :], S12[:, j * NT:(j + 1) * NT, :], val, ALU.mult)
                    link(last)
                    link(v.tensor_reduce(out=LOHI[:, row, :], in_=PROD, axis=AX, op=ALU.add))
                ok = LOHI[:, 2, :]
                v.tensor_tensor(LOHI[:, 3, :], LOHI[:, 3, :], ok, ALU.mult)
                for j in range(2):
                    v.tensor_tensor(LOHI[:, 5, j * NT:(j + 1) * NT], ktab[:, P + PAIRS + 2 * EXPERTS:], ok[:, 0:NT] if j == 0 else ok[:, NT:], ALU.mult)
                link(v.scalar_tensor_tensor(out=LOHI[:, 4, :], in0=LOHI[:, 1, :], scalar=float(P), in1=LOHI[:, 0, :], op0=ALU.mult, op1=ALU.add))
                link(v.tensor_tensor(LOHI[:, 4, :], LOHI[:, 4, :], ok, ALU.mult))
                v.tensor_copy(ROWI, LOHI[:, 4, :])
                for j in range(2 * NT):
                    v.tensor_scalar(OHLO[:, j, :], ktab[:, 0:P], LOHI[:, 0, j:j + 1], None, ALU.is_equal)
                    last = v.tensor_scalar(OHHI[:, j, :], ktab[:, P:P + PAIRS], LOHI[:, 1, j:j + 1], LOHI[:, 5, j:j + 1],
                                           ALU.is_equal, ALU.mult)
                feed(last)
                b = filled(dve, ("slot", layer))
                v.tensor_copy(IDX, b[:, 0:PAIRS]).then_inc(idx_ready, 1)
                dve.wait_ge(idx_ready, layer + 1)
                dve.sem_inc(emptied["v"], 1)

            def pairs(layer):
                B = PAIRS * layer

                def activate(i, q):
                    s0 = 3 * B
                    dve.wait_ge(gexp_ready, B + i + 1)
                    v.tensor_scalar(GE[q], GE[q], 1.0, None, ALU.add).then_inc(p_step, 1)
                    dve.wait_ge(p_step, s0 + 3 * i + 1)
                    v.reciprocal(GE[q], GE[q]).then_inc(p_step, 1)
                    dve.wait_ge(p_step, s0 + 3 * i + 2)
                    v.tensor_tensor(GE[q], banks[2 + q][:, 0:FF], GE[q], ALU.mult).then_inc(p_step, 1)
                    dve.wait_ge(p_step, s0 + 3 * i + 3)
                    at_least(dve, actt_filled, B + i - 1)
                    v.tensor_tensor(ACTV[q], banks[2 + q][:, FF:2 * FF], GE[q], ALU.mult).then_inc(act_made, 1)

                def copy_y(i, q):
                    dve.wait_ge(y_filled, B + i + 1)
                    at_least(dve, y_out[q], 16 * HALF * layer + 8 * (i - q))
                    v.tensor_copy(YS[q][:, 0:512], banks[5][:, :]).then_inc(y_copied["v"], 1)

                def copy_x(i, q):
                    dve.wait_ge(xt_filled, B + i + 1)
                    at_least(dve, gu_filled, B + i - 1)
                    v.tensor_copy(XGT[q][:, 4:8, :], banks[1][:, :].rearrange("p (c n) -> p c n", c=4)).then_inc(xt_ready["v"], 1)

                def step(i, q):
                    activate(i, q)
                    copy_y(i - 1, 1 - q)
                    copy_x(i + 1, 1 - q)

                copy_x(0, 0)
                activate(0, 0)
                copy_x(1, 1)
                over_pairs(dve, step)
                activate(PAIRS - 1, 1)
                copy_y(PAIRS - 2, 0)
                copy_y(PAIRS - 1, 1)
                for t in range(NT):
                    dve.wait_ge(y_back[t], 32 * (layer + 1))
                    y1, y2 = YG[:, t, :], YG[:, NT + t, :]
                    link(v.tensor_scalar(y1, y1, LOHI[:, 3, t:t + 1], None, ALU.mult))
                    link(v.scalar_tensor_tensor(out=y1, in0=y2, scalar=LOHI[:, 3, NT + t:NT + t + 1], in1=y1, op0=ALU.mult, op1=ALU.add))
                    link(v.tensor_tensor(y1, y1, MOD[:, 0 if t == 0 else 1, 2, :], ALU.mult))
                    link(v.tensor_tensor(X[:, t, :], X[:, t, :], y1, ALU.add))
                dve.sem_inc(combined, 1)

            def every_expert(layer):
                F = fb[layer]
                chained = [0]

                def chain(ins):
                    chained[0] += 1
                    ins.then_inc(F["chain"], 1)
                    dve.wait_ge(F["chain"], chained[0])

                with dve.If(overflow(dve)):
                    chain(v.memset(YACC, 0.0))
                    dve.sem_inc(F["y_emptied"], 4)
                    dve.sem_inc(F["act_ready"], 2)
                    with dve.Fori(0, EXPERTS // 2) as i:
                        for q in range(2):
                            for f in range(2):
                                n = 2 * q + f
                                dve.wait_ge(F["gexp_done"], n + 1 + 4 * i)
                                v.tensor_scalar(EE[:, f, :], EE[:, f, :], 1.0, None, ALU.add).then_inc(F["step"], 1)
                                dve.wait_ge(F["step"], 3 * n + 1 + 12 * i)
                                v.reciprocal(EE[:, f, :], EE[:, f, :]).then_inc(F["step"], 1)
                                dve.wait_ge(F["step"], 3 * n + 2 + 12 * i)
                                v.tensor_tensor(EE[:, f, :], banks[f][:, 0:TOK], EE[:, f, :], ALU.mult).then_inc(F["step"], 1)
                                dve.wait_ge(F["step"], 3 * n + 3 + 12 * i)
                                v.tensor_tensor(AT[:, q, f, :], banks[2 + f][:, 0:TOK], EE[:, f, :], ALU.mult)\
                                    .then_inc(F["act_ready"], 1)
                            for j in range(6):
                                h, t = divmod(j, NT)
                                k = 6 * q + j
                                dve.wait_ge(F["y_done"], k + 1 + 12 * i)
                                ys = YACC[:, t, h * 512:(h + 1) * 512]
                                dve.wait_ge(F["y_emptied"], 4 + k + 12 * i)
                                v.scalar_tensor_tensor(out=ys, in0=banks[4 + k % 4][:, :], scalar=OVER[:, t, bass.ds(2 * i + q, 1)],
                                                       in1=ys, op0=ALU.mult, op1=ALU.add).then_inc(F["y_emptied"], 1)
                    dve.wait_ge(F["y_emptied"], 6 * EXPERTS + 4)
                    for t in range(NT):
                        chain(v.tensor_tensor(YACC[:, t, :], YACC[:, t, :], MOD[:, 0 if t == 0 else 1, 2, :], ALU.mult))
                        chain(v.tensor_tensor(X[:, t, :], X[:, t, :], YACC[:, t, :], ALU.add))
                dve.sem_inc(experts_over, 1)

            def modulation(layer):
                for b in range(12):
                    bk = filled(dve, ("mod", layer, b))
                    dve.wait_ge(modbias_in[b % 2], 32 * (6 * layer + b // 2 + 1))
                    if b >= 2:
                        dve.wait_ge(modrow_out[b % 2], 16 * (6 * layer + b // 2))
                    v.tensor_tensor(modrow[0:2, b % 2, :], bk[0:2, :], modbias[0:2, b % 2, :], ALU.add).then_inc(modrow_ready, 1)
                    dve.wait_ge(modrow_ready, 12 * layer + b + 1)
                    dve.sem_inc(emptied["v"], 1)

            v.memset(small[:, 62:63], EPS)
            for j in range(8):
                v.memset(iota[:, j:j + 1], float(j))
                v.memset(iota[:, 8 + j:9 + j], float(64 + j))
            get()
            link(v.tensor_scalar(cond[:], cond[:], 1.0, None, ALU.add))
            link(v.reciprocal(cond[:], cond[:]))
            v.tensor_tensor(cond[:], cond[:], cond2[:], ALU.mult).then_inc(cond_ready, 1)
            dve.wait_ge(tokens_in, 32)
            for layer in range(2):
                modulation(layer)
                adaln("hT", layer, CONSTS + 32 * layer, 2 * layer + 1)
                if layer == 0:
                    emptied_now(dve, ("qkv", 1, 2))
                    dve.wait_ge(l1params_in, 48)
                    for t in (1, 2):
                        x = QKVt[:, t, 0:640].rearrange("p (h r) -> p h r", r=HD)
                        link(v.tensor_tensor(ROT[:, 0, :].rearrange("p (h r) -> p h r", r=HD), x,
                                             rope_cs[:, t - 1, 0].unsqueeze(1).to_broadcast([P, 10, HD]), ALU.mult))
                        for half in range(4):
                            o = half ^ 1
                            r = ROT[:, 1, :].rearrange("p (h r) -> p h r", r=HD)
                            link(v.tensor_tensor(r[:, :, 16 * half:16 * half + 16], x[:, :, 16 * o:16 * o + 16],
                                                 rope_cs[:, t - 1, 1, 16 * half:16 * half + 16].unsqueeze(1).to_broadcast([P, 10, 16]),
                                                 ALU.mult))
                        link(v.tensor_tensor(QKVt[:, t, 0:640], ROT[:, 0, :], ROT[:, 1, :], ALU.add))
                    for kt in (0, 2, 3):
                        t = 0 if kt == 0 else kt - 1
                        for dup in range(2):
                            last = v.tensor_copy(KD[:, kt, :, dup * HD:dup * HD + HD],
                                                 QKVt[:, t, 512:640].rearrange("p (g d) -> p g d", g=2))
                    feed(last)
                    for t in range(NT):
                        b = filled(dve, ("qT", t))
                        emptied_by_me(v.tensor_copy(QT[:, :, t * P:(t + 1) * P], b[:, :].rearrange("p (j n) -> p j n", j=4)))
                    for k in range(2):
                        b = filled(dve, ("kT0", k))
                        for j in range(2):
                            ins = v.tensor_copy(KT[:, :, (2 * k + j) * P:(2 * k + j + 1) * P],
                                                b[:, 2 * j * P:(2 * j + 2) * P].rearrange("p (g n) -> p g n", g=2))
                        emptied_by_me(ins)
                    attention(0)
                    emptied_now(dve, ("pv", 0, 5))
                    emptied_now(dve, ("vg", 1, 2))
                    dve.wait_ge(stored, 32)
                    give(v.tensor_tensor(lbs[:, 1, :, :], lbc[:], lbc[:], ALU.subtract))
                    get()
                    link(v.reciprocal(lbs[:, 5, :, :], lbs[:, 0, :, :]))
                    link(v.tensor_tensor(lbs[:, 0, :, :], lbs[:, 0, :, :], lbs[:, 5, :, :], ALU.mult))
                    link(v.tensor_tensor(lbs[:, 1, :, :], lbs[:, 0, :, :], lbs[:, 0, :, :], ALU.subtract))
                    link(v.tensor_scalar(lbs[:, 1, :, :], lbs[:, 1, :, :], 0.0, 1.0 - 1e-6, ALU.max, ALU.min))
                    give(v.tensor_scalar(lbs[:, 2, :, :], lbs[:, 1, :, :], 1e-30, None, ALU.max))
                    QHf, GGf = QH.rearrange("p h t -> p (h t)"), GG.rearrange("p h t -> p (h t)")
                    link(v.tensor_scalar(BIG, BIG, 1.0, None, ALU.add))
                    link(v.reciprocal(BIG, BIG))
                    v.scalar_tensor_tensor(out=QHf, in0=QHf, scalar=HGRN_SCALE, in1=BIG[:, 0:1536], op0=ALU.mult, op1=ALU.mult)
                    link(v.tensor_tensor(GGf, GGf, BIG[:, 1536:3072], ALU.mult))
                    get()
                    link(v.tensor_scalar(lbs[:, 3, :, :], lbs[:, 3, :, :], -60 * LN2, None, ALU.add))
                    dve.sem_inc(to_act, 1)
                    get()
                    LFf = LF.rearrange("p d n -> p (d n)")
                    LF8 = LFf.rearrange("p (b n) -> p b n", b=8)
                    BIG8 = BIG.rearrange("p (b n) -> p b n", b=8)
                    A8 = lbs[:, 3, :, :].rearrange("p d h -> p (d h)").unsqueeze(2).to_broadcast([P, 8, TOK])
                    C8 = lbs[:, 4, :, :].rearrange("p d h -> p (d h)").unsqueeze(2).to_broadcast([P, 8, TOK])
                    link(v.scalar_tensor_tensor(out=LFf, in0=LFf, scalar=0.0, in1=BIG, op0=ALU.min, op1=ALU.subtract))
                    link(v.tensor_tensor(LF8, LF8, C8, ALU.add))
                    give(v.tensor_tensor(BIG8, LF8, A8, ALU.subtract))
                    link(v.tensor_tensor(LF8, LF8, A8, ALU.max))
                    get()
                    give(v.tensor_tensor(LFf, LFf, BIG, ALU.add))
                    get()
                    link(v.tensor_scalar(KK.rearrange("p d n -> p (d n)"), KK.rearrange("p d n -> p (d n)"), -1.0, 1.0, ALU.mult, ALU.add))
                    v.memset(BIG[:, 0:1536], 1.0).then_inc(v_step, 1)
                    step[0] += 1
                    dve.wait_ge(v_step, step[0])
                    link(v.memset(BIG[:, 0:1536].rearrange("p (n t) -> p n t", t=P)[:, :, 0:1], 0.0))
                    for d in range(2):
                        link(v.tensor_tensor_scan(out=BIG2[:, d * 1536:(d + 1) * 1536], data0=BIG[:, 0:1536],
                                                  data1=LF[:, d, :], initial=0.0, op0=ALU.mult, op1=ALU.add))
                    link(v.tensor_copy(LF[:, 0, :], BIG2[:, 0:1536]))
                    link(v.tensor_tensor(LF[:, 1, :], LF[:, 1, :], BIG2[:, 1536:3072], ALU.subtract))
                    b2 = BIG2[:, 1536:3072].rearrange("p (n t) -> p n t", t=P)
                    l2 = LF[:, 1, :].rearrange("p (n t) -> p n t", t=P)
                    link(v.tensor_tensor(l2, l2, b2[:, :, P - 1:P].to_broadcast([P, GH * NT, P]), ALU.add))
                    for lv, half in enumerate(LEVELS):
                        nb = GH * TOK // (2 * half)
                        for d in range(2):
                            b3 = LF[:, d, :].rearrange("p (n w) -> p n w", w=2 * half)
                            ref = half - 1 if d == 0 else half
                            if lv:
                                dve.wait_ge(bank_filled, number[("lvl", lv - 1, d, NT - 1)] + 1)
                            give(v.tensor_tensor(LE[d].rearrange("p (n w) -> p n w", w=2 * half), b3,
                                                 b3[:, :, ref:ref + 1].to_broadcast([P, nb, 2 * half]), ALU.subtract))
                        for d in range(2):
                            get()
                            link(v.tensor_tensor(LK[d], LE[d], KK[:, d, :], ALU.mult))
                            feed(v.tensor_tensor(LE[d], LE[d], QHf, ALU.mult))
                            for t in range(NT):
                                b = filled(dve, ("lvl", lv, d, t))
                                emptied_by_me(v.copy_predicated(ATT[:, t], MASK[:, 2 * lv + d].unsqueeze(1).to_broadcast([P, GH, P]),
                                                                b[:, :].rearrange("p (h n) -> p h n", h=GH)))
                    feed(v.tensor_tensor(LK[0], KK[:, 0, :], KK[:, 1, :], ALU.add))
                    dve.wait_ge(to_pe, fed[0])
                    for t in range(NT):
                        b = filled(dve, ("diag", t))
                        emptied_by_me(v.copy_predicated(ATT[:, t], MASK[:, 14].unsqueeze(1).to_broadcast([P, GH, P]),
                                                        b[:, :].rearrange("p (h n) -> p h n", h=GH)))
                    UNITS = ((0, 0), (1, 0), (0, 1), (1, 2))
                    for u, (d, t) in enumerate(UNITS):
                        b3 = LF[:, d, :].rearrange("p (h n) -> p h n", h=GH)[:, :, t * P:(t + 1) * P]
                        end = b3[:, :, P - 1:P] if d == 0 else b3[:, :, 0:1]
                        link(v.tensor_tensor(KD4[:, u, :].rearrange("p (h n) -> p h n", h=GH),
                                             end.to_broadcast([P, GH, P]), b3, ALU.subtract))
                        if u >= 2:
                            link(v.tensor_copy(smallp[:, u - 2, 0:4].unsqueeze(2), end))
                            link(v.tensor_copy(smallp[:, u - 2, 4:8].unsqueeze(2), end))
                    for d in range(2):
                        b3 = LF[:, d, :].rearrange("p (h n) -> p h n", h=GH)[:, :, P:TOK]
                        ins = v.tensor_copy(QI[:, d, :].rearrange("p (h n) -> p h n", h=GH), b3)
                    give(ins)
                    get()
                    for u, (d, t) in enumerate(UNITS):
                        k3 = KK[:, d, :].rearrange("p (h n) -> p h n", h=GH)[:, :, t * P:(t + 1) * P]
                        kd = KD4[:, u, :].rearrange("p (h n) -> p h n", h=GH)
                        ins = v.tensor_tensor(kd, kd, k3, ALU.mult)
                    for d in range(2):
                        qi = QI[:, d, :].rearrange("p (h n) -> p h n", h=GH)
                        ins = v.tensor_tensor(qi, qi, QH[:, :, P:TOK], ALU.mult)
                    ins.then_inc(out_ready, 1)
                    dve.wait_ge(out_ready, 1)
                    fed[0] += 1
                    dve.sem_inc(to_pe, 1)
                    for u in range(2):
                        b = filled(dve, ("state", u))
                        v.tensor_copy(ST[:, 2 + u, :], b[:, :]).then_inc(out_ready, 1)
                        dve.wait_ge(out_ready, 2 + u)
                        dve.sem_inc(emptied["v"], 1)
                    dve.wait_ge(l1params_in, 80)
                    for u in (2, 3):
                        b = filled(dve, ("state", u))
                        for h in range(GH):
                            hs = slice(h * P, (h + 1) * P)
                            ins = v.scalar_tensor_tensor(out=ST[:, 2 + u, hs], in0=ST[:, u - 2, hs], scalar=smallp[:, u - 2, h:h + 1],
                                                         in1=b[:, hs], op0=ALU.mult, op1=ALU.add)
                        emptied_by_me(ins)
                    emptied_now(dve, ("o", 2))
                    ob = OB.rearrange("p t n -> p (t n)")
                    link(v.tensor_tensor(OB2.rearrange("p t n -> p (t n)"), ob, ob, ALU.mult))
                    link(v.tensor_reduce(out=small[:, 16:28], in_=OB2.rearrange("p t (h n) -> p (t h) n", h=GH), axis=AX, op=ALU.add))
                    give(v.tensor_scalar(small[:, 16:28], small[:, 16:28], 1.0 / P, None, ALU.mult))
                    get()
                    o3 = OB.rearrange("p t (h n) -> p (t h) n", h=GH)
                    link(v.tensor_tensor(o3, o3, small[:, 48:60].unsqueeze(2).to_broadcast([P, 12, P]), ALU.mult))
                    link(v.tensor_tensor(o3, o3, gnw[:].unsqueeze(1).to_broadcast([P, 12, P]), ALU.mult))
                    for t in range(NT):
                        feed(v.tensor_tensor(MIX[:, t, 512:1024], OB[:, t, :], GG[:, t, :], ALU.mult))
                else:
                    emptied_now(dve, ("dqkv", 1, 2))
                    for t in range(NT):
                        for j, (lo, n) in enumerate(((0, QR), (QR, KVR))):
                            link(v.tensor_tensor_reduce(out=SQ[:, 0:n], in0=CQ[:, t, lo:lo + n], in1=CQ[:, t, lo:lo + n],
                                                        scale=1.0 / n, scalar=0.0, op0=ALU.mult, op1=ALU.add,
                                                        accum_out=small[:, 16 + 2 * t + j:17 + 2 * t + j]))
                    dve.sem_inc(to_act, 1)
                    v.memset(KR, 0.0).then_inc(out_ready, 1)
                    dve.wait_ge(out_ready, 4)
                    get()
                    dve.wait_ge(l1params_in, 16 * 9)
                    for t in range(NT):
                        for j, (lo, n) in enumerate(((0, QR), (QR, KVR))):
                            r = small[:, 48 + 2 * t + j:49 + 2 * t + j]
                            ins = v.scalar_tensor_tensor(out=CQ[:, t, lo:lo + n], in0=CQ[:, t, lo:lo + n], scalar=r,
                                                         in1=qnw[:, lo:lo + n], op0=ALU.mult, op1=ALU.mult)
                    ins.then_inc(out_ready, 1)
                    for t in (1, 2):
                        x = CQ[:, t, QR + KVR:]
                        link(v.tensor_tensor(KR[:, t + 1, 64:96], x, rope32[:, t - 1, 0], ALU.mult))
                        for half in range(4):
                            o = half ^ 1
                            link(v.tensor_tensor(SQ[:, 8 * half:8 * half + 8], x[:, 8 * o:8 * o + 8],
                                                 rope32[:, t - 1, 1, 8 * half:8 * half + 8], ALU.mult))
                        link(v.tensor_tensor(KR[:, t + 1, 64:96], KR[:, t + 1, 64:96], SQ[:, 0:32], ALU.add))
                    link(v.tensor_copy(KR[:, 0, 64:96], CQ[:, 0, QR + KVR:]))
                    fed[0] += 1
                    dve.sem_inc(to_pe, 1)
                    for t in range(NT):
                        b = filled(dve, ("cqT", t))
                        emptied_by_me(v.tensor_copy(CQT[:, :, t * P:(t + 1) * P], b[:, 0:TOK].rearrange("p (c n) -> p c n", c=3)))
                    for k in range(2):
                        b = filled(dve, ("ckvT", k))
                        for j in range(2):
                            ins = v.tensor_copy(CKVT[:, :, (2 * k + j) * P:(2 * k + j + 1) * P],
                                                b[:, 2 * j * P:(2 * j + 2) * P].rearrange("p (c n) -> p c n", c=2))
                        emptied_by_me(ins)
                    b = filled(dve, ("krT",))
                    emptied_by_me(v.tensor_copy(KRT[64:96, :], b[64:96, :]))
                    emptied_now(dve, ("krT",))
                    attention(1)
                    emptied_now(dve, ("pv", 1, 11))
                    for t in range(NT):
                        fed[0] += 1
                        dve.sem_inc(to_pe, 1)
                to_features("mixT", layer)
                residual(layer)
                dve.sem_inc(mod_free, 1)
                adaln("h2T", layer, CONSTS + 16 + 32 * layer, 2 * layer + 2)
                route(layer)
                pairs(layer)
                every_expert(layer)
                dve.sem_inc(mod_free, 1)
            rstd(X, D)
            dve.wait_ge(consts_in, CONSTS + 64)
            for t in range(NT):
                ins = v.scalar_tensor_tensor(out=MIX[:, t, :], in0=X[:, t, :], scalar=small[:, 8 + t:9 + t],
                                             in1=normw[:], op0=ALU.mult, op1=ALU.mult)
            ins.then_inc(out_ready, 1)


_SCRATCH = [("h2_dram", (TOK, D)), ("y_dram", (PAIRS, P, D))]


def _constants():
    import numpy as np
    s, t = np.arange(P)[:, None], np.arange(P)[None, :]
    masks = []
    for h in LEVELS:
        same = s // (2 * h) == t // (2 * h)
        masks.append(same & (s % (2 * h) < h) & (t % (2 * h) >= h))
        masks.append(same & (s % (2 * h) >= h) & (t % (2 * h) < h))
    masks.append(s == t)
    band = np.zeros((P, 2, P), np.float32)
    band[:, 0, :][~(t <= s)] = -8e30
    band[:, 1, :][~(t >= s)] = -8e30

    def angles(dim):
        nf = dim // 4
        inv = np.exp(np.float32(-np.log(10000.0)) * np.arange(nf, dtype=np.float32) / np.float32(nf)).astype(np.float32)
        tok = np.arange(2 * P)
        ang = [(p.astype(np.float32)[:, None] * inv[None]).astype(np.float32) for p in (tok // 64, tok % 64)]
        cos = np.concatenate([np.cos(a) for a in (ang[0], ang[0], ang[1], ang[1])], 1)
        sin = np.concatenate([-np.sin(ang[0]), np.sin(ang[0]), -np.sin(ang[1]), np.sin(ang[1])], 1)
        return cos.astype(np.float32), sin.astype(np.float32)

    out = {"k_ident": np.eye(P, dtype=np.float32), "k_mask": np.stack(masks, 1).astype(np.int32), "k_band": band}
    for dim in (64, 32):
        cos, sin = angles(dim)
        out[f"k_rope{dim}"] = np.ascontiguousarray(np.stack([cos, sin]).reshape(2, 2, P, dim).transpose(2, 1, 0, 3))
    out["k_tri"] = np.stack([(s < t), np.ones((P, P), bool)], 1).astype(np.float32)
    e = np.arange(EXPERTS)
    row = np.concatenate([np.arange(P), np.arange(PAIRS), 64 * (e % 2), e // 2])
    out["k_tab"] = np.concatenate([np.broadcast_to(row, (P, row.size)), s + P * np.arange(NT)[None]], 1).astype(np.float32)
    ropeT = np.zeros((P, 2 * P), np.float32)
    ropeT[64:96], ropeT[96:128] = cos.T, sin.T
    out["k_ropeT"] = ropeT
    return out


_INS = ['x_prompt', 'x_sample', 'c', 'cache_swa_k', 'cache_swa_v', 'state_hgrn', 'cache_mla_ckv',
        'cache_mla_krope', 'c_ctx', 'mod_w', 'mod_b', 'norm1_w', 'norm2_w', 'final_norm_w',
        'even_w_in', 'even_w_out', 'swa_sink', 'hgrn_lb_fwd', 'hgrn_lb_bwd', 'hgrn_gnorm_w',
        'mla_w_dq', 'mla_qnorm_w', 'mla_w_uq', 'mla_w_dkv', 'mla_kvnorm_w', 'mla_w_ukv', 'mla_w_o',
        'moe_router_group_w', 'moe_router_group_b', 'moe_router_expert_w', 'moe_router_expert_b',
        'moe_w_gate', 'moe_w_up', 'moe_w_down']
_OUTS = [(1, 128, 1024), (1, 256, 1024), (1, 1, 128, 2, 64), (1, 1, 128, 2, 64), (1, 1, 2, 4, 128, 128),
         (1, 1, 128, 256), (1, 1, 128, 32)]


def kernel(**inputs):
    import numpy as np
    import concourse.bacc as bacc
    from concourse.bass_utils import run_bass_kernel_spmd

    nc = bacc.Bacc("TRN2", target_bir_lowering=False, num_devices=1)
    given = {name: np.ascontiguousarray(inputs[name]) for name in _INS}
    given.update(_constants())
    arrays, I, O = {}, {}, []
    for name, a in given.items():
        arrays[f"in_{name}"] = a
        I[name] = nc.dram_tensor(f"in_{name}", a.shape, mybir.dt.from_np(a.dtype), kind="ExternalInput").ap()
    for i, shape in enumerate(_OUTS):
        O.append(nc.dram_tensor(f"out_{i}", shape, mybir.dt.float32, kind="ExternalOutput").ap())
    mod_dram = nc.dram_tensor("mod_dram", (2, 2, 6 * D), mybir.dt.float32, kind="Internal").ap()
    scratch = [nc.dram_tensor(name, shape, mybir.dt.float32, kind="Internal").ap() for name, shape in _SCRATCH]
    build(nc, I, O, mod_dram, *scratch)
    r = run_bass_kernel_spmd(nc, [arrays], core_ids=[0])
    return tuple(r.results[0][f"out_{i}"] for i in range(len(_OUTS)))
```

```python
import concourse.bass as bass
from concourse import mybir
from contextlib import ExitStack

P = 128
D = 1024
DC = D // P
NT = 3
TOK = NT * P
HEADS, KVH, HD = 8, 2, 64
GH = 4
QKV = (HEADS + 2 * KVH) * HD
MH, QR, KVR, RD, ND, VD = 16, 384, 256, 32, 64, 64
EXPERTS, GROUPS, PER = 32, 4, 8
FF = 256
BANKS = 8
PAIRS = EXPERTS // 2
HALF = PAIRS // 2
CAP = 48
SLOTS = 2 * CAP
RING = 3
SLOT = 4096
LEVELS = [64, 32, 16, 8, 4, 2, 1]
EPS = 1e-6
WORK = 25600
HGRN_SCALE = P ** -0.5
LN2 = 0.6931471805599453
KEYT = 4


def attention_groups(layer):
    return [(g, t) for g in range(2 if layer == 0 else 4) for t in range(NT)]


def key_tiles(t):
    return [0] if t == 0 else [1, 2, 3]


MODS = 24
MOD_FIRST = 4
MOD_IN_PROJECTIONS = MOD_FIRST + 7
MOD_IN_ATTENTION = {n: MOD_IN_PROJECTIONS + n for n in range(6)}


def mod_after_level(lv):
    first = MOD_IN_PROJECTIONS + len(MOD_IN_ATTENTION)
    per = -(-(MODS - first) // len(LEVELS))
    return range(min(first + per * lv, MODS), min(first + per * (lv + 1), MODS))


def state_update(lv):
    return lv - 1 if 1 <= lv <= 4 else None


def score_heads(layer, t):
    if t == 0:
        return [[0, 1, 2, 3]] if layer else [[0, 2], [1, 3]]
    return [[0], [1], [2], [3]]


def matmul_jobs():
    jobs = []

    def add(key, eng):
        jobs.append((key, eng))

    def values(first, end):
        for kt in range(first, end):
            for k in range(2):
                add(("val", kt, k), "a")

    def attention(layer):
        groups = attention_groups(layer)

        def scores(n):
            for i in range(len(score_heads(layer, groups[n][1]))):
                add(("score", layer, n, i), "a")

        def queries_keys(g):
            for i in range(2):
                add(("kT", g, i), "v")
            for i in range(4):
                add(("qT1", g, i), "v")

        def results(n):
            add(("pv", layer, n), "v")
            if layer == 0 and n in MOD_IN_ATTENTION:
                add(("mod", MOD_IN_ATTENTION[n]), "v")

        if layer == 1:
            queries_keys(0)
            values(2, 4)
        scores(0)
        for n, (g, t) in enumerate(groups):
            if n + 1 < len(groups):
                scores(n + 1)
            if layer == 1 and t == 0 and g < 3:
                queries_keys(g + 1)
            for i in range(len(key_tiles(t))):
                add(("pT", layer, n, i), "a" if i == 0 else "v")
            if n:
                results(n - 1)
        results(len(groups) - 1)

    def to_features(kind, layer):
        for t in range(NT):
            for k in range(2):
                add((kind, layer, t, k), "v" if k else "a")

    for n in range(MOD_FIRST):
        add(("mod", n), "v")
    for layer in range(2):
        to_features("hT", layer)
        if layer == 0:
            projections = [("qff", b) for b in (1, 2, 0)] + [("qkv", b) for b in (0, 1)] + [("vg", b) for b in (0, 1)]
            for n, (kind, b) in enumerate(projections):
                for i in range(GH if kind == "qff" else NT):
                    add((kind, b, i), "a")
                add(("mod", MOD_FIRST + n), "v")
            for t in range(NT):
                add(("qT", t), "v")
            for k in range(2):
                add(("kT0", k), "v")
            attention(0)
            for lv in range(len(LEVELS)):
                for t in range(NT):
                    add(("lvl", lv, t), "v")
                u = state_update(lv)
                if u is not None:
                    add(("kdT", u), "a")
                for n in mod_after_level(lv):
                    add(("mod", n), "v")
                if u is not None:
                    add(("state", u), "v")
            for t in range(NT):
                add(("diag", t), "v")
            for t in range(NT):
                add(("o", t), "a")
        else:
            for b in (1, 0):
                for t in range(NT):
                    add(("dqkv", b, t), "a")
            for k in range(2):
                add(("ckvT", k), "v")
            add(("krT",), "v")
            values(0, 2)
            for t in range(NT):
                add(("cqT", t), "v")
            attention(1)
        to_features("mixT", layer)
        for n in range(2):
            for t in range(NT):
                add(("proj", layer, n, t), "v")
        to_features("h2T", layer)
        add(("router", layer), "v")
        add(("pos", layer), "v")
        add(("slot", layer), "v")
    return jobs


def build(nc, I, O, mod_dram, h2_dram, y_dram):
    f32, i32 = mybir.dt.float32, mybir.dt.int32
    ALU, ACT = mybir.AluOpType, mybir.ActivationFunctionType
    AX = mybir.AxisListType.X

    jobs = matmul_jobs()
    number = {key: n for n, (key, _) in enumerate(jobs)}
    drains = []
    count = {"v": 0, "a": 0}
    for _, e in jobs:
        count[e] += 1
        drains.append(count[e])

    with ExitStack() as ctx:
        def sb(name, shape, dt=f32):
            return ctx.enter_context(nc.sbuf_tensor(name, shape, dt))

        def sem(name):
            return ctx.enter_context(nc.semaphore(name))

        X = sb("X", [P, NT, D])
        hT = sb("hT", [P, DC, TOK])
        MOD = sb("MOD", [P, 2, 3, D])
        RINGB = sb("RINGB", [P, RING, SLOT])
        W = sb("W", [P, WORK])
        ident = sb("ident", [P, P])
        normw = sb("normw", [P, D])
        WR = sb("WR", [P, DC, 36])
        BR = sb("BR", [P, 36])
        cond = sb("cond", [P, 2, DC])
        cond2 = sb("cond2", [P, 2, DC])
        small = sb("small", [P, 64])
        banks = [ctx.enter_context(nc.psum_tensor(f"bank{i}", [P, 512], f32)) for i in range(BANKS)]

        def cut(at, shape, dt=None):
            n = 1
            for s in shape:
                n *= s
            v = W[:, at:at + n]
            if dt is not None:
                v = v.bitcast(dt)
            if len(shape) == 2:
                v = v.rearrange("p (a b) -> p a b", a=shape[0])
            if len(shape) == 3:
                v = v.rearrange("p (a b c) -> p a b c", a=shape[0], b=shape[1])
            return v

        modbias = cut(25088, (2, P))
        modrow = cut(25344, (2, P))
        MIX = cut(0, (NT, D))
        ATT = cut(3072, (NT, GH, P))
        QH = cut(4608, (GH, TOK))
        LF = cut(6144, (2, GH * TOK))
        KK = cut(9216, (2, GH * TOK))
        VV = cut(12288, (NT, GH * P))
        GG = cut(13824, (NT, GH * P))
        MASK = cut(15360, (8, P), i32)
        T0 = 17280
        QKVt = cut(T0, (NT, QKV))
        QT = cut(T0 + 2304, (4, TOK))
        KT = cut(T0 + 3840, (2, KEYT * P))
        KD = cut(T0 + 4864, (KEYT, KVH, 2 * HD))
        ROT = cut(T0 + 5888, (2, 640))
        VC = cut(T0 + 7424, (P,))
        band = cut(T0 + 7552, (2, P))
        hTf = hT[:].rearrange("p c n -> p (c n)")
        P0 = [hTf[:, 1536 * i:1536 * i + 1536].rearrange("p (h n) -> p h n", h=4) for i in range(2)]
        TD = [cut(T0 + 2304, (GH * TOK,)), cut(T0 + 5888, (GH * TOK,))]
        RESET = cut(3072, (GH * TOK,))
        PT0 = [cut(3072, (NT, 4 * P)), cut(T0 + 5888, (NT, 4 * P))]
        LE = [cut(T0 + 3072 * i, (GH * TOK,)) for i in range(2)]
        LK = [cut(T0 + 3072 * i + 1536, (GH * TOK,)) for i in range(2)]
        LEK = [cut(T0 + 3072 * i, (2 * GH * TOK,)) for i in range(2)]
        KDEC = [cut(T0 + 7168, (GH * P,)), MIX[:, 0, 512:1024]]
        KDT = cut(16384, (GH * P,))
        QI = [cut(T0 + 6144, (2, GH * P)), MIX[:, 1:3, 512:1024]]
        ST = hTf.rearrange("p (s n) -> p s n", s=6)
        OB = cut(T0, (NT, GH * P))
        OB2 = cut(T0 + 1536, (NT, GH * P))
        CQ = cut(3072, (NT, QR + KVR + RD))
        CACHE = cut(5088, (KVR,))
        KR = cut(5344, (KEYT, 96))
        CQT = cut(5728, (3, TOK))
        CKVT = cut(6880, (2, KEYT * P))
        VAL = cut(7904, (KEYT, MH * VD))
        Q1 = [cut(12000 + 1536 * i, (4, TOK)) for i in range(2)]
        K1 = [cut(15072 + 2048 * i, (4, KEYT * P)) for i in range(2)]
        P1 = [cut(19168 + 1536 * i, (4, TOK)) for i in range(2)]
        PT1 = [hTf[:, 1536 * i:1536 * i + 1536].rearrange("p (k n) -> p k n", k=3) for i in range(2)]
        KRT = cut(23776, (KEYT * P,))
        SQ = cut(24288, (QR,))
        qnw = cut(24672, (QR + KVR,))
        WQB = cut(3072, (3, 4 * P))
        RINGF = RINGB[:].rearrange("p s n -> p (s n)")
        WSET = [RINGF, cut(0, (3 * SLOT,))]
        XG = [cut(12288 + 1024 * i, (D,)) for i in range(2)]
        XGT = [cut(14336 + 1024 * i, (DC, P)) for i in range(2)]
        YS = [cut(16384 + 1024 * i, (D,)) for i in range(2)]
        ACTV = [cut(18432 + 256 * i, (FF,)) for i in range(2)]
        GE = [cut(18944 + 256 * i, (FF,)) for i in range(2)]
        ACTT = [cut(19456 + 256 * i, (2, P)) for i in range(2)]
        RT = cut(19968, (NT * 36 * 4,))
        COMB = cut(20400, (NT, EXPERTS))
        OVER = cut(20496, (NT, EXPERTS))
        S12 = cut(20592, (2 * NT, EXPERTS))
        SEL = cut(20784, (NT, EXPERTS))
        POS = cut(20880, (NT, EXPERTS))
        PROD = cut(20976, (2 * NT, EXPERTS))
        LOHI = cut(21168, (8, 2 * NT))
        PROD4 = cut(21216, (4, 2 * NT * EXPERTS))
        OHLO = cut(21216, (2 * NT, P))
        OHHI = cut(21984, (2 * NT, PAIRS))
        SEL2 = cut(22112, (NT, EXPERTS))
        IDX = cut(22080, (PAIRS,), i32)
        ROWI = cut(22096, (2 * NT,), i32)
        FULL = cut(22106, (1,), i32)
        FULLF = cut(22107, (1,))
        YG = cut(0, (2 * NT, D))
        YACC = cut(0, (NT, D))
        EE = cut(3200, (2, TOK))
        AT = cut(5000, (2, 2, TOK))

        rope_cs = sb("rope_cs", [P, 2, 2, HD])
        rope32 = sb("rope32", [P, 2, 2, RD])
        ropeT = sb("ropeT", [P, 2 * P])
        smallp = sb("smallp", [P, 3, 32])
        sink = sb("sink", [P, HEADS])
        lbc = sb("lbc", [P, 2, GH])
        lbs = sb("lbs", [P, 6, 2, GH])
        gnw = sb("gnw", [P, P])
        iota = sb("iota", [P, 16])
        tri = sb("tri", [P, 2, P])
        ktab = sb("ktab", [P, P + PAIRS + 2 * EXPERTS + NT])

        consts_in = sem("consts_in")
        tables_in = sem("tables_in")
        cond_in = sem("cond_in")
        tokens_in = sem("tokens_in")
        weight_in = [sem(f"weight_in{i}") for i in range(RING)]
        modbias_in = [sem(f"modbias_in{i}") for i in range(2)]
        block_used = sem("block_used")
        bank_filled = sem("bank_filled")
        emptied = {"v": sem("emptied_by_vector"), "a": sem("emptied_by_scalar")}
        v_step = sem("v_step")
        a_step = sem("a_step")
        to_act = sem("input_for_scalar")
        from_act = sem("output_of_scalar")
        to_pe = sem("input_for_tensor")
        cond_ready = sem("cond_ready")
        modrow_ready = sem("modrow_ready")
        modrow_out = [sem(f"modrow_out{i}") for i in range(2)]
        mod_ss_in = sem("shift_scale_in")
        mod_gate_in = sem("gate_in")
        xg_cleared = sem("xg_cleared")
        mod_free = sem("mod_free")
        router_in = sem("router_in")
        l1params_in = sem("l1params_in")
        pool_free = sem("pool_free")
        stored = sem("stored")
        out_ready = sem("out_ready")
        experts_over = sem("experts_over")
        h2_made = sem("h2_made")
        h2_out = sem("h2_out")
        pair_gu_in = [sem(f"pair_gu_in{i}") for i in range(2)]
        pair_dn_in = [sem(f"pair_down_in{i}") for i in range(2)]
        gathered = [sem(f"gathered{i}") for i in range(2)]
        idx_ready = sem("idx_ready")
        xt_filled = sem("xt_filled")
        xt_ready = {"v": sem("xt_ready_v"), "a": sem("xt_ready_a")}
        gu_filled = sem("gu_filled")
        gate_ready = sem("gate_ready")
        act_made = sem("act_made")
        actt_filled = sem("actt_filled")
        actt_ready = sem("actt_ready")
        y_filled = sem("y_filled")
        y_copied = {"v": sem("y_copied_v"), "a": sem("y_copied_a")}
        y_out = [sem(f"y_out{i}") for i in range(2)]
        y_back = [sem(f"y_back{i}") for i in range(NT)]
        pairs_over = sem("pairs_over")
        fb = [{k: sem(f"every{layer}_{k}") for k in ("gu_in0", "gu_in1", "dn_in0", "dn_in1", "gu_done", "gate_done",
                                                     "act_ready", "y_done", "y_emptied", "chain")}
              for layer in range(2)]

        UNITS = ((0, 0), (1, 0), (0, 1), (1, 2))

        blocks = []

        def rows(ap, chunks):
            return ap.rearrange("(p c) n -> p c n", c=chunks)

        def mod_block(n):
            b = n % 12
            blocks.append((("mod", n), rows(I["mod_w"][n // 12], DC)[:, :, b * 512:b * 512 + 512], (DC, 512)))

        WIN = [(0, 512), (512, 768), (768, 1280), (1280, 1792), (1792, 2304), (2304, 2816), (2816, 3328)]
        WIN_ORDER = (3, 4, 2, 0, 1, 5, 6)
        for n in range(MOD_FIRST):
            mod_block(n)
        for layer in range(2):
            if layer == 0:
                win = rows(I["even_w_in"][0], DC)
                for n, b in enumerate(WIN_ORDER):
                    lo, hi = WIN[b]
                    blocks.append((("win", b), win[:, :, lo:hi], (DC, hi - lo)))
                    mod_block(MOD_FIRST + n)
                for n in range(MOD_IN_PROJECTIONS, MODS):
                    mod_block(n)
                for n in range(2):
                    blocks.append((("wout", 0, n), rows(I["even_w_out"][0], DC)[:, :, n * 512:n * 512 + 512], (DC, 512)))
            else:
                blocks.append((("dkv",), rows(I["mla_w_dkv"][0], DC), (DC, KVR + RD)))
                blocks.append((("dq",), rows(I["mla_w_dq"][0], DC), (DC, QR)))
                blocks.append((("ukv",), rows(I["mla_w_ukv"][0], 2), (2, 2048)))
                for n in range(2):
                    blocks.append((("uq", n), rows(I["mla_w_uq"][0], 3)[:, :, n * 768:n * 768 + 768], (3, 768)))
                for n in range(2):
                    blocks.append((("wout", 1, n), rows(I["mla_w_o"][0], DC)[:, :, n * 512:n * 512 + 512], (DC, 512)))
        blockno = {key: n for n, (key, _, _) in enumerate(blocks)}
        first1 = blockno[("dkv",)]

        def block_view(key):
            n = blockno[key]
            c, w = blocks[n][2]
            return RINGB[:, n % RING, 0:c * w].rearrange("p (c n) -> p c n", c=c)

        def weights_arrived(eng, key):
            n = blockno[key]
            eng.wait_ge(weight_in[n % RING], 16 * (n // RING + 1))

        def filled(eng, key):
            n = number[key]
            eng.wait_ge(bank_filled, n + 1)
            return banks[n % BANKS]

        def emptied_now(eng, key):
            n = number[key]
            eng.wait_ge(emptied[jobs[n][1]], drains[n])

        block = ctx.enter_context(nc.Block())

        wg = lambda layer, e: I["moe_w_gate"][layer, e, :, :].rearrange("(p c) n -> p c n", c=DC)
        wu = lambda layer, e: I["moe_w_up"][layer, e, :, :].rearrange("(p c) n -> p c n", c=DC)
        wd = lambda layer, e: I["moe_w_down"][layer, e, :, :].rearrange("(p c) n -> p c n", c=2)

        def gu_slot(q):
            return RINGB[:, q, :].rearrange("p (g c n) -> p g c n", g=2, c=DC)

        def dn_slot(q):
            return RINGB[:, 2, q * 2048:q * 2048 + 2048].rearrange("p (c n) -> p c n", c=2)

        def pair_gu(sset):
            return WSET[sset][:, 0:8192].rearrange("p (e g n) -> p e g n", e=2, g=2)

        def pair_dn(sset):
            return WSET[sset][:, 8192:12288].rearrange("p (e n) -> p e n", e=2)

        def at_least(eng, semaphore, value):
            if not isinstance(value, int) or value > 0:
                eng.wait_ge(semaphore, value)

        def overflow(eng):
            return eng.value_load(FULL[0:1, 0:1], min_val=0, max_val=TOK) > CAP

        def over_pairs(eng, step):
            with eng.Fori(0, HALF - 1) as k:
                for j in range(2):
                    step(2 * k + 1 + j, (1 + j) % 2)

        @block.sync
        def _(sp):
            def load(n):
                if n >= RING:
                    sp.wait_ge(block_used, n - RING + 1)
                if n == MOD_FIRST:
                    sp.wait_ge(mod_ss_in, 32)
                key, src, (c, w) = blocks[n]
                sp.dma_start(block_view(key), src).then_inc(weight_in[n % RING], 16)
                if key[0] == "mod":
                    m = key[1]
                    if m >= 2:
                        sp.wait_ge(modrow_ready, m - 1)
                    bias = I["mod_b"][m // 12, m % 12 * 512:m % 12 * 512 + 512].rearrange("(j n) -> j n", n=P)
                    for g in range(2):
                        sp.dma_start(modbias[g:g + 97:32, m % 2, :], bias).then_inc(modbias_in[m % 2], 16)

            def pairs(layer):
                B = PAIRS * layer

                def load_pair(i, q):
                    def part(name):
                        if isinstance(i, int):
                            return I[name][layer, 2 * i:2 * i + 2]
                        return I[name][layer, bass.ds(2 * i, 2)]
                    gu, dn = pair_gu(q), pair_dn(q)
                    if not (isinstance(i, int) and i < 2):
                        sp.wait_ge(gu_filled, B + i - 1)
                    for g, name in enumerate(("moe_w_gate", "moe_w_up")):
                        sp.dma_start(gu[:, :, g, :], part(name).rearrange("e (p c) n -> p e (c n)", c=DC)).then_inc(pair_gu_in[q], 16)
                    if isinstance(i, int) and i == 1:
                        sp.wait_ge(gathered[0], 16 * (HALF * layer + 1))
                    if not (isinstance(i, int) and i < 2):
                        sp.wait_ge(y_filled, B + i - 1)
                    sp.dma_start(dn, part("moe_w_down").rearrange("e (p c) n -> p e (c n)", c=2)).then_inc(pair_dn_in[q], 16)

                sp.wait_ge(block_used, first1 if layer == 0 else len(blocks))
                load_pair(0, 0)
                sp.wait_ge(h2_out, 16 * (layer + 1))
                sp.wait_ge(bank_filled, number[("h2T", layer, NT - 1, 1)] + 1)
                load_pair(1, 1)
                with sp.Fori(0, HALF - 1) as k:
                    for q in range(2):
                        load_pair(2 * k + 2 + q, q)

            def every_expert(layer):
                F = fb[layer]

                def load_expert(e, q, after):
                    if after is not None:
                        sp.wait_ge(F["gu_done"], after)
                    sp.dma_start(gu_slot(q)[:, 0], wg(layer, e)).then_inc(F[f"gu_in{q}"], 16)
                    sp.dma_start(gu_slot(q)[:, 1], wu(layer, e)).then_inc(F[f"gu_in{q}"], 16)
                    if after is not None:
                        sp.wait_ge(F["y_done"], after * 3)
                    sp.dma_start(dn_slot(q), wd(layer, e)).then_inc(F[f"dn_in{q}"], 16)

                sp.wait_ge(pairs_over, layer + 1)
                with sp.If(overflow(sp)):
                    for q in range(2):
                        load_expert(q, q, None)
                    with sp.Fori(0, EXPERTS // 2 - 1) as i:
                        for q in range(2):
                            load_expert(2 * i + 2 + q, q, 4 * i + 2 * q + 2)

            for n in range(first1):
                load(n)
            pairs(0)
            every_expert(0)
            sp.wait_ge(experts_over, 1)
            sp.wait_ge(y_back[NT - 1], 32)
            for n in range(first1, len(blocks)):
                load(n)
            pairs(1)
            every_expert(1)

        @block.gpsimd
        def _(pool):
            def dma(out, src, s):
                pool.dma_start(out, src).then_inc(s, 16)
            dma(cond2[:, 0, :], I["c_ctx"].rearrange("(p c) -> p c", c=DC), cond_in)
            dma(cond2[:, 1, :], I["c"][0].rearrange("(p c) -> p c", c=DC), cond_in)

            def rowblocks(first, end):
                for m in range(first, end):
                    pool.wait_ge(modrow_ready, m + 1)
                    for g in range(2):
                        dma(mod_dram[m // 12, g, m % 12 * 512:m % 12 * 512 + 512].rearrange("(j n) -> j n", n=P),
                            modrow[g:g + 97:32, m % 2, :], modrow_out[m % 2])

            def spread(layer, part, lo, hi, s):
                last = 12 * layer + 6 * part + 2 * hi
                for par in range(2):
                    pool.wait_ge(modrow_out[par], 32 * ((last + 1 - par) // 2))
                for g in range(2):
                    src = mod_dram[layer, g:g + 1, (part * 3 + lo) * D:(part * 3 + hi) * D]
                    dma(MOD[:, g, lo:hi, :].rearrange("p v d -> p (v d)"), src.to_broadcast([P, (hi - lo) * D]), s)

            def router(layer):
                if layer:
                    emptied_now(pool, ("router", 0))
                dma(WR[:, :, 0:4], I["moe_router_group_w"][layer].rearrange("(p c) n -> p c n", c=DC), router_in)
                for g in range(GROUPS):
                    dma(WR[:, :, 4 + 8 * g:12 + 8 * g],
                        I["moe_router_expert_w"][layer, g].rearrange("(p c) n -> p c n", c=DC), router_in)
                dma(BR[:, 0:4], I["moe_router_group_b"][layer:layer + 1, :].to_broadcast([P, 4]), router_in)
                dma(BR[:, 4:36], I["moe_router_expert_b"][layer].rearrange("g e -> (g e)").unsqueeze(0).to_broadcast([P, 32]), router_in)

            def pairs(layer, meanwhile):
                B = PAIRS * layer
                pool.wait_ge(h2_made, layer + 1)
                for q in range(2):
                    nc.gpsimd.memset(XG[q], 0.0).then_inc(xg_cleared, 1)
                pool.wait_ge(xg_cleared, 2 * (layer + 1))
                dma(h2_dram.rearrange("(t p) d -> p t d", p=P), MIX, h2_out)
                pool.wait_ge(h2_out, 16 * (layer + 1))
                pool.wait_ge(idx_ready, layer + 1)

                def gather(i, q):
                    if i >= 2:
                        pool.wait_ge(xt_filled, B + i - 1)
                    pool.indirect_dma_start(XG[q][0:SLOTS], None, h2_dram,
                                            bass.IndirectOffsetOnAxis(ap=IDX[0:SLOTS, i:i + 1], axis=0),
                                            bounds_check=TOK - 1, oob_is_err=False)\
                        .then_inc(gathered[q], 16)

                def store(i, q):
                    pool.wait_ge(y_copied["v"], B + i + 1)
                    pool.wait_ge(y_copied["a"], B + i + 1)
                    for e in range(2):
                        dma(y_dram[i, CAP * e:CAP * e + CAP], YS[q][64 * e:64 * e + CAP], y_out[q])

                gather(0, 0)
                gather(1, 1)
                meanwhile()
                for i in range(PAIRS):
                    if i + 2 < PAIRS:
                        gather(i + 2, i % 2)
                    store(i, i % 2)
                for q in range(2):
                    pool.wait_ge(y_out[q], 32 * HALF * (layer + 1))
                pool.wait_ge(experts_over, layer + 1)
                for t in range(NT):
                    for j in range(2):
                        pool.indirect_dma_start(YG[:, j * NT + t, :], None, y_dram.rearrange("a p d -> (a p) d"),
                                                bass.IndirectOffsetOnAxis(ap=ROWI[:, j * NT + t:j * NT + t + 1], axis=0))\
                            .then_inc(y_back[t], 16)

            rowblocks(0, 1)
            dma(X[:, 0, :], I["x_prompt"][0], tokens_in)
            dma(X[:, 1:3, :], I["x_sample"][0].rearrange("(t p) d -> p t d", p=P), tokens_in)
            dma(ident[:], I["k_ident"], consts_in)
            dma(normw[:], I["norm1_w"][0:1, :].to_broadcast([P, D]), consts_in)
            for d, nm in enumerate(("hgrn_lb_fwd", "hgrn_lb_bwd")):
                with nc.allow_non_contiguous_dma(reason="512 values, once"):
                    dma(lbc[:, d, :], I[nm][0].rearrange("(h p) -> p h", p=P), consts_in)
            rowblocks(1, MOD_FIRST)
            spread(0, 0, 0, 2, mod_ss_in)
            dma(MASK, I["k_mask"], tables_in)
            dma(rope_cs[:], I["k_rope64"], tables_in)
            dma(rope32[:], I["k_rope32"], tables_in)
            dma(ropeT[:], I["k_ropeT"], tables_in)
            dma(sink[:], I["swa_sink"][0:1, :].to_broadcast([P, HEADS]), tables_in)
            dma(gnw[:], I["hgrn_gnorm_w"][0:1, :].to_broadcast([P, P]), tables_in)
            dma(band, I["k_band"], tables_in)
            dma(tri[:], I["k_tri"], tables_in)
            dma(ktab[:], I["k_tab"], tables_in)
            router(0)
            for dup in range(2):
                dma(KD[:, 1, :, dup * HD:dup * HD + HD], I["cache_swa_k"][0, 0], l1params_in)
            dma(VC, I["cache_swa_v"][0, 0].rearrange("s h d -> s (h d)"), l1params_in)
            pool.wait_ge(pool_free, 1)
            dma(normw[:], I["norm2_w"][0:1, :].to_broadcast([P, D]), consts_in)
            rowblocks(MOD_FIRST, 6)
            spread(0, 0, 2, 3, mod_gate_in)
            rowblocks(6, 8)
            emptied_now(pool, ("qkv", 1, 0))
            dma(O[2][0, 0].rearrange("s h d -> s (h d)"), QKVt[:, 0, 512:640], stored)
            dma(O[3][0, 0].rearrange("s h d -> s (h d)"), QKVt[:, 0, 640:768], stored)
            rowblocks(8, 10)
            spread(0, 1, 0, 2, mod_ss_in)
            rowblocks(10, MOD_IN_PROJECTIONS + len(MOD_IN_ATTENTION))
            pool.wait_ge(out_ready, 1)
            dma(ST[:, 0, :].rearrange("p (h e) -> p h e", h=GH), I["state_hgrn"][0, 0, 0].rearrange("h k v -> k h v"), l1params_in)
            dma(ST[:, 1, :].rearrange("p (h e) -> p h e", h=GH), I["state_hgrn"][0, 0, 1].rearrange("h k v -> k h v"), l1params_in)
            rowblocks(MOD_IN_PROJECTIONS + len(MOD_IN_ATTENTION), mod_after_level(1).start)
            for d in range(2):
                rowblocks(mod_after_level(1 + d).start, mod_after_level(1 + d).stop)
                pool.wait_ge(out_ready, 2 + d)
                dma(O[4][0, 0, d].rearrange("h k v -> k h v"), ST[:, 2 + d, :].rearrange("p (h e) -> p h e", h=GH), stored)
            rowblocks(mod_after_level(3).start, MODS)

            def gate_and_next_norm():
                pool.wait_ge(mod_free, 1)
                spread(0, 1, 2, 3, mod_gate_in)
                pool.wait_ge(pool_free, 2)
                dma(normw[:], I["norm1_w"][1:2, :].to_broadcast([P, D]), consts_in)
                spread(1, 0, 0, 2, mod_ss_in)

            pairs(0, gate_and_next_norm)
            router(1)
            pool.wait_ge(mod_free, 2)
            spread(1, 0, 2, 3, mod_gate_in)
            dma(qnw[:, 0:QR], I["mla_qnorm_w"][0:1, :].to_broadcast([P, QR]), l1params_in)
            dma(qnw[:, QR:QR + KVR], I["mla_kvnorm_w"][0:1, :].to_broadcast([P, KVR]), l1params_in)
            dma(CACHE, I["cache_mla_ckv"][0, 0], l1params_in)
            pool.wait_ge(pool_free, 3)
            spread(1, 1, 0, 2, mod_ss_in)
            dma(normw[:], I["norm2_w"][1:2, :].to_broadcast([P, D]), consts_in)
            pool.wait_ge(out_ready, 4)
            dma(KR[:, 1, 64:96], I["cache_mla_krope"][0, 0], l1params_in)
            pool.wait_ge(out_ready, 5)
            dma(O[5][0, 0], CQ[:, 0, QR:QR + KVR], stored)
            dma(O[6][0, 0], CQ[:, 0, QR + KVR:], stored)

            def gate_and_final_norm():
                pool.wait_ge(mod_free, 3)
                spread(1, 1, 2, 3, mod_gate_in)
                pool.wait_ge(pool_free, 4)
                dma(normw[:], I["final_norm_w"].unsqueeze(0).to_broadcast([P, D]), consts_in)

            pairs(1, gate_and_final_norm)
            pool.wait_ge(out_ready, 6)
            dma(O[0][0], MIX[:, 0, :], stored)
            dma(O[1][0].rearrange("(t p) d -> p t d", p=P), MIX[:, 1:3, :], stored)
            pool.wait_ge(stored, 16 * 8)

        CONSTS = 16 * 4

        @block.tensor
        def _(pe):
            inputs = [0]

            def new_input():
                inputs[0] += 1
                pe.wait_ge(to_pe, inputs[0])

            def bank(key):
                n = number[key]
                if n >= BANKS:
                    pe.wait_ge(emptied[jobs[n - BANKS][1]], drains[n - BANKS])
                return banks[n % BANKS]

            def contract(out, lhs, rhs, chunks):
                for c in range(chunks):
                    last = nc.tensor.matmul(out, lhs(c), rhs(c), start=(c == 0), stop=(c == chunks - 1))
                return last

            def transposed(kind, layer, src):
                for t in range(NT):
                    new_input()
                    for k in range(2):
                        b = bank((kind, layer, t, k))
                        for j in range(4):
                            last = nc.tensor.transpose(b[:, j * P:(j + 1) * P], src[:, t, 4 * k + j::DC], ident[:])
                        last.then_inc(bank_filled, 1)

            def modulation(m):
                key = ("mod", m)
                weights_arrived(pe, key)
                w = block_view(key)
                out = bank(key)
                for c in range(DC):
                    for j in range(4):
                        last = nc.tensor.matmul(out[32 * j:32 * j + 2, 0:P], cond[:, :, c], w[:, c, j * P:(j + 1) * P],
                                                start=(c == 0), stop=(c == DC - 1))
                last.then_inc(bank_filled, 1)
                used(key)

            def used(key):
                pe.wait_ge(bank_filled, number[key] + 1)
                pe.sem_inc(block_used, 1)

            def values(first, end):
                kv = block_view(("ukv",)).rearrange("p c (h n) -> p c h n", h=MH)
                for kt in range(first, end):
                    for k in range(2):
                        out = bank(("val", kt, k))
                        contract(out[:, :], lambda c: CKVT[:, c, kt * P:(kt + 1) * P],
                                 lambda c: kv[:, c, 8 * k:8 * k + 8, ND:], 2).then_inc(bank_filled, 1)

            def attention(layer):
                groups = attention_groups(layer)

                def queries_keys(g):
                    if g % 2 == 0:
                        weights_arrived(pe, ("uq", g // 2))
                    kv = block_view(("ukv",)).rearrange("p c (h n) -> p c h n", h=MH)
                    for i in range(2):
                        key = ("kT", g, i)
                        out = bank(key)
                        h = 4 * g + 2 * i
                        for j in range(2):
                            last = contract(out[64 * j:64 * j + 64, :], lambda c: kv[:, c, h + j, 0:ND],
                                            lambda c: CKVT[:, c, :], 2)
                        last.then_inc(bank_filled, 1)
                    new_input()
                    for i in range(4):
                        out = bank(("qT1", g, i))
                        contract(out[:, 0:TOK], lambda c: WQB[:, c, i * P:(i + 1) * P], lambda c: CQT[:, c, :], 3)\
                            .then_inc(bank_filled, 1)
                    if g == 3:
                        for _ in range(3):
                            used(("qT1", g, 3))

                def scores(n):
                    g, t = groups[n]
                    if layer == 1 and t == 0:
                        new_input()
                    kts = key_tiles(t)
                    nk = len(kts) * P
                    for i, hs in enumerate(score_heads(layer, t)):
                        out = bank(("score", layer, n, i))
                        for j, h in enumerate(hs):
                            o = out[:, j * nk:(j + 1) * nk]
                            if layer == 0:
                                hh = (4 * g + h) % 2
                                q = QT[64 * hh:64 * hh + 64, (4 * g + h) // 2, t * P:(t + 1) * P]
                                k = KT[64 * hh:64 * hh + 64, g, kts[0] * P:kts[0] * P + nk]
                            else:
                                q = Q1[g % 2][0:96, h, t * P:(t + 1) * P]
                                k = K1[g % 2][0:96, h, kts[0] * P:kts[0] * P + nk]
                            masked = layer == 0 and t > 0
                            last = nc.tensor.matmul(o, q, k, start=True, stop=not masked)
                            if masked:
                                far = 3 if t == 1 else 2
                                last = nc.tensor.matmul(out[:, (far - 1) * P:far * P], ident[:], band[:, t - 1, :],
                                                        start=False, stop=True)
                        last.then_inc(bank_filled, 1)

                def results(n):
                    g, t = groups[n]
                    kts = key_tiles(t)
                    pt = (PT0 if layer == 0 else PT1)[n % 2]
                    out = bank(("pv", layer, n))
                    emptied_now(pe, ("pT", layer, n, 0))
                    emptied_now(pe, ("pT", layer, n, len(kts) - 1))
                    for h in range(4):
                        for i, kt in enumerate(kts):
                            if layer == 0:
                                v = VC[:, g * HD:(g + 1) * HD] if kt == 1 else \
                                    QKVt[:, 0 if kt == 0 else kt - 1, 640 + g * HD:640 + (g + 1) * HD]
                            else:
                                v = VAL[:, kt, (4 * g + h) * VD:(4 * g + h + 1) * VD]
                            last = nc.tensor.matmul(out[:, h * 64:(h + 1) * 64], pt[:, i, h * P:(h + 1) * P], v,
                                                    start=(i == 0), stop=(i == len(kts) - 1))
                    last.then_inc(bank_filled, 1)
                    if layer == 0 and n in MOD_IN_ATTENTION:
                        modulation(MOD_IN_ATTENTION[n])

                if layer == 1:
                    queries_keys(0)
                    values(2, 4)
                scores(0)
                if layer == 1:
                    for kt in range(KEYT):
                        emptied_now(pe, ("val", kt, 1))
                for n, (g, t) in enumerate(groups):
                    if n + 1 < len(groups):
                        scores(n + 1)
                    if layer == 1 and t == 0 and g < 3:
                        queries_keys(g + 1)
                    kts = key_tiles(t)
                    prob = (P0 if layer == 0 else P1)[n % 2]
                    emptied_now(pe, ("score", layer, n, len(score_heads(layer, t)) - 1))
                    pr = prob.rearrange("p h k -> p (h k)")[:, 0:4 * P * len(kts)].rearrange("p (h k) -> p h k", h=4)
                    for i in range(len(kts)):
                        out = bank(("pT", layer, n, i))
                        for h in range(4):
                            last = nc.tensor.transpose(out[:, h * P:(h + 1) * P], pr[:, h, i * P:(i + 1) * P], ident[:])
                        last.then_inc(bank_filled, 1)
                    if n:
                        results(n - 1)
                results(len(groups) - 1)

            def project(layer):
                transposed("mixT", layer, MIX)
                for n in range(2):
                    weights_arrived(pe, ("wout", layer, n))
                    w = block_view(("wout", layer, n))
                    for t in range(NT):
                        if n == 0:
                            emptied_now(pe, ("mixT", layer, t, 0))
                            emptied_now(pe, ("mixT", layer, t, 1))
                        out = bank(("proj", layer, n, t))
                        contract(out[:, :], lambda c: hT[:, c, t * P:(t + 1) * P], lambda c: w[:, c, :], DC)\
                            .then_inc(bank_filled, 1)
                    used(("proj", layer, n, NT - 1))

            def router(layer):
                transposed("h2T", layer, MIX)
                pe.wait_ge(router_in, 16 * 7 * (layer + 1))
                out = bank(("router", layer))
                for t in range(NT):
                    emptied_now(pe, ("h2T", layer, t, 0))
                    emptied_now(pe, ("h2T", layer, t, 1))
                    last = contract(out[:, t * 36:t * 36 + 36], lambda c: hT[:, c, t * P:(t + 1) * P],
                                    lambda c: WR[:, c, :], DC)
                last.then_inc(bank_filled, 1)

            def assign(layer):
                new_input()
                out = bank(("pos", layer))
                for t in range(NT):
                    cols = out[:, t * EXPERTS:(t + 1) * EXPERTS]
                    last = nc.tensor.matmul(cols, tri[:, 0, :], SEL[:, t, :], start=True, stop=(t == 0))
                    for u in range(t):
                        last = nc.tensor.matmul(cols, tri[:, 1, :], SEL[:, u, :], start=False, stop=(u == t - 1))
                for t in range(NT):
                    last = nc.tensor.matmul(out[:, NT * EXPERTS:(NT + 1) * EXPERTS], tri[:, 1, :], SEL[:, t, :],
                                            start=(t == 0), stop=(t == NT - 1))
                last.then_inc(bank_filled, 1)
                new_input()
                out = bank(("slot", layer))
                for j in range(2 * NT):
                    last = nc.tensor.matmul(out[:, 0:PAIRS], OHLO[:, j, :], OHHI[:, j, :], start=(j == 0), stop=(j == 2 * NT - 1))
                last.then_inc(bank_filled, 1)
                emptied_now(pe, ("slot", layer))

            def pairs(layer):
                B = PAIRS * layer

                def turn(i, q):
                    pe.wait_ge(gathered[q], 16 * (HALF * layer + 1) + 8 * (i - q))
                    for e in ("v", "a"):
                        at_least(pe, xt_ready[e], B + i)
                    for c in range(DC):
                        last = nc.tensor.transpose(banks[c // 4][:, (c % 4) * P:(c % 4 + 1) * P], XG[q][:, c::DC], ident[:])
                    last.then_inc(xt_filled, 1)

                def gate_up(i, q):
                    for e in ("v", "a"):
                        pe.wait_ge(xt_ready[e], B + i + 1)
                    at_least(pe, act_made, B + i - 1)
                    pe.wait_ge(pair_gu_in[q], 32 * (HALF * layer + 1) + 16 * (i - q))
                    w = pair_gu(q).rearrange("p e g (c n) -> p e g c n", c=DC)
                    for c in range(DC):
                        for e in range(2):
                            last = nc.tensor.matmul(banks[2 + q][64 * e:64 * e + 64, :], XGT[q][:, c, CAP * e:CAP * e + 64],
                                                    w[:, e, :, c, :], start=(c == 0), stop=(c == DC - 1))
                    last.then_inc(gu_filled, 1)

                def turn_act(i, q):
                    pe.wait_ge(act_made, B + i + 1)
                    at_least(pe, actt_ready, B + i)
                    for f in range(2):
                        last = nc.tensor.transpose(banks[4][:, f * P:(f + 1) * P], ACTV[q][:, f::2], ident[:])
                    last.then_inc(actt_filled, 1)

                def down(i, q):
                    pe.wait_ge(actt_ready, B + i + 1)
                    pe.wait_ge(pair_dn_in[q], 16 * (HALF * layer + 1) + 8 * (i - q))
                    for e in ("v", "a"):
                        at_least(pe, y_copied[e], B + i)
                    w = pair_dn(q).rearrange("p e (c n) -> p e c n", c=2)
                    for n in range(2):
                        for c in range(2):
                            for e in range(2):
                                last = nc.tensor.matmul(banks[5 + n][64 * e:64 * e + 64, :], ACTT[q][:, c, 64 * e:64 * e + 64],
                                                        w[:, e, c, n * 512:(n + 1) * 512], start=(c == 0), stop=(c == 1))
                    last.then_inc(y_filled, 1)

                def step(i, q):
                    gate_up(i, q)
                    down(i - 1, 1 - q)
                    turn(i + 1, 1 - q)
                    turn_act(i, q)

                turn(0, 0)
                gate_up(0, 0)
                turn(1, 1)
                turn_act(0, 0)
                over_pairs(pe, step)
                gate_up(PAIRS - 1, 1)
                down(PAIRS - 2, 0)
                turn_act(PAIRS - 1, 1)
                down(PAIRS - 1, 1)

            def every_expert(layer):
                F = fb[layer]
                pe.wait_ge(pairs_over, layer + 1)
                with pe.If(overflow(pe)):
                    with pe.Fori(0, EXPERTS // 2) as i:
                        for q in range(2):
                            pe.wait_ge(F[f"gu_in{q}"], 32 + 32 * i)
                            for f in range(2):
                                pe.wait_ge(F["act_ready"], 2 * q + f + 1 + 4 * i)
                                for g in range(2):
                                    last = contract(banks[2 * g + f][:, 0:TOK], lambda c: gu_slot(q)[:, g, c, f::2],
                                                    lambda c: hT[:, c, :], DC)
                                last.then_inc(F["gu_done"], 1)
                            pe.wait_ge(F[f"dn_in{q}"], 16 + 16 * i)
                            pe.wait_ge(F["act_ready"], 2 * q + 4 + 4 * i)
                            for j in range(6):
                                n, t = divmod(j, NT)
                                k = 6 * q + j
                                pe.wait_ge(F["y_emptied"], k + 1 + 12 * i)
                                contract(banks[4 + k % 4][:, :], lambda c: AT[:, q, c, t * P:(t + 1) * P],
                                         lambda c: dn_slot(q)[:, c, n * 512:(n + 1) * 512], 2).then_inc(F["y_done"], 1)
                pe.wait_ge(experts_over, layer + 1)

            pe.wait_ge(cond_ready, 1)
            for m in range(MOD_FIRST):
                modulation(m)
            for layer in range(2):
                if layer == 0:
                    pe.wait_ge(consts_in, CONSTS)
                transposed("hT", layer, MIX)
                for t in range(NT):
                    for k in range(2):
                        emptied_now(pe, ("hT", layer, t, k))
                if layer == 0:
                    for nth, b in enumerate(WIN_ORDER):
                        weights_arrived(pe, ("win", b))
                        w = block_view(("win", b))
                        if b in (0, 1, 5, 6):
                            for t in range(NT):
                                key = ("qkv", b, t) if b < 2 else ("vg", b - 5, t)
                                out = bank(key)
                                contract(out[:, 0:blocks[blockno[("win", b)]][2][1]],
                                         lambda c: hT[:, c, t * P:(t + 1) * P], lambda c: w[:, c, :], DC)\
                                    .then_inc(bank_filled, 1)
                        else:
                            for h in range(GH):
                                key = ("qff", b - 2, h)
                                out = bank(key)
                                contract(out[:, 0:TOK], lambda c: w[:, c, h * P:(h + 1) * P], lambda c: hT[:, c, :], DC)\
                                    .then_inc(bank_filled, 1)
                        used(key)
                        modulation(MOD_FIRST + nth)
                    pe.wait_ge(tables_in, 16 * 9)
                    new_input()
                    for t in range(NT):
                        out = bank(("qT", t))
                        for j in range(4):
                            last = nc.tensor.transpose(out[:, j * P:(j + 1) * P], QKVt[:, t, j * P:(j + 1) * P], ident[:])
                        last.then_inc(bank_filled, 1)
                    for k in range(2):
                        out = bank(("kT0", k))
                        for j in range(4):
                            last = nc.tensor.transpose(out[:, j * P:(j + 1) * P], KD[:, 2 * k + j // 2, j % 2, :], ident[:])
                        last.then_inc(bank_filled, 1)
                    emptied_now(pe, ("qT", 2))
                    emptied_now(pe, ("kT0", 1))
                    attention(0)
                    for lv in range(len(LEVELS)):
                        new_input()
                        for t in range(NT):
                            out = bank(("lvl", lv, t))
                            for h in range(GH):
                                at = h * TOK + t * P
                                last = nc.tensor.matmul(out[:, h * P:(h + 1) * P], LK[lv % 2][:, at:at + P],
                                                        LE[lv % 2][:, at:at + P], start=True, stop=True)
                            last.then_inc(bank_filled, 1)
                        u = state_update(lv)
                        if u is not None:
                            new_input()
                            out = bank(("kdT", u))
                            for h in range(GH):
                                last = nc.tensor.transpose(out[:, h * P:(h + 1) * P], KDEC[u % 2][:, h * P:(h + 1) * P], ident[:])
                            last.then_inc(bank_filled, 1)
                        for m in mod_after_level(lv):
                            modulation(m)
                        if u is not None:
                            out = bank(("state", u))
                            emptied_now(pe, ("kdT", u))
                            t = UNITS[u][1]
                            for h in range(GH):
                                last = nc.tensor.matmul(out[:, h * P:(h + 1) * P], KDT[:, h * P:(h + 1) * P],
                                                        VV[:, t, h * P:(h + 1) * P], start=True, stop=True)
                            last.then_inc(bank_filled, 1)
                    new_input()
                    for t in range(NT):
                        out = bank(("diag", t))
                        for h in range(GH):
                            at = h * TOK + t * P
                            last = nc.tensor.matmul(out[:, h * P:(h + 1) * P], LK[1][:, at:at + P],
                                                    QH[:, h, t * P:(t + 1) * P], start=True, stop=True)
                        last.then_inc(bank_filled, 1)
                    emptied_now(pe, ("state", 3))
                    emptied_now(pe, ("diag", 2))
                    for t in range(NT):
                        out = bank(("o", t))
                        for h in range(GH):
                            hs = slice(h * P, (h + 1) * P)
                            last = nc.tensor.matmul(out[:, hs], ATT[:, t, h, :], VV[:, t, hs], start=True, stop=(t == 0))
                            if t:
                                for d in range(2):
                                    s = (0 if t == 1 else 4) if d == 0 else (1 if t == 2 else 5)
                                    last = nc.tensor.matmul(out[:, hs], QI[d][:, t - 1, hs], ST[:, s, hs],
                                                            start=False, stop=(d == 1))
                        last.then_inc(bank_filled, 1)
                else:
                    for b, nm, n in ((1, "dkv", KVR + RD), (0, "dq", QR)):
                        weights_arrived(pe, (nm,))
                        w = block_view((nm,))
                        for t in range(NT):
                            out = bank(("dqkv", b, t))
                            contract(out[:, 0:n], lambda c: hT[:, c, t * P:(t + 1) * P], lambda c: w[:, c, :], DC)\
                                .then_inc(bank_filled, 1)
                        used(("dqkv", b, NT - 1))
                    new_input()
                    for k in range(2):
                        out = bank(("ckvT", k))
                        for j in range(4):
                            kt, c = 2 * k + j // 2, j % 2
                            src = CACHE[:, c::2] if kt == 1 else CQ[:, 0 if kt == 0 else kt - 1, QR + c:QR + KVR:2]
                            last = nc.tensor.transpose(out[:, j * P:(j + 1) * P], src, ident[:])
                        last.then_inc(bank_filled, 1)
                    out = bank(("krT",))
                    for kt in range(KEYT):
                        last = nc.tensor.transpose(out[0:96, kt * P:(kt + 1) * P], KR[:, kt, :], ident[:])
                    last.then_inc(bank_filled, 1)
                    emptied_now(pe, ("krT",))
                    weights_arrived(pe, ("ukv",))
                    values(0, 2)
                    new_input()
                    for t in range(NT):
                        out = bank(("cqT", t))
                        for c in range(3):
                            last = nc.tensor.transpose(out[:, c * P:(c + 1) * P], CQ[:, t, c:QR:3], ident[:])
                        last.then_inc(bank_filled, 1)
                    emptied_now(pe, ("cqT", NT - 1))
                    attention(1)
                project(layer)
                router(layer)
                assign(layer)
                pairs(layer)
                every_expert(layer)

        @block.scalar
        def _(act):
            step = [0]
            given = [0]

            def link(ins):
                step[0] += 1
                ins.then_inc(a_step, 1)
                act.wait_ge(a_step, step[0])

            def go():
                given[0] += 1
                act.wait_ge(to_act, given[0])

            def done(ins):
                ins.then_inc(from_act, 1)

            def emptied_by_me(ins):
                ins.then_inc(emptied["a"], 1)

            nc.scalar.preload_act_table_set("natural_log_exp_and_others")

            def norm():
                for t in range(NT):
                    go()
                    link(nc.scalar.activation(MIX[:, t, :], X[:, t, :], ACT.Square, scale=D ** -0.5, accum_out=small[:, t:t + 1]))
                    link(nc.scalar.activation(small[:, 4 + t:5 + t], small[:, t:t + 1], ACT.Ln, bias=small[:, 62:63]))
                    done(nc.scalar.activation(small[:, 8 + t:9 + t], small[:, 4 + t:5 + t], ACT.Exp, scale=-0.5))

            def to_features(kind, layer):
                for t in range(NT):
                    b = filled(act, (kind, layer, t, 0))
                    emptied_by_me(nc.scalar.activation(hT[:, 0:4, t * P:(t + 1) * P],
                                                       b[:, :].rearrange("p (c n) -> p c n", c=4), ACT.Copy))

            def values(first, end):
                for kt in range(first, end):
                    for k in range(2):
                        bk = filled(act, ("val", kt, k))
                        emptied_by_me(nc.scalar.activation(VAL[:, kt, k * 512:(k + 1) * 512], bk[:, :], ACT.Copy))

            def attention(layer):
                groups = attention_groups(layer)
                scale = 0.125 if layer == 0 else 96 ** -0.5

                def exps(n):
                    g, t = groups[n]
                    nk = len(key_tiles(t)) * P
                    prob = (P0 if layer == 0 else P1)[n % 2]
                    pr = prob.rearrange("p h k -> p (h k)")[:, 0:4 * nk].rearrange("p (h k) -> p h k", h=4)
                    go()
                    if n >= 2:
                        gp, tp = groups[n - 2]
                        act.wait_ge(bank_filled, number[("pT", layer, n - 2, len(key_tiles(tp)) - 1)] + 1)
                    nb = smallp[:, n % 3, 0:4]
                    rs = smallp[:, n % 3, 4:8]
                    if layer == 0:
                        nc.scalar.activation(smallp[:, n % 3, 12:16], smallp[:, n % 3, 8:12], ACT.Exp)
                    share = score_heads(layer, t)
                    for h in range(4):
                        i = [h in hs for hs in share].index(True)
                        j = share[i].index(h)
                        b = banks[number[("score", layer, n, i)] % BANKS]
                        src = b[:, j * nk:(j + 1) * nk]
                        ins = nc.scalar.activation(pr[:, h, :], src, ACT.Exp, bias=nb[:, h:h + 1], scale=scale,
                                                   accum_out=rs[:, h:h + 1])
                        if h == share[i][-1]:
                            emptied_by_me(ins)

                if layer == 1:
                    values(2, 4)
                exps(0)
                for n, (g, t) in enumerate(groups):
                    if n + 1 < len(groups):
                        exps(n + 1)
                    pt = (PT0 if layer == 0 else PT1)
                    b = filled(act, ("pT", layer, n, 0))
                    if n >= len(pt):
                        act.wait_ge(bank_filled, number[("pv", layer, n - len(pt))] + 1)
                    emptied_by_me(nc.scalar.activation(pt[n % len(pt)][:, 0, :], b[:, :], ACT.Copy))

            def pairs(layer):
                B = PAIRS * layer

                def gate_exp(i, q):
                    act.wait_ge(gu_filled, B + i + 1)
                    at_least(act, act_made, B + i - 1)
                    nc.scalar.activation(GE[q], banks[2 + q][:, 0:FF], ACT.Silu).then_inc(gate_ready, 1)

                def copy_y(i, q):
                    act.wait_ge(y_filled, B + i + 1)
                    at_least(act, y_out[q], 32 * HALF * layer + 16 * (i - q))
                    nc.scalar.activation(YS[q][:, 512:1024], banks[6][:, :], ACT.Copy).then_inc(y_copied["a"], 1)

                def copy_x(i, q):
                    act.wait_ge(xt_filled, B + i + 1)
                    at_least(act, gu_filled, B + i - 1)
                    nc.scalar.activation(XGT[q][:, 0:4, :], banks[0][:, :].rearrange("p (c n) -> p c n", c=4), ACT.Copy)\
                        .then_inc(xt_ready["a"], 1)

                def copy_act(i, q):
                    act.wait_ge(actt_filled, B + i + 1)
                    at_least(act, y_filled, B + i - 1)
                    nc.scalar.activation(ACTT[q], banks[4][:, 0:2 * P].rearrange("p (f n) -> p f n", f=2), ACT.Copy)\
                        .then_inc(actt_ready, 1)

                def step(i, q):
                    gate_exp(i, q)
                    copy_y(i - 1, 1 - q)
                    copy_x(i + 1, 1 - q)
                    copy_act(i, q)

                copy_x(0, 0)
                gate_exp(0, 0)
                copy_x(1, 1)
                copy_act(0, 0)
                over_pairs(act, step)
                gate_exp(PAIRS - 1, 1)
                copy_y(PAIRS - 2, 0)
                copy_act(PAIRS - 1, 1)
                copy_y(PAIRS - 1, 1)

            def every_expert(layer):
                F = fb[layer]
                act.wait_ge(pairs_over, layer + 1)
                with act.If(overflow(act)):
                    with act.Fori(0, EXPERTS // 2) as i:
                        for q in range(2):
                            for f in range(2):
                                act.wait_ge(F["gu_done"], 2 * q + f + 1 + 4 * i)
                                act.wait_ge(F["act_ready"], 2 * q + f + 1 + 4 * i)
                                nc.scalar.activation(EE[:, f, :], banks[f][:, 0:TOK], ACT.Silu)\
                                    .then_inc(F["gate_done"], 1)

            act.wait_ge(cond_in, 32)
            done(nc.scalar.activation(cond[:], cond2[:], ACT.Exp, scale=-1.0))
            go()
            done(nc.scalar.activation(lbs[:, 0, :, :], lbs[:, 1, :, :], ACT.Exp))
            go()
            nc.scalar.activation(lbs[:, 3, :, :], lbs[:, 2, :, :], ACT.Ln, scale=float(2.0 ** 60))
            done(nc.scalar.activation(lbs[:, 4, :, :], lbs[:, 1, :, :], ACT.Ln, scale=-1.0, bias=1.0))
            for layer in range(2):
                norm()
                to_features("hT", layer)
                if layer == 0:
                    for b in (1, 2):
                        for h in range(GH):
                            bk = filled(act, ("qff", b, h))
                            emptied_by_me(nc.scalar.activation(LF[:, b - 1, h * TOK:(h + 1) * TOK], bk[:, 0:TOK], ACT.Copy))
                        emptied_now(act, ("qff", b, GH - 1))
                        link(nc.scalar.activation(TD[b - 1], LF[:, b - 1, :], ACT.Abs))
                        link(nc.scalar.activation(TD[b - 1], TD[b - 1], ACT.Exp, scale=-1.0))
                        done(nc.scalar.activation(TD[b - 1], TD[b - 1], ACT.Ln, bias=1.0))
                    for d in range(2):
                        go()
                        link(nc.scalar.activation(TD[d], TD[d], ACT.Abs))
                        link(nc.scalar.activation(TD[d], TD[d], ACT.Exp, scale=-1.0))
                        done(nc.scalar.activation(TD[d], TD[d], ACT.Ln, bias=1.0))
                    for d in range(2):
                        go()
                        done(nc.scalar.activation(KK[:, d, :], LF[:, d, :], ACT.Exp))
                    for h in range(GH):
                        bk = filled(act, ("qff", 0, h))
                        emptied_by_me(nc.scalar.activation(QH[:, h, :], bk[:, 0:TOK], ACT.Silu))
                    for b in range(2):
                        for t in range(NT):
                            bk = filled(act, ("qkv", b, t))
                            w = 512 if b == 0 else 256
                            emptied_by_me(nc.scalar.activation(QKVt[:, t, 512 * b:512 * b + w], bk[:, 0:w], ACT.Copy))
                    for b in range(2):
                        for t in range(NT):
                            bk = filled(act, ("vg", b, t))
                            emptied_by_me(nc.scalar.activation((VV, GG)[b][:, t, :], bk[:, :], ACT.Silu if b else ACT.Copy))
                    nc.scalar.preload_act_table_set("natural_log_exp_and_others")
                    attention(0)
                    def exponents(lv):
                        go()
                        u = state_update(lv)
                        if u is not None:
                            nc.scalar.activation(KDEC[u % 2], KDEC[u % 2], ACT.Exp)
                            if u >= 2:
                                nc.scalar.activation(smallp[:, u - 2, 0:4], smallp[:, u - 2, 0:4], ACT.Exp)
                        if lv == 5:
                            for d in range(2):
                                nc.scalar.activation(QI[d], QI[d], ACT.Exp)
                        done(nc.scalar.activation(LEK[lv % 2], LEK[lv % 2], ACT.Exp))

                    exponents(0)
                    for lv in range(len(LEVELS)):
                        if lv + 1 < len(LEVELS):
                            exponents(lv + 1)
                        u = state_update(lv)
                        if u is not None:
                            bk = filled(act, ("kdT", u))
                            if u:
                                act.wait_ge(bank_filled, number[("state", u - 1)] + 1)
                            emptied_by_me(nc.scalar.activation(KDT, bk[:, :], ACT.Copy))
                    for t in range(NT):
                        bk = filled(act, ("o", t))
                        emptied_by_me(nc.scalar.activation(OB[:, t, :], bk[:, :], ACT.Copy))
                    for t in range(NT):
                        go()
                        sq, ln, rs = (small[:, at + 4 * t:at + 4 * t + 4] for at in (16, 32, 48))
                        link(nc.scalar.activation(ln, sq, ACT.Ln, bias=small[:, 62:63], scale=1.0 / P))
                        done(nc.scalar.activation(rs, ln, ACT.Exp, scale=-0.5))
                else:
                    for b in (1, 0):
                        for t in range(NT):
                            bk = filled(act, ("dqkv", b, t))
                            lo, w = (0, QR) if b == 0 else (QR, KVR + RD)
                            emptied_by_me(nc.scalar.activation(CQ[:, t, lo:lo + w], bk[:, 0:w], ACT.Copy))
                        go()
                        sq, ln, rs = (small[:, at + 3 * b:at + 3 * b + 3] for at in (16, 32, 48))
                        link(nc.scalar.activation(ln, sq, ACT.Ln, bias=small[:, 62:63]))
                        done(nc.scalar.activation(rs, ln, ACT.Exp, scale=-0.5))
                    values(0, 2)
                    attention(1)
                if layer == 0:
                    act.wait_ge(stored, 16 * 4)
                to_features("mixT", layer)
                norm()
                to_features("h2T", layer)
                go()
                done(nc.scalar.activation(RT[:, 128:140], RT[:, 128:140], ACT.Exp))
                go()
                done(nc.scalar.activation(RT[:, 256:280], RT[:, 256:280], ACT.Exp))
                pairs(layer)
                every_expert(layer)
                nc.scalar.preload_act_table_set("natural_log_exp_and_others")
            norm()

        @block.vector
        def _(dve):
            v = nc.vector
            step = [0]
            waited = [0]

            def link(ins):
                step[0] += 1
                ins.then_inc(v_step, 1)
                dve.wait_ge(v_step, step[0])

            def give(ins):
                ins.then_inc(to_act, 1)

            def get():
                waited[0] += 1
                dve.wait_ge(from_act, waited[0])

            fed = [0]

            def feed(ins):
                fed[0] += 1
                ins.then_inc(to_pe, 1)

            def emptied_by_me(ins):
                ins.then_inc(emptied["v"], 1)

            def norms():
                for t in range(NT):
                    dve.sem_inc(to_act, 1)

            def scales(consts, nth):
                dve.wait_ge(mod_ss_in, 32 * nth)
                dve.wait_ge(consts_in, consts)
                for g in range(2):
                    link(v.scalar_tensor_tensor(out=MOD[:, g, 1, :], in0=MOD[:, g, 1, :], scalar=1.0, in1=normw[:],
                                                op0=ALU.add, op1=ALU.mult))

            def adaln(kind, layer):
                for t in range(NT):
                    g = 0 if t == 0 else 1
                    get()
                    link(v.scalar_tensor_tensor(out=MIX[:, t, :], in0=X[:, t, :], scalar=small[:, 8 + t:9 + t],
                                                in1=MOD[:, g, 1, :], op0=ALU.mult, op1=ALU.mult))
                    feed(v.tensor_tensor(MIX[:, t, :], MIX[:, t, :], MOD[:, g, 0, :], ALU.add))
                dve.wait_ge(to_pe, fed[0])
                if kind == "h2T":
                    dve.sem_inc(h2_made, 1)
                dve.sem_inc(pool_free, 1)
                to_features(kind, layer)

            def to_features(kind, layer):
                for t in range(NT):
                    b = filled(dve, (kind, layer, t, 1))
                    emptied_by_me(v.tensor_copy(hT[:, 4:8, t * P:(t + 1) * P], b[:, :].rearrange("p (c n) -> p c n", c=4)))

            def attention(layer):
                groups = attention_groups(layer)
                scale = 0.125 if layer == 0 else 96 ** -0.5

                def maxima(n):
                    g, t = groups[n]
                    nk = len(key_tiles(t)) * P
                    sp_ = smallp[:, n % 3]
                    share = score_heads(layer, t)
                    for i, hs in enumerate(share):
                        b = filled(dve, ("score", layer, n, i))
                        link(v.tensor_reduce(out=sp_[:, 16 + i:20:len(share)],
                                             in_=b[:, 0:len(hs) * nk].rearrange("p (h k) -> p h k", k=nk), axis=AX, op=ALU.max))
                    if layer == 0:
                        sk = sink[:, 4 * g:4 * g + 4]
                        link(v.scalar_tensor_tensor(out=sp_[:, 16:20], in0=sp_[:, 16:20], scalar=scale, in1=sk,
                                                    op0=ALU.mult, op1=ALU.max))
                        link(v.tensor_tensor(sp_[:, 8:12], sk, sp_[:, 16:20], ALU.subtract))
                        give(v.tensor_scalar(sp_[:, 0:4], sp_[:, 16:20], -1.0, None, ALU.mult))
                    else:
                        give(v.tensor_scalar(sp_[:, 0:4], sp_[:, 16:20], -scale, None, ALU.mult))

                def results(n):
                    g, t = groups[n]
                    sp_ = smallp[:, n % 3]
                    emptied_now(dve, ("score", layer, n, len(score_heads(layer, t)) - 1))
                    if layer == 0:
                        link(v.tensor_tensor(sp_[:, 4:8], sp_[:, 4:8], sp_[:, 12:16], ALU.add))
                    link(v.reciprocal(sp_[:, 20:24], sp_[:, 4:8]))
                    b = filled(dve, ("pv", layer, n))
                    emptied_by_me(v.tensor_tensor(MIX[:, t, 256 * g:256 * g + 256].rearrange("p (h e) -> p h e", h=4),
                                                  b[:, 0:256].rearrange("p (h e) -> p h e", h=4),
                                                  sp_[:, 20:24].unsqueeze(2).to_broadcast([P, 4, 64]), ALU.mult))
                    if layer == 0 and n in MOD_IN_ATTENTION:
                        modulation(MOD_IN_ATTENTION[n])

                if layer == 1:
                    queries_keys(0)
                maxima(0)
                for n, (g, t) in enumerate(groups):
                    if n + 1 < len(groups):
                        maxima(n + 1)
                    if layer == 1 and t == 0 and g < 3:
                        queries_keys(g + 1)
                    if layer == 0 and n == 2:
                        emptied_now(dve, ("vg", 1, 2))
                        gg = GG.rearrange("p t (h n) -> p (t h) n", h=GH)
                        v.tensor_tensor(gg, gg, gnw[:].unsqueeze(1).to_broadcast([P, 12, P]), ALU.mult)
                    if layer == 0 and n == 4:
                        qh = QH.rearrange("p h t -> p (h t)")
                        link(v.tensor_scalar(qh, qh, HGRN_SCALE, None, ALU.mult))
                    pt = (PT0 if layer == 0 else PT1)
                    for i in range(1, len(key_tiles(t))):
                        b = filled(dve, ("pT", layer, n, i))
                        if n >= len(pt):
                            dve.wait_ge(bank_filled, number[("pv", layer, n - len(pt))] + 1)
                        emptied_by_me(v.tensor_copy(pt[n % len(pt)][:, i, :], b[:, :]))
                    if n:
                        results(n - 1)
                results(len(groups) - 1)

            def queries_keys(g):
                uq = block_view(("uq", g // 2)).rearrange("p c (h n) -> p c h n", h=8)
                hs = slice(4 * (g % 2), 4 * (g % 2) + 4)
                if g % 2 == 0:
                    weights_arrived(dve, ("uq", g // 2))
                wq = WQB[:].rearrange("p c (h n) -> p c h n", h=4)
                if g == 0:
                    dve.wait_ge(stored, 16 * 6)
                if g:
                    dve.wait_ge(bank_filled, number[("qT1", g - 1, 3)] + 1)
                for c in range(3):
                    v.tensor_copy(wq[:, c, :, 0:96], uq[:, c, hs, :])
                    for half in range(4):
                        to = 96 + 8 * half
                        fr = 64 + 8 * (half ^ 1)
                        last = v.tensor_copy(wq[:, c, :, to:to + 8], uq[:, c, hs, fr:fr + 8])
                feed(last)
                K, Q = K1[g % 2], Q1[g % 2]
                if g >= 2:
                    dve.wait_ge(bank_filled, number[("score", 1, 3 * (g - 2) + 2, 3)] + 1)
                for i in range(2):
                    b = filled(dve, ("kT", g, i))
                    v.tensor_copy(K[0:64, 2 * i, :], b[0:64, :])
                    emptied_by_me(v.tensor_copy(K[0:64, 2 * i + 1, :], b[64:128, :]))
                for i in range(4):
                    b = filled(dve, ("qT1", g, i))
                    v.tensor_copy(Q[0:64, i, :], b[0:64, 0:TOK])
                    v.tensor_copy(Q[64:96, i, 0:P], b[64:96, 0:P])
                    v.tensor_tensor(Q[64:96, i, P:TOK], b[64:96, P:TOK], ropeT[64:96, :], ALU.mult)
                    link(v.tensor_tensor(SQ[64:96, 0:2 * P], b[96:128, P:TOK], ropeT[96:128, :], ALU.mult))
                    emptied_by_me(v.tensor_tensor(Q[64:96, i, P:TOK], Q[64:96, i, P:TOK], SQ[64:96, 0:2 * P], ALU.add))
                    emptied_now(dve, ("qT1", g, i))
                feed(v.tensor_copy(K[64:96, :, :], KRT[64:96, :].unsqueeze(1).to_broadcast([32, 4, KEYT * P])))

            def residual(layer):
                dve.wait_ge(mod_gate_in, 32 * (2 * layer + 1))
                for n in range(2):
                    for t in range(NT):
                        g = 0 if t == 0 else 1
                        cs = slice(n * 512, (n + 1) * 512)
                        b = filled(dve, ("proj", layer, n, t))
                        emptied_by_me(v.tensor_tensor(MIX[:, t, cs], b[:, :], MOD[:, g, 2, cs], ALU.mult))
                        emptied_now(dve, ("proj", layer, n, t))
                        link(v.tensor_tensor(X[:, t, cs], X[:, t, cs], MIX[:, t, cs], ALU.add))
                        if n:
                            dve.sem_inc(to_act, 1)

            def first_hot(out, val, mx, tmp, n):
                io = iota[:, 0:n].unsqueeze(1).to_broadcast([P, NT, n])
                io64 = iota[:, 8:8 + n].unsqueeze(1).to_broadcast([P, NT, n])
                link(v.tensor_tensor(tmp, val, mx.to_broadcast([P, NT, n]), ALU.is_ge))
                link(v.scalar_tensor_tensor(out=tmp, in0=tmp, scalar=-64.0, in1=io64, op0=ALU.mult, op1=ALU.add))
                link(v.tensor_reduce(out=RT[:, 400:403], in_=tmp, axis=AX, op=ALU.min))
                link(v.tensor_tensor(out, RT[:, 400:403].unsqueeze(2).to_broadcast([P, NT, n]), io, ALU.is_equal))

            def route(layer):
                def cols(at, n):
                    return RT[:, at:at + NT * n].rearrange("p (t n) -> p t n", t=NT)

                L = cols(0, 36)
                b = filled(dve, ("router", layer))
                dve.wait_ge(router_in, 16 * 7 * (layer + 1))
                emptied_by_me(v.tensor_tensor(L, b[:, 0:108].rearrange("p (t n) -> p t n", t=NT),
                                              BR[:].unsqueeze(1).to_broadcast([P, NT, 36]), ALU.add))
                emptied_now(dve, ("router", layer))
                GL = L[:, :, 0:4]
                gm, gsum = cols(112, 1), cols(116, 1)
                eg = cols(128, 4)
                link(v.tensor_reduce(out=gm, in_=GL, axis=AX, op=ALU.max))
                give(v.tensor_tensor(eg, GL, gm.to_broadcast([P, NT, 4]), ALU.subtract))
                goh, tmp = cols(144, 4), cols(160, 8)
                first_hot(goh, GL, gm, tmp[:, :, 0:4], 4)
                prod = RT[:, 300:396].rearrange("p (t g e) -> p t g e", t=NT, g=4)
                for t in range(NT):
                    link(v.tensor_tensor(prod[:, t], L[:, t, 4:36].rearrange("p (g e) -> p g e", g=4),
                                         goh[:, t].unsqueeze(2).to_broadcast([P, 4, 8]), ALU.mult))
                esel = cols(224, 8)
                link(v.tensor_reduce(out=esel, in_=prod.rearrange("p t g e -> p t e g"), axis=AX, op=ALU.add))
                m1 = cols(120, 1)
                link(v.tensor_reduce(out=m1, in_=esel, axis=AX, op=ALU.max))
                e8 = cols(256, 8)
                get()
                give(v.tensor_tensor(e8, esel, m1.to_broadcast([P, NT, 8]), ALU.subtract))
                link(v.tensor_reduce(out=gsum, in_=eg, axis=AX, op=ALU.add))
                link(v.reciprocal(gsum, gsum))
                o1, o2 = cols(184, 8), cols(404 - 0, 8)
                first_hot(o1, esel, m1, tmp, 8)
                link(v.scalar_tensor_tensor(out=esel, in0=o1, scalar=-1e30, in1=esel, op0=ALU.mult, op1=ALU.add))
                link(v.tensor_reduce(out=m1, in_=esel, axis=AX, op=ALU.max))
                first_hot(o2, esel, m1, tmp, 8)
                get()
                o12 = tmp
                link(v.tensor_tensor(o12, o1, o2, ALU.add))
                link(v.tensor_tensor(e8, e8, o12, ALU.mult))
                den = cols(124, 1)
                link(v.tensor_reduce(out=den, in_=e8, axis=AX, op=ALU.add))
                link(v.reciprocal(den, den))
                link(v.tensor_tensor(den, den, gsum, ALU.mult))
                link(v.tensor_tensor(e8, e8, den.to_broadcast([P, NT, 8]), ALU.mult))
                for t in range(NT):
                    last = v.tensor_tensor(COMB[:, t, :].rearrange("p (g e) -> p g e", g=4),
                                           goh[:, t].unsqueeze(2).to_broadcast([P, 4, 8]),
                                           e8[:, t].unsqueeze(1).to_broadcast([P, 4, 8]), ALU.mult)
                    for j, o in enumerate((o1, o2)):
                        last = v.tensor_tensor(S12[:, j * NT + t, :].rearrange("p (g e) -> p g e", g=4),
                                               goh[:, t].unsqueeze(2).to_broadcast([P, 4, 8]),
                                               o[:, t].unsqueeze(1).to_broadcast([P, 4, 8]), ALU.mult)
                link(last)
                feed(v.tensor_tensor(SEL, S12[:, 0:NT, :], S12[:, NT:, :], ALU.add))
                b = filled(dve, ("pos", layer))
                v.tensor_copy(POS, b[:, 0:96].rearrange("p (t n) -> p t n", t=NT))
                link(v.tensor_reduce(out=FULLF, in_=b[:, 96:128], axis=AX, op=ALU.max))
                emptied_by_me(v.tensor_copy(FULL, FULLF))
                emptied_now(dve, ("pos", layer))
                link(v.tensor_scalar(OVER, POS, float(CAP), None, ALU.is_ge))
                link(v.tensor_scalar(SEL2, OVER, -1.0, 1.0, ALU.mult, ALU.add))
                link(v.tensor_tensor(OVER, OVER, COMB, ALU.mult))
                link(v.tensor_tensor(POS, POS, ktab[:, P + PAIRS:P + PAIRS + EXPERTS].unsqueeze(1).to_broadcast([P, NT, EXPERTS]), ALU.add))
                higher = ktab[:, P + PAIRS + EXPERTS:P + PAIRS + 2 * EXPERTS].unsqueeze(1).to_broadcast([P, NT, EXPERTS])
                for row, val in enumerate((POS, higher, SEL2, COMB)):
                    for j in range(2):
                        last = v.tensor_tensor(PROD4[:, row, j * 3 * EXPERTS:(j + 1) * 3 * EXPERTS].rearrange("p (t e) -> p t e", t=NT),
                                               S12[:, j * NT:(j + 1) * NT, :], val, ALU.mult)
                link(last)
                link(v.tensor_reduce(out=LOHI[:, 0:4, :], in_=PROD4.rearrange("p r (k e) -> p r k e", e=EXPERTS), axis=AX, op=ALU.add))
                ok = LOHI[:, 2, :]
                v.tensor_tensor(LOHI[:, 3, :], LOHI[:, 3, :], ok, ALU.mult)
                for j in range(2):
                    v.tensor_tensor(LOHI[:, 5, j * NT:(j + 1) * NT], ktab[:, P + PAIRS + 2 * EXPERTS:], ok[:, 0:NT] if j == 0 else ok[:, NT:], ALU.mult)
                link(v.scalar_tensor_tensor(out=LOHI[:, 4, :], in0=LOHI[:, 1, :], scalar=float(SLOTS), in1=LOHI[:, 0, :], op0=ALU.mult, op1=ALU.add))
                link(v.tensor_tensor(LOHI[:, 4, :], LOHI[:, 4, :], ok, ALU.mult))
                v.tensor_copy(ROWI, LOHI[:, 4, :])
                for j in range(2 * NT):
                    v.tensor_scalar(OHLO[:, j, :], ktab[:, 0:P], LOHI[:, 0, j:j + 1], None, ALU.is_equal)
                    last = v.tensor_scalar(OHHI[:, j, :], ktab[:, P:P + PAIRS], LOHI[:, 1, j:j + 1], LOHI[:, 5, j:j + 1],
                                           ALU.is_equal, ALU.mult)
                feed(last)
                b = filled(dve, ("slot", layer))
                link(v.tensor_scalar(PROD[:, 0, 0:PAIRS], b[:, 0:PAIRS], 0.0, 4096.0, ALU.is_equal, ALU.mult))
                link(v.scalar_tensor_tensor(out=PROD[:, 0, 0:PAIRS], in0=b[:, 0:PAIRS], scalar=-1.0, in1=PROD[:, 0, 0:PAIRS],
                                            op0=ALU.add, op1=ALU.add))
                v.tensor_copy(IDX, PROD[:, 0, 0:PAIRS]).then_inc(idx_ready, 1)
                dve.wait_ge(idx_ready, layer + 1)
                dve.sem_inc(emptied["v"], 1)

            def pairs(layer):
                B = PAIRS * layer

                def activate(i, q):
                    dve.wait_ge(gate_ready, B + i + 1)
                    at_least(dve, actt_filled, B + i - 1)
                    v.tensor_tensor(ACTV[q], banks[2 + q][:, FF:2 * FF], GE[q], ALU.mult).then_inc(act_made, 1)

                def copy_y(i, q):
                    dve.wait_ge(y_filled, B + i + 1)
                    at_least(dve, y_out[q], 32 * HALF * layer + 16 * (i - q))
                    v.tensor_copy(YS[q][:, 0:512], banks[5][:, :]).then_inc(y_copied["v"], 1)

                def copy_x(i, q):
                    dve.wait_ge(xt_filled, B + i + 1)
                    at_least(dve, gu_filled, B + i - 1)
                    v.tensor_copy(XGT[q][:, 4:8, :], banks[1][:, :].rearrange("p (c n) -> p c n", c=4)).then_inc(xt_ready["v"], 1)

                def step(i, q):
                    activate(i, q)
                    copy_y(i - 1, 1 - q)
                    copy_x(i + 1, 1 - q)

                copy_x(0, 0)
                activate(0, 0)
                copy_x(1, 1)
                over_pairs(dve, step)
                activate(PAIRS - 1, 1)
                copy_y(PAIRS - 2, 0)
                copy_y(PAIRS - 1, 1)
                dve.wait_ge(y_copied["a"], B + PAIRS)
                dve.sem_inc(pairs_over, 1)

            def combine(layer):
                if layer == 0:
                    scales(CONSTS + 32, 3)
                dve.wait_ge(mod_gate_in, 32 * (2 * layer + 2))
                for t in range(NT):
                    dve.wait_ge(y_back[t], 32 * (layer + 1))
                    y1, y2 = YG[:, t, :], YG[:, NT + t, :]
                    link(v.tensor_scalar(y1, y1, LOHI[:, 3, t:t + 1], None, ALU.mult))
                    link(v.scalar_tensor_tensor(out=y1, in0=y2, scalar=LOHI[:, 3, NT + t:NT + t + 1], in1=y1, op0=ALU.mult, op1=ALU.add))
                    link(v.tensor_tensor(y1, y1, MOD[:, 0 if t == 0 else 1, 2, :], ALU.mult))
                    link(v.tensor_tensor(X[:, t, :], X[:, t, :], y1, ALU.add))
                    dve.sem_inc(to_act, 1)

            def every_expert(layer):
                F = fb[layer]
                chained = [0]

                def chain(ins):
                    chained[0] += 1
                    ins.then_inc(F["chain"], 1)
                    dve.wait_ge(F["chain"], chained[0])

                dve.wait_ge(mod_gate_in, 32 * (2 * layer + 2))
                with dve.If(overflow(dve)):
                    chain(v.memset(YACC, 0.0))
                    dve.sem_inc(F["y_emptied"], 4)
                    dve.sem_inc(F["act_ready"], 2)
                    with dve.Fori(0, EXPERTS // 2) as i:
                        for q in range(2):
                            for f in range(2):
                                n = 2 * q + f
                                dve.wait_ge(F["gate_done"], n + 1 + 4 * i)
                                v.tensor_tensor(AT[:, q, f, :], banks[2 + f][:, 0:TOK], EE[:, f, :], ALU.mult)\
                                    .then_inc(F["act_ready"], 1)
                            for j in range(6):
                                h, t = divmod(j, NT)
                                k = 6 * q + j
                                dve.wait_ge(F["y_done"], k + 1 + 12 * i)
                                ys = YACC[:, t, h * 512:(h + 1) * 512]
                                dve.wait_ge(F["y_emptied"], 4 + k + 12 * i)
                                v.scalar_tensor_tensor(out=ys, in0=banks[4 + k % 4][:, :], scalar=OVER[:, t, bass.ds(2 * i + q, 1)],
                                                       in1=ys, op0=ALU.mult, op1=ALU.add).then_inc(F["y_emptied"], 1)
                    dve.wait_ge(F["y_emptied"], 6 * EXPERTS + 4)
                    for t in range(NT):
                        chain(v.tensor_tensor(YACC[:, t, :], YACC[:, t, :], MOD[:, 0 if t == 0 else 1, 2, :], ALU.mult))
                        chain(v.tensor_tensor(X[:, t, :], X[:, t, :], YACC[:, t, :], ALU.add))
                dve.sem_inc(experts_over, 1)

            def modulation(m):
                bk = filled(dve, ("mod", m))
                dve.wait_ge(modbias_in[m % 2], 32 * (m // 2 + 1))
                if m >= 2:
                    dve.wait_ge(modrow_out[m % 2], 32 * (m // 2))
                for j in range(4):
                    rs = slice(32 * j, 32 * j + 2)
                    ins = v.tensor_tensor(modrow[rs, m % 2, :], bk[rs, 0:P], modbias[rs, m % 2, :], ALU.add)
                ins.then_inc(modrow_ready, 1)
                dve.wait_ge(modrow_ready, m + 1)
                dve.sem_inc(emptied["v"], 1)

            v.memset(small[:, 62:63], EPS)
            for j in range(8):
                v.memset(iota[:, j:j + 1], float(j))
                v.memset(iota[:, 8 + j:9 + j], float(64 + j))
            get()
            link(v.tensor_scalar(cond[:], cond[:], 1.0, None, ALU.add))
            link(v.reciprocal(cond[:], cond[:]))
            v.tensor_tensor(cond[:], cond[:], cond2[:], ALU.mult).then_inc(cond_ready, 1)
            for m in range(MOD_FIRST):
                modulation(m)
            dve.wait_ge(consts_in, CONSTS)
            give(v.tensor_tensor(lbs[:, 1, :, :], lbc[:], lbc[:], ALU.subtract))
            get()
            link(v.reciprocal(lbs[:, 5, :, :], lbs[:, 0, :, :]))
            link(v.tensor_tensor(lbs[:, 0, :, :], lbs[:, 0, :, :], lbs[:, 5, :, :], ALU.mult))
            link(v.tensor_tensor(lbs[:, 1, :, :], lbs[:, 0, :, :], lbs[:, 0, :, :], ALU.subtract))
            link(v.tensor_scalar(lbs[:, 1, :, :], lbs[:, 1, :, :], 0.0, 1.0 - 1e-6, ALU.max, ALU.min))
            give(v.tensor_scalar(lbs[:, 2, :, :], lbs[:, 1, :, :], 1e-30, None, ALU.max))
            get()
            link(v.tensor_scalar(lbs[:, 3, :, :], lbs[:, 3, :, :], -60 * LN2, None, ALU.add))
            dve.wait_ge(tokens_in, 32)
            norms()
            scales(CONSTS, 1)
            for layer in range(2):
                adaln("hT", layer)
                if layer == 0:
                    link(v.memset(RESET, 1.0))
                    link(v.memset(RESET.rearrange("p (n t) -> p n t", t=P)[:, :, 0:1], 0.0))
                    def by_head(x):
                        return x.rearrange("p (h n) -> p h n", h=GH)
                    for d in range(2):
                        A4 = lbs[:, 3, d, :].unsqueeze(2).to_broadcast([P, GH, TOK])
                        C4 = lbs[:, 4, d, :].unsqueeze(2).to_broadcast([P, GH, TOK])
                        get()
                        link(v.scalar_tensor_tensor(out=LF[:, d, :], in0=LF[:, d, :], scalar=0.0, in1=TD[d], op0=ALU.min, op1=ALU.subtract))
                        link(v.tensor_tensor(by_head(LF[:, d, :]), by_head(LF[:, d, :]), C4, ALU.add))
                        give(v.tensor_tensor(by_head(TD[d]), by_head(LF[:, d, :]), A4, ALU.subtract))
                        link(v.tensor_tensor(by_head(LF[:, d, :]), by_head(LF[:, d, :]), A4, ALU.max))
                        modulation(MOD_FIRST + d)
                    for d in range(2):
                        get()
                        give(v.tensor_tensor(LF[:, d, :], LF[:, d, :], TD[d], ALU.add))
                    for d in range(2):
                        get()
                        v.tensor_scalar(KK[:, d, :], KK[:, d, :], -1.0, 1.0, ALU.mult, ALU.add)
                        link(v.tensor_tensor_scan(out=TD[d], data0=RESET, data1=LF[:, d, :], initial=0.0, op0=ALU.mult, op1=ALU.add))
                    v.tensor_copy(LF[:, 0, :], TD[0])
                    link(v.tensor_tensor(LF[:, 1, :], LF[:, 1, :], TD[1], ALU.subtract))
                    b2 = TD[1].rearrange("p (n t) -> p n t", t=P)
                    l2 = LF[:, 1, :].rearrange("p (n t) -> p n t", t=P)
                    link(v.tensor_tensor(l2, l2, b2[:, :, P - 1:P].to_broadcast([P, GH * NT, P]), ALU.add))
                if layer == 0:
                    for n in (2, 3, 4):
                        modulation(MOD_FIRST + n)
                    emptied_now(dve, ("qkv", 1, 2))
                    dve.wait_ge(tables_in, 16 * 9)
                    dve.wait_ge(l1params_in, 48)
                    for t in (1, 2):
                        x = QKVt[:, t, 0:640].rearrange("p (h r) -> p h r", r=HD)
                        link(v.tensor_tensor(ROT[:, 0, :].rearrange("p (h r) -> p h r", r=HD), x,
                                             rope_cs[:, t - 1, 0].unsqueeze(1).to_broadcast([P, 10, HD]), ALU.mult))
                        for half in range(4):
                            o = half ^ 1
                            r = ROT[:, 1, :].rearrange("p (h r) -> p h r", r=HD)
                            link(v.tensor_tensor(r[:, :, 16 * half:16 * half + 16], x[:, :, 16 * o:16 * o + 16],
                                                 rope_cs[:, t - 1, 1, 16 * half:16 * half + 16].unsqueeze(1).to_broadcast([P, 10, 16]),
                                                 ALU.mult))
                        link(v.tensor_tensor(QKVt[:, t, 0:640], ROT[:, 0, :], ROT[:, 1, :], ALU.add))
                    for kt in (0, 2, 3):
                        t = 0 if kt == 0 else kt - 1
                        for dup in range(2):
                            last = v.tensor_copy(KD[:, kt, :, dup * HD:dup * HD + HD],
                                                 QKVt[:, t, 512:640].rearrange("p (g d) -> p g d", g=2))
                    feed(last)
                    for n in (5, 6):
                        modulation(MOD_FIRST + n)
                    for t in range(NT):
                        b = filled(dve, ("qT", t))
                        emptied_by_me(v.tensor_copy(QT[:, :, t * P:(t + 1) * P], b[:, :].rearrange("p (j n) -> p j n", j=4)))
                    for k in range(2):
                        b = filled(dve, ("kT0", k))
                        for j in range(2):
                            ins = v.tensor_copy(KT[:, :, (2 * k + j) * P:(2 * k + j + 1) * P],
                                                b[:, 2 * j * P:(2 * j + 2) * P].rearrange("p (g n) -> p g n", g=2))
                        emptied_by_me(ins)
                    attention(0)
                    emptied_now(dve, ("pv", 0, 5))
                    emptied_now(dve, ("vg", 1, 2))
                    dve.sem_inc(out_ready, 1)
                    dve.wait_ge(stored, 32)
                    QHf = QH.rearrange("p h t -> p (h t)")

                    def exponents(lv):
                        half = LEVELS[lv]
                        n = GH * TOK // (2 * half)
                        w = 2 * half
                        fwd, bwd = (LF[:, d, :].rearrange("p (n w) -> p n w", w=w) for d in range(2))
                        ks, qs = (x[lv % 2].rearrange("p (n w) -> p n w", w=w) for x in (LK, LE))
                        left, right = slice(0, half), slice(half, w)
                        fref = fwd[:, :, half - 1:half].to_broadcast([P, n, half])
                        bref = bwd[:, :, half:half + 1].to_broadcast([P, n, half])
                        if lv >= 2:
                            dve.wait_ge(bank_filled, number[("lvl", lv - 2, NT - 1)] + 1)
                        v.tensor_tensor(ks[:, :, left], fref, fwd[:, :, left], ALU.subtract)
                        v.tensor_tensor(ks[:, :, right], bref, bwd[:, :, right], ALU.subtract)
                        v.tensor_tensor(qs[:, :, left], bwd[:, :, left], bref, ALU.subtract)
                        u = state_update(lv)
                        if u is not None:
                            d, t = UNITS[u]
                            if u >= 2:
                                dve.wait_ge(bank_filled, number[("kdT", u - 2)] + 1)
                            b3 = LF[:, d, :].rearrange("p (h n) -> p h n", h=GH)[:, :, t * P:(t + 1) * P]
                            end = b3[:, :, P - 1:P] if d == 0 else b3[:, :, 0:1]
                            v.tensor_tensor(KDEC[u % 2].rearrange("p (h n) -> p h n", h=GH),
                                            end.to_broadcast([P, GH, P]), b3, ALU.subtract)
                            if u >= 2:
                                v.tensor_copy(smallp[:, u - 2, 0:4].unsqueeze(2), end)
                        if lv == 5:
                            for d in range(2):
                                b3 = LF[:, d, :].rearrange("p (h t n) -> p t h n", h=GH, t=NT)
                                for t in (1, 2):
                                    v.tensor_copy(QI[d][:, t - 1, :].rearrange("p (h n) -> p h n", h=GH), b3[:, t])
                        give(v.tensor_tensor(qs[:, :, right], fwd[:, :, right], fref, ALU.subtract))

                    def drain_level(lv):
                        for t in range(NT):
                            b = filled(dve, ("lvl", lv, t))
                            emptied_by_me(v.copy_predicated(ATT[:, t], MASK[:, lv].unsqueeze(1).to_broadcast([P, GH, P]),
                                                            b[:, :].rearrange("p (h n) -> p h n", h=GH)))
                        for m in mod_after_level(lv):
                            modulation(m)
                        u = state_update(lv)
                        if u is None:
                            return
                        if u >= 2:
                            dve.wait_ge(l1params_in, 80)
                        b = filled(dve, ("state", u))
                        if u < 2:
                            v.tensor_copy(ST[:, 2 + u, :], b[:, :]).then_inc(out_ready, 1)
                            dve.wait_ge(out_ready, 2 + u)
                            dve.sem_inc(emptied["v"], 1)
                            return
                        for h in range(GH):
                            hs = slice(h * P, (h + 1) * P)
                            ins = v.scalar_tensor_tensor(out=ST[:, 2 + u, hs], in0=ST[:, u - 2, hs], scalar=smallp[:, u - 2, h:h + 1],
                                                         in1=b[:, hs], op0=ALU.mult, op1=ALU.add)
                        emptied_by_me(ins)

                    exponents(0)
                    for lv, half in enumerate(LEVELS):
                        if lv + 1 < len(LEVELS):
                            exponents(lv + 1)
                        get()
                        kl, kf, kb = (x.rearrange("p (n w) -> p n w", w=2 * half) for x in (LK[lv % 2], KK[:, 0, :], KK[:, 1, :]))
                        v.tensor_tensor(kl[:, :, 0:half], kl[:, :, 0:half], kf[:, :, 0:half], ALU.mult)
                        v.tensor_tensor(kl[:, :, half:], kl[:, :, half:], kb[:, :, half:], ALU.mult)
                        feed(v.tensor_tensor(LE[lv % 2], LE[lv % 2], QHf, ALU.mult))
                        dve.wait_ge(to_pe, fed[0])
                        u = state_update(lv)
                        if u is not None:
                            d, t = UNITS[u]
                            kd = KDEC[u % 2].rearrange("p (h n) -> p h n", h=GH)
                            feed(v.tensor_tensor(kd, kd, KK[:, d, :].rearrange("p (h n) -> p h n", h=GH)[:, :, t * P:(t + 1) * P],
                                                 ALU.mult))
                        if lv == 5:
                            for d in range(2):
                                for t in (1, 2):
                                    qi = QI[d][:, t - 1, :].rearrange("p (h n) -> p h n", h=GH)
                                    v.tensor_tensor(qi, qi, QH[:, :, t * P:(t + 1) * P], ALU.mult)
                        if lv:
                            drain_level(lv - 1)
                    dve.wait_ge(bank_filled, number[("lvl", len(LEVELS) - 2, NT - 1)] + 1)
                    feed(v.tensor_tensor(LK[1], KK[:, 0, :], KK[:, 1, :], ALU.add))
                    dve.wait_ge(to_pe, fed[0])
                    drain_level(len(LEVELS) - 1)
                    for t in range(NT):
                        emptied_now(dve, ("lvl", len(LEVELS) - 1, t))
                        b = filled(dve, ("diag", t))
                        emptied_by_me(v.copy_predicated(ATT[:, t], MASK[:, 7].unsqueeze(1).to_broadcast([P, GH, P]),
                                                        b[:, :].rearrange("p (h n) -> p h n", h=GH)))
                    def heads(x, t):
                        return x[:, t, :].rearrange("p (h n) -> p h n", h=GH)

                    for t in range(NT):
                        emptied_now(dve, ("o", t))
                        link(v.tensor_tensor(OB2[:, t, :], OB[:, t, :], OB[:, t, :], ALU.mult))
                        give(v.tensor_reduce(out=small[:, 16 + 4 * t:20 + 4 * t], in_=heads(OB2, t), axis=AX, op=ALU.add))
                    for t in range(NT):
                        get()
                        link(v.tensor_tensor(heads(OB, t), heads(OB, t),
                                             small[:, 48 + 4 * t:52 + 4 * t].unsqueeze(2).to_broadcast([P, GH, P]), ALU.mult))
                        feed(v.tensor_tensor(MIX[:, t, 512:1024], OB[:, t, :], GG[:, t, :], ALU.mult))
                else:
                    v.memset(KR, 0.0).then_inc(out_ready, 1)
                    dve.wait_ge(out_ready, 4)

                    def squares(b, lo, n):
                        for t in range(NT):
                            emptied_now(dve, ("dqkv", b, t))
                            link(v.tensor_tensor_reduce(out=SQ[:, 0:n], in0=CQ[:, t, lo:lo + n], in1=CQ[:, t, lo:lo + n],
                                                        scale=1.0 / n, scalar=0.0, op0=ALU.mult, op1=ALU.add,
                                                        accum_out=small[:, 16 + 3 * b + t:17 + 3 * b + t]))
                        dve.sem_inc(to_act, 1)

                    def normalised(b, lo, n):
                        get()
                        for t in range(NT):
                            r = small[:, 48 + 3 * b + t:49 + 3 * b + t]
                            ins = v.scalar_tensor_tensor(out=CQ[:, t, lo:lo + n], in0=CQ[:, t, lo:lo + n], scalar=r,
                                                         in1=qnw[:, lo:lo + n], op0=ALU.mult, op1=ALU.mult)
                        return ins

                    squares(1, QR, KVR)
                    dve.wait_ge(l1params_in, 16 * 9)
                    for t in (1, 2):
                        x = CQ[:, t, QR + KVR:]
                        link(v.tensor_tensor(KR[:, t + 1, 64:96], x, rope32[:, t - 1, 0], ALU.mult))
                        for half in range(4):
                            o = half ^ 1
                            link(v.tensor_tensor(SQ[:, 8 * half:8 * half + 8], x[:, 8 * o:8 * o + 8],
                                                 rope32[:, t - 1, 1, 8 * half:8 * half + 8], ALU.mult))
                        link(v.tensor_tensor(KR[:, t + 1, 64:96], KR[:, t + 1, 64:96], SQ[:, 0:32], ALU.add))
                    link(v.tensor_copy(KR[:, 0, 64:96], CQ[:, 0, QR + KVR:]))
                    normalised(1, QR, KVR).then_inc(out_ready, 1)
                    dve.wait_ge(out_ready, 5)
                    fed[0] += 1
                    dve.sem_inc(to_pe, 1)
                    squares(0, 0, QR)
                    for k in range(2):
                        b = filled(dve, ("ckvT", k))
                        for j in range(2):
                            ins = v.tensor_copy(CKVT[:, :, (2 * k + j) * P:(2 * k + j + 1) * P],
                                                b[:, 2 * j * P:(2 * j + 2) * P].rearrange("p (c n) -> p c n", c=2))
                        emptied_by_me(ins)
                    b = filled(dve, ("krT",))
                    emptied_by_me(v.tensor_copy(KRT[64:96, :], b[64:96, :]))
                    emptied_now(dve, ("krT",))
                    feed(normalised(0, 0, QR))
                    for t in range(NT):
                        b = filled(dve, ("cqT", t))
                        emptied_by_me(v.tensor_copy(CQT[:, :, t * P:(t + 1) * P], b[:, 0:TOK].rearrange("p (c n) -> p c n", c=3)))
                    attention(1)
                    emptied_now(dve, ("pv", 1, 11))
                    for t in range(NT):
                        fed[0] += 1
                        dve.sem_inc(to_pe, 1)
                if layer == 0:
                    dve.wait_ge(stored, 16 * 4)
                to_features("mixT", layer)
                scales(CONSTS + 16 + 32 * layer, 2 * layer + 2)
                residual(layer)
                dve.sem_inc(mod_free, 1)
                adaln("h2T", layer)
                route(layer)
                pairs(layer)
                every_expert(layer)
                combine(layer)
                dve.sem_inc(mod_free, 1)
            dve.wait_ge(consts_in, CONSTS + 64)
            for t in range(NT):
                get()
                ins = v.scalar_tensor_tensor(out=MIX[:, t, :], in0=X[:, t, :], scalar=small[:, 8 + t:9 + t],
                                             in1=normw[:], op0=ALU.mult, op1=ALU.mult)
            ins.then_inc(out_ready, 1)


_SCRATCH = [("h2_dram", (TOK, D)), ("y_dram", (PAIRS, SLOTS, D))]


def _constants():
    import numpy as np
    s, t = np.arange(P)[:, None], np.arange(P)[None, :]
    masks = []
    for h in LEVELS:
        same = s // (2 * h) == t // (2 * h)
        masks.append(same & ((s % (2 * h) < h) != (t % (2 * h) < h)))
    masks.append(s == t)
    band = np.zeros((P, 2, P), np.float32)
    band[:, 0, :][~(t <= s)] = -8e30
    band[:, 1, :][~(t >= s)] = -8e30

    def angles(dim):
        nf = dim // 4
        inv = np.exp(np.float32(-np.log(10000.0)) * np.arange(nf, dtype=np.float32) / np.float32(nf)).astype(np.float32)
        tok = np.arange(2 * P)
        ang = [(p.astype(np.float32)[:, None] * inv[None]).astype(np.float32) for p in (tok // 64, tok % 64)]
        cos = np.concatenate([np.cos(a) for a in (ang[0], ang[0], ang[1], ang[1])], 1)
        sin = np.concatenate([-np.sin(ang[0]), np.sin(ang[0]), -np.sin(ang[1]), np.sin(ang[1])], 1)
        return cos.astype(np.float32), sin.astype(np.float32)

    out = {"k_ident": np.eye(P, dtype=np.float32), "k_mask": np.stack(masks, 1).astype(np.int32), "k_band": band}
    for dim in (64, 32):
        cos, sin = angles(dim)
        out[f"k_rope{dim}"] = np.ascontiguousarray(np.stack([cos, sin]).reshape(2, 2, P, dim).transpose(2, 1, 0, 3))
    out["k_tri"] = np.stack([(s < t), np.ones((P, P), bool)], 1).astype(np.float32)
    e = np.arange(EXPERTS)
    row = np.concatenate([np.arange(P), np.arange(PAIRS), CAP * (e % 2), e // 2])
    out["k_tab"] = np.concatenate([np.broadcast_to(row, (P, row.size)), s + P * np.arange(NT)[None] + 1], 1).astype(np.float32)
    ropeT = np.zeros((P, 2 * P), np.float32)
    ropeT[64:96], ropeT[96:128] = cos.T, sin.T
    out["k_ropeT"] = ropeT
    return out


_INS = ['x_prompt', 'x_sample', 'c', 'cache_swa_k', 'cache_swa_v', 'state_hgrn', 'cache_mla_ckv',
        'cache_mla_krope', 'c_ctx', 'mod_w', 'mod_b', 'norm1_w', 'norm2_w', 'final_norm_w',
        'even_w_in', 'even_w_out', 'swa_sink', 'hgrn_lb_fwd', 'hgrn_lb_bwd', 'hgrn_gnorm_w',
        'mla_w_dq', 'mla_qnorm_w', 'mla_w_uq', 'mla_w_dkv', 'mla_kvnorm_w', 'mla_w_ukv', 'mla_w_o',
        'moe_router_group_w', 'moe_router_group_b', 'moe_router_expert_w', 'moe_router_expert_b',
        'moe_w_gate', 'moe_w_up', 'moe_w_down']
_OUTS = [(1, 128, 1024), (1, 256, 1024), (1, 1, 128, 2, 64), (1, 1, 128, 2, 64), (1, 1, 2, 4, 128, 128),
         (1, 1, 128, 256), (1, 1, 128, 32)]


def kernel(**inputs):
    import numpy as np
    import concourse.bacc as bacc
    from concourse.bass_utils import run_bass_kernel_spmd

    nc = bacc.Bacc("TRN2", target_bir_lowering=False, num_devices=1)
    given = {name: np.ascontiguousarray(inputs[name]) for name in _INS}
    given.update(_constants())
    arrays, I, O = {}, {}, []
    for name, a in given.items():
        arrays[f"in_{name}"] = a
        I[name] = nc.dram_tensor(f"in_{name}", a.shape, mybir.dt.from_np(a.dtype), kind="ExternalInput").ap()
    for i, shape in enumerate(_OUTS):
        O.append(nc.dram_tensor(f"out_{i}", shape, mybir.dt.float32, kind="ExternalOutput").ap())
    mod_dram = nc.dram_tensor("mod_dram", (2, 2, 6 * D), mybir.dt.float32, kind="Internal").ap()
    scratch = [nc.dram_tensor(name, shape, mybir.dt.float32, kind="Internal").ap() for name, shape in _SCRATCH]
    build(nc, I, O, mod_dram, *scratch)
    r = run_bass_kernel_spmd(nc, [arrays], core_ids=[0])
    return tuple(r.results[0][f"out_{i}"] for i in range(len(_OUTS)))
```
